# Optimizing a Trainium2 kernel written in Bass

```python
import math
import jax
import jax.numpy as jnp
from jax import lax

D_MODEL = 1024
BATCH = 1
SEQ = 256
DEPTH = 2

MIX_WIDTH = D_MODEL
N_MIX_GROUPS = 4
GROUP_WIDTH = MIX_WIDTH // N_MIX_GROUPS
HEAD_DIM = 64
N_HEADS_G = GROUP_WIDTH // HEAD_DIM
NORM_EPS = 1e-6
NEG_INF = -1e30

ROPE_THETA = 500000.0
ROPE_DIMS = HEAD_DIM // 4

RET_THETA = 10000.0
RET_CHUNK = 128

MOBA_BLOCK = 256
MOBA_TOPK = 3

SSM_D_INNER = GROUP_WIDTH
SSM_HEADDIM = 64
SSM_HEADS = SSM_D_INNER // SSM_HEADDIM
SSM_NGROUPS = 2
SSM_D_STATE = 128
SSM_CONV = 4
SSM_CHUNK = 256
SSM_CONV_CH = SSM_D_INNER + 2 * SSM_NGROUPS * SSM_D_STATE

NSA_CMP_BLOCK = 32
NSA_CMP_STRIDE = 16
NSA_CMP_HIDDEN = 256
NSA_SLC_BLOCK = 64
NSA_SLC_TOPK = 16
NSA_WINDOW = 512
NSA_FORCE_BONUS = 1e6

PEER_HEADS = 8
PEER_NKEYS = 128
PEER_EXPERTS = PEER_NKEYS * PEER_NKEYS
PEER_KEY_DIM = 128
PEER_TOPK = 16
PEER_TOKEN_BLOCK = 128

Q_BLOCK = 128
SEQ_MULTIPLE = 256

IN_SPLITS = (
    ('ret_q', GROUP_WIDTH), ('ret_k', GROUP_WIDTH), ('ret_v', GROUP_WIDTH), ('ret_g', GROUP_WIDTH),
    ('moba_q', GROUP_WIDTH), ('moba_k', GROUP_WIDTH), ('moba_v', GROUP_WIDTH),
    ('ssm_z', SSM_D_INNER), ('ssm_xbc', SSM_CONV_CH), ('ssm_dt', SSM_HEADS),
    ('nsa_q', GROUP_WIDTH),
    ('nsa_k_cmp', HEAD_DIM), ('nsa_v_cmp', HEAD_DIM),
    ('nsa_k_slc', HEAD_DIM), ('nsa_v_slc', HEAD_DIM),
    ('nsa_k_win', HEAD_DIM), ('nsa_v_win', HEAD_DIM),
    ('nsa_gate', 3 * N_HEADS_G),
)
IN_COLS = sum(w for _, w in IN_SPLITS)

kernel_name = 'hybrid_ret_moba_ssd_nsa_peer'

def rmsnorm(x, w):
    x32 = x.astype(jnp.float32)
    y = x32 * lax.rsqrt(jnp.mean(x32 * x32, axis=-1, keepdims=True) + NORM_EPS)
    return (y * w.astype(jnp.float32)).astype(x.dtype)

def split_columns(y):
    parts = {}
    off = 0
    for name, width in IN_SPLITS:
        parts[name] = y[..., off:off + width]
        off += width
    return parts

def rope_tables(seq, rot_dims, theta):
    inv = 1.0 / (theta ** (jnp.arange(0, rot_dims, 2, dtype=jnp.float32) / rot_dims))
    ang = jnp.arange(seq, dtype=jnp.float32)[:, None] * inv[None, :]
    return jnp.cos(ang), jnp.sin(ang)

def apply_rope(x, cos, sin):
    half = cos.shape[-1]
    rot = 2 * half
    c = cos[None, :, None, :].astype(x.dtype)
    s = sin[None, :, None, :].astype(x.dtype)
    x1 = x[..., :half]
    x2 = x[..., half:rot]
    return jnp.concatenate([x1 * c - x2 * s, x1 * s + x2 * c, x[..., rot:]], axis=-1)

def retention(q, k, v, g, norm_w):
    b, s, h, d = q.shape
    cos, sin = rope_tables(s, d, RET_THETA)
    q = apply_rope(q, cos, sin)
    k = apply_rope(k, cos, sin) * (d ** -0.5)
    c = RET_CHUNK
    n = s // c
    log_gamma = jnp.log1p(-jnp.exp2(-5.0 - jnp.arange(h, dtype=jnp.float32)))
    pos = jnp.arange(c, dtype=jnp.float32)
    diff = pos[:, None] - pos[None, :]
    intra = jnp.where(diff >= 0, jnp.exp(log_gamma[:, None, None] * jnp.maximum(diff, 0.0)), 0.0).astype(q.dtype)
    q_dec = jnp.exp(log_gamma[:, None] * (pos + 1.0)).astype(q.dtype)
    k_dec = jnp.exp(log_gamma[:, None] * (c - 1.0 - pos)).astype(q.dtype)
    c_dec = jnp.exp(log_gamma * c).astype(q.dtype)
    qc = q.reshape(b, n, c, h, d)
    kc = k.reshape(b, n, c, h, d)
    vc = v.reshape(b, n, c, h, d)
    att = jnp.einsum('bnihd,bnjhd->bnhij', qc, kc) * intra
    o_in = jnp.einsum('bnhij,bnjhe->bnihe', att, vc)
    kv = jnp.einsum('bnjhd,hj,bnjhe->nbhde', kc, k_dec, vc)

    def step(state, kv_n):
        return state * c_dec[None, :, None, None] + kv_n, state

    _, prev = lax.scan(step, jnp.zeros_like(kv[0]), kv)
    o_x = jnp.einsum('bnihd,nbhde,hi->bnihe', qc, prev, q_dec)
    o = (o_in + o_x).reshape(b, s, h, d)
    o = rmsnorm(o, norm_w.reshape(h, d))
    return jax.nn.silu(g) * o.reshape(b, s, h * d)

def moba(q, k, v):
    b, s, h, d = q.shape
    nb = s // MOBA_BLOCK
    topk = min(MOBA_TOPK, nb)
    scale = d ** -0.5
    qh = q.transpose(0, 2, 1, 3)
    kblk = k.transpose(0, 2, 1, 3).reshape(b, h, nb, MOBA_BLOCK, d)
    vblk = v.transpose(0, 2, 1, 3).reshape(b, h, nb, MOBA_BLOCK, d)
    kmean = jnp.mean(kblk, axis=3)
    blk_pos = jnp.arange(MOBA_BLOCK)
    head_ix = jnp.arange(h)[:, None, None]

    def one_batch(args):
        qb, kb, vb, kmb = args

        def one_chunk(ci):
            t0 = ci * Q_BLOCK
            tpos = t0 + jnp.arange(Q_BLOCK)
            cur = t0 // MOBA_BLOCK
            qc = lax.dynamic_slice_in_dim(qb, t0, Q_BLOCK, axis=1)
            gate = jnp.einsum('hqd,hnd->hqn', qc, kmb).astype(jnp.float32)
            gate = jnp.where(jnp.arange(nb) < cur, gate, NEG_INF)
            _, sel = lax.top_k(gate, topk)
            sel_ok = sel < cur
            kg = kb[head_ix, sel]
            vg = vb[head_ix, sel]
            s_sel = jnp.einsum('hqd,hqnjd->hqnj', qc, kg).astype(jnp.float32) * scale
            s_sel = jnp.where(sel_ok[..., None], s_sel, NEG_INF).reshape(h, Q_BLOCK, topk * MOBA_BLOCK)
            k_own = lax.dynamic_index_in_dim(kb, cur, axis=1, keepdims=False)
            v_own = lax.dynamic_index_in_dim(vb, cur, axis=1, keepdims=False)
            s_own = jnp.einsum('hqd,hjd->hqj', qc, k_own).astype(jnp.float32) * scale
            own_ok = (cur * MOBA_BLOCK + blk_pos)[None, :] <= tpos[:, None]
            s_own = jnp.where(own_ok, s_own, NEG_INF)
            p = jax.nn.softmax(jnp.concatenate([s_sel, s_own], axis=-1), axis=-1).astype(qc.dtype)
            p_sel = p[..., :topk * MOBA_BLOCK].reshape(h, Q_BLOCK, topk, MOBA_BLOCK)
            p_own = p[..., topk * MOBA_BLOCK:]
            return (jnp.einsum('hqnj,hqnjd->qhd', p_sel, vg)
                    + jnp.einsum('hqj,hjd->qhd', p_own, v_own))

        out = lax.map(one_chunk, jnp.arange(s // Q_BLOCK))
        return out.reshape(s, h, d)

    return lax.map(one_batch, (qh, kblk, vblk, kmean))

def ssd_chunked(x, dt, a, bm, cm):
    b, s, h, p = x.shape
    g, n = bm.shape[2], bm.shape[3]
    rep = h // g
    L = SSM_CHUNK
    nc = s // L
    bh = jnp.repeat(bm, rep, axis=2).reshape(b, nc, L, h, n)
    ch = jnp.repeat(cm, rep, axis=2).reshape(b, nc, L, h, n)
    xdt = (x * dt[..., None].astype(x.dtype)).reshape(b, nc, L, h, p)
    acum = jnp.cumsum((dt * a).reshape(b, nc, L, h), axis=2)
    causal = jnp.tril(jnp.ones((L, L), dtype=bool))[None, None, :, :, None]
    seg = acum[:, :, :, None, :] - acum[:, :, None, :, :]
    decay = jnp.where(causal, jnp.exp(jnp.where(causal, seg, 0.0)), 0.0).astype(x.dtype)
    scores = jnp.einsum('bclhn,bcshn->bclsh', ch, bh) * decay
    y_diag = jnp.einsum('bclsh,bcshp->bclhp', scores, xdt)
    to_end = jnp.exp(acum[:, :, -1:, :] - acum).astype(x.dtype)
    states = jnp.einsum('bclhn,bclh,bclhp->cbhpn', bh, to_end, xdt)
    chunk_dec = jnp.exp(acum[:, :, -1, :]).astype(x.dtype).transpose(1, 0, 2)

    def step(st, inp):
        s_c, d_c = inp
        return st * d_c[:, :, None, None] + s_c, st

    _, prev = lax.scan(step, jnp.zeros_like(states[0]), (states, chunk_dec))
    y_off = jnp.einsum('bclhn,cbhpn,bclh->bclhp', ch, prev, jnp.exp(acum).astype(x.dtype))
    return (y_diag + y_off).reshape(b, s, h, p)

def mamba2(z, xbc, dt_raw, conv_w, conv_b, dt_bias, a_log, d_skip, norm_w):
    b, s, _ = xbc.shape
    gn = SSM_NGROUPS * SSM_D_STATE
    xbc = lax.conv_general_dilated(xbc, conv_w[:, None, :], window_strides=(1,),
                                   padding=[(SSM_CONV - 1, 0)],
                                   dimension_numbers=('NWC', 'WIO', 'NWC'),
                                   feature_group_count=SSM_CONV_CH) + conv_b
    xbc = jax.nn.silu(xbc)
    xs = xbc[..., :SSM_D_INNER].reshape(b, s, SSM_HEADS, SSM_HEADDIM)
    bm = xbc[..., SSM_D_INNER:SSM_D_INNER + gn].reshape(b, s, SSM_NGROUPS, SSM_D_STATE)
    cm = xbc[..., SSM_D_INNER + gn:].reshape(b, s, SSM_NGROUPS, SSM_D_STATE)
    dt = jax.nn.softplus((dt_raw + dt_bias).astype(jnp.float32))
    a = -jnp.exp(a_log.astype(jnp.float32))
    y = ssd_chunked(xs, dt, a, bm, cm) + xs * d_skip[:, None]
    y = y.reshape(b, s, SSM_D_INNER) * jax.nn.silu(z)
    y = rmsnorm(y.reshape(b, s, SSM_NGROUPS, SSM_D_INNER // SSM_NGROUPS),
                norm_w.reshape(SSM_NGROUPS, SSM_D_INNER // SSM_NGROUPS))
    return y.reshape(b, s, SSM_D_INNER)

def nsa(q, k_cmp, v_cmp, k_slc, v_slc, k_win, v_win, gate_raw,
        pe_k, w1_k, w2_k, pe_v, w1_v, w2_v):
    b, s, h, d = q.shape
    scale = d ** -0.5
    tpos = jnp.arange(s)
    nc = (s - NSA_CMP_BLOCK) // NSA_CMP_STRIDE + 1
    starts = jnp.arange(nc) * NSA_CMP_STRIDE
    win_idx = starts[:, None] + jnp.arange(NSA_CMP_BLOCK)[None, :]

    def compress(t, pe, w1, w2):
        blocks = (t[:, win_idx] + pe).reshape(b, nc, NSA_CMP_BLOCK * d)
        return jax.nn.gelu(blocks @ w1, approximate=False) @ w2

    kc = compress(k_cmp, pe_k, w1_k, w2_k)
    vc = compress(v_cmp, pe_v, w1_v, w2_v)
    cmp_ok = (starts + NSA_CMP_BLOCK - 1)[None, :] <= tpos[:, None]
    s_cmp = jnp.einsum('bshd,bcd->bhsc', q, kc).astype(jnp.float32) * scale
    s_cmp = jnp.where(cmp_ok, s_cmp, NEG_INF)
    any_ok = jnp.any(cmp_ok, axis=-1, keepdims=True).astype(jnp.float32)
    p_cmp = jax.nn.softmax(s_cmp, axis=-1) * any_ok
    o_cmp = jnp.einsum('bhsc,bcd->bshd', p_cmp.astype(q.dtype), vc)
    nsb = s // NSA_SLC_BLOCK
    sb = jnp.arange(nsb)
    overlap = ((starts[:, None] < (sb[None, :] + 1) * NSA_SLC_BLOCK)
               & ((starts + NSA_CMP_BLOCK)[:, None] > sb[None, :] * NSA_SLC_BLOCK)).astype(jnp.float32)
    imp = jnp.einsum('bhsc,cj->bsj', p_cmp, overlap)
    cur_b = tpos // NSA_SLC_BLOCK
    slc_ok = sb[None, :] <= cur_b[:, None]
    forced = (sb[None, :] == 0) | (sb[None, :] == cur_b[:, None]) | (sb[None, :] == cur_b[:, None] - 1)
    imp = jnp.where(forced, imp + NSA_FORCE_BONUS, imp)
    imp = jnp.where(slc_ok, imp, NEG_INF)
    ksel = min(NSA_SLC_TOPK, nsb)
    _, sel = lax.top_k(imp, ksel)
    ks_blk = k_slc.reshape(b, nsb, NSA_SLC_BLOCK, d)
    vs_blk = v_slc.reshape(b, nsb, NSA_SLC_BLOCK, d)
    kw = jnp.pad(k_win, ((0, 0), (NSA_WINDOW, 0), (0, 0)))
    vw = jnp.pad(v_win, ((0, 0), (NSA_WINDOW, 0), (0, 0)))
    slc_pos = jnp.arange(NSA_SLC_BLOCK)
    win_span = jnp.arange(NSA_WINDOW + Q_BLOCK)

    def one_batch(args):
        qb, ksb, vsb, kwb, vwb, selb = args

        def one_chunk(ci):
            t0 = ci * Q_BLOCK
            tq = t0 + jnp.arange(Q_BLOCK)
            qc = lax.dynamic_slice_in_dim(qb, t0, Q_BLOCK, axis=0)
            sc = lax.dynamic_slice_in_dim(selb, t0, Q_BLOCK, axis=0)
            kg = ksb[sc]
            vg = vsb[sc]
            key_pos = sc[..., None] * NSA_SLC_BLOCK + slc_pos
            ok = key_pos <= tq[:, None, None]
            s_s = jnp.einsum('qhd,qnjd->qhnj', qc, kg).astype(jnp.float32) * scale
            s_s = jnp.where(ok[:, None], s_s, NEG_INF).reshape(Q_BLOCK, h, ksel * NSA_SLC_BLOCK)
            p_s = jax.nn.softmax(s_s, axis=-1).astype(qc.dtype).reshape(Q_BLOCK, h, ksel, NSA_SLC_BLOCK)
            o_s = jnp.einsum('qhnj,qnjd->qhd', p_s, vg)
            kwc = lax.dynamic_slice_in_dim(kwb, t0, NSA_WINDOW + Q_BLOCK, axis=0)
            vwc = lax.dynamic_slice_in_dim(vwb, t0, NSA_WINDOW + Q_BLOCK, axis=0)
            kpos = t0 - NSA_WINDOW + win_span
            wok = ((kpos[None, :] <= tq[:, None]) & (kpos[None, :] > tq[:, None] - NSA_WINDOW)
                   & (kpos[None, :] >= 0))
            s_w = jnp.einsum('qhd,kd->qhk', qc, kwc).astype(jnp.float32) * scale
            s_w = jnp.where(wok[:, None, :], s_w, NEG_INF)
            o_w = jnp.einsum('qhk,kd->qhd', jax.nn.softmax(s_w, axis=-1).astype(qc.dtype), vwc)
            return o_s, o_w

        o_s, o_w = lax.map(one_chunk, jnp.arange(s // Q_BLOCK))
        return o_s.reshape(s, h, d), o_w.reshape(s, h, d)

    o_slc, o_win = lax.map(one_batch, (q, ks_blk, vs_blk, kw, vw, sel))
    gates = jax.nn.sigmoid(gate_raw.astype(jnp.float32)).astype(q.dtype).reshape(b, s, 3, h)
    o = (gates[:, :, 0, :, None] * o_cmp + gates[:, :, 1, :, None] * o_slc
         + gates[:, :, 2, :, None] * o_win)
    return o.reshape(b, s, h * d)

def token_mixer(h, w_in, ret_norm, ssm_conv_w, ssm_conv_b, ssm_dt_bias, ssm_a_log, ssm_d,
                ssm_norm, nsa_pe_k, nsa_w1_k, nsa_w2_k, nsa_pe_v, nsa_w1_v, nsa_w2_v, w_out):
    b, s, _ = h.shape
    s_pad = -(-s // SEQ_MULTIPLE) * SEQ_MULTIPLE
    hp = jnp.pad(h, ((0, 0), (0, s_pad - s), (0, 0)))
    c = split_columns(hp @ w_in)

    def heads(t):
        return t.reshape(b, s_pad, -1, HEAD_DIM)

    cos, sin = rope_tables(s_pad, ROPE_DIMS, ROPE_THETA)

    def rope_kv(t):
        return apply_rope(t[:, :, None, :], cos, sin)[:, :, 0, :]

    o_ret = retention(heads(c['ret_q']), heads(c['ret_k']), heads(c['ret_v']), c['ret_g'], ret_norm)
    o_moba = moba(apply_rope(heads(c['moba_q']), cos, sin),
                  apply_rope(heads(c['moba_k']), cos, sin),
                  heads(c['moba_v'])).reshape(b, s_pad, GROUP_WIDTH)
    o_ssm = mamba2(c['ssm_z'], c['ssm_xbc'], c['ssm_dt'], ssm_conv_w, ssm_conv_b,
                   ssm_dt_bias, ssm_a_log, ssm_d, ssm_norm)
    o_nsa = nsa(apply_rope(heads(c['nsa_q']), cos, sin),
                rope_kv(c['nsa_k_cmp']), c['nsa_v_cmp'],
                rope_kv(c['nsa_k_slc']), c['nsa_v_slc'],
                rope_kv(c['nsa_k_win']), c['nsa_v_win'], c['nsa_gate'],
                nsa_pe_k, nsa_w1_k, nsa_w2_k, nsa_pe_v, nsa_w1_v, nsa_w2_v)
    mixed = jnp.concatenate([o_ret, o_moba, o_ssm, o_nsa], axis=-1)[:, :s]
    return mixed @ w_out

def peer(h, w_q, sub_keys, u, v):
    b, s, dm = h.shape
    tb = PEER_TOKEN_BLOCK
    hb = h.reshape((b * s) // tb, tb, dm)

    def one_block(xb):
        q = (xb @ w_q).reshape(tb, PEER_HEADS, 2, PEER_KEY_DIM)
        sc = jnp.einsum('thpk,hpnk->thpn', q, sub_keys).astype(jnp.float32)
        s1, i1 = lax.top_k(sc[:, :, 0], PEER_TOPK)
        s2, i2 = lax.top_k(sc[:, :, 1], PEER_TOPK)
        cand = (s1[..., :, None] + s2[..., None, :]).reshape(tb, PEER_HEADS, PEER_TOPK * PEER_TOPK)
        cidx = (i1[..., :, None] * PEER_NKEYS + i2[..., None, :]).reshape(tb, PEER_HEADS, PEER_TOPK * PEER_TOPK)
        top_s, pos = lax.top_k(cand, PEER_TOPK)
        idx = jnp.take_along_axis(cidx, pos, axis=-1)
        gw = jax.nn.softmax(top_s, axis=-1).astype(xb.dtype)
        act = jax.nn.gelu(jnp.einsum('td,thkd->thk', xb, u[idx]), approximate=False)
        return jnp.einsum('thk,thkd->td', act * gw, v[idx])

    return lax.map(one_block, hb).reshape(b, s, dm)

def setup_inputs(seed: int = 0) -> dict:
    key = jax.random.key(seed)
    k = jax.random.split(key, 23)
    f32 = jnp.float32
    L = DEPTH

    def normal(kk, shape, scale):
        return scale * jax.random.normal(kk, shape, f32)

    def gain(kk, shape):
        return 1.0 + 0.05 * jax.random.normal(kk, shape, f32)

    flat_cmp = NSA_CMP_BLOCK * HEAD_DIM
    dt0 = jnp.exp(jax.random.uniform(k[7], (L, SSM_HEADS), f32, math.log(1e-3), math.log(1e-1)))
    return {
        'x': normal(k[0], (BATCH, SEQ, D_MODEL), 1.0),
        'norm_mix': gain(k[1], (L, D_MODEL)),
        'w_in': normal(k[2], (L, D_MODEL, IN_COLS), D_MODEL ** -0.5),
        'ret_norm': gain(k[3], (L, GROUP_WIDTH)),
        'ssm_conv_w': normal(k[4], (L, SSM_CONV, SSM_CONV_CH), SSM_CONV ** -0.5),
        'ssm_conv_b': normal(k[5], (L, SSM_CONV_CH), 0.02),
        'ssm_dt_bias': dt0 + jnp.log(-jnp.expm1(-dt0)),
        'ssm_a_log': jnp.log(jax.random.uniform(k[8], (L, SSM_HEADS), f32, 1.0, 16.0)),
        'ssm_d': gain(k[9], (L, SSM_HEADS)),
        'ssm_norm': gain(k[10], (L, SSM_D_INNER)),
        'nsa_pe_k': normal(k[11], (L, NSA_CMP_BLOCK, HEAD_DIM), 0.1),
        'nsa_w1_k': normal(k[12], (L, flat_cmp, NSA_CMP_HIDDEN), flat_cmp ** -0.5),
        'nsa_w2_k': normal(k[13], (L, NSA_CMP_HIDDEN, HEAD_DIM), NSA_CMP_HIDDEN ** -0.5),
        'nsa_pe_v': normal(k[14], (L, NSA_CMP_BLOCK, HEAD_DIM), 0.1),
        'nsa_w1_v': normal(k[15], (L, flat_cmp, NSA_CMP_HIDDEN), flat_cmp ** -0.5),
        'nsa_w2_v': normal(k[16], (L, NSA_CMP_HIDDEN, HEAD_DIM), NSA_CMP_HIDDEN ** -0.5),
        'w_out': normal(k[17], (L, MIX_WIDTH, D_MODEL), MIX_WIDTH ** -0.5),
        'norm_ffn': gain(k[18], (L, D_MODEL)),
        'peer_wq': normal(k[19], (L, D_MODEL, PEER_HEADS * 2 * PEER_KEY_DIM), D_MODEL ** -0.5),
        'peer_keys': normal(k[20], (L, PEER_HEADS, 2, PEER_NKEYS, PEER_KEY_DIM), PEER_KEY_DIM ** -0.5),
        'peer_u': normal(k[21], (L, PEER_EXPERTS, D_MODEL), D_MODEL ** -0.5),
        'peer_v': normal(k[22], (L, PEER_EXPERTS, D_MODEL), PEER_HEADS ** -0.5),
        'norm_final': gain(k[6], (D_MODEL,)),
    }

def reference(x, norm_mix, w_in, ret_norm, ssm_conv_w, ssm_conv_b, ssm_dt_bias, ssm_a_log,
              ssm_d, ssm_norm, nsa_pe_k, nsa_w1_k, nsa_w2_k, nsa_pe_v, nsa_w1_v, nsa_w2_v,
              w_out, norm_ffn, peer_wq, peer_keys, peer_u, peer_v, norm_final):
    for i in range(DEPTH):
        h = rmsnorm(x, norm_mix[i])
        x = x + token_mixer(h, w_in[i], ret_norm[i], ssm_conv_w[i], ssm_conv_b[i],
                            ssm_dt_bias[i], ssm_a_log[i], ssm_d[i], ssm_norm[i],
                            nsa_pe_k[i], nsa_w1_k[i], nsa_w2_k[i],
                            nsa_pe_v[i], nsa_w1_v[i], nsa_w2_v[i], w_out[i])
        x = x + peer(rmsnorm(x, norm_ffn[i]), peer_wq[i], peer_keys[i], peer_u[i], peer_v[i])
    return rmsnorm(x, norm_final)


_drawn_inputs = setup_inputs


def setup_inputs(seed=0):
    import zlib

    import numpy as np

    out = dict(_drawn_inputs(seed))
    spreads = {}
    factors = {'nsa_pe_k': 4.192}
    for name, (base, spread) in spreads.items():
        noise = np.random.default_rng([zlib.crc32(name.encode()), seed]).standard_normal(out[name].shape)
        drawn = base * np.exp(spread * noise) if base else spread * noise
        out[name] = jnp.asarray(drawn.astype(out[name].dtype))
    for name, factor in factors.items():
        out[name] = (out[name] * factor).astype(out[name].dtype)
    return out
```

```python
from contextlib import ExitStack

import numpy as np

import concourse.bass as bass
from concourse import mybir

F32 = mybir.dt.float32
U32 = mybir.dt.uint32
ALU = mybir.AluOpType
ACT = mybir.ActivationFunctionType
AX = mybir.AxisListType

P = 128
DEPTH, SEQ, D = 2, 256, 1024
TT = SEQ // P
DC = D // P
HD, NH = 64, 4
GW = HD * NH
NEG = -1e30
EPS = 1e-6
CONV = 4
CMP_LEN, CMP_STRIDE = 32, 16
NCMP = (SEQ - CMP_LEN) // CMP_STRIDE + 1
CPAD = 32
CHUNKS = CMP_LEN * HD // P
ROPE16 = 16
HEADS, KEYS, TOPK = 8, 128, 16
EXPERTS = KEYS * KEYS

SLOTS = 4
PIECE = 2048
N_XBC, N_PROJ, N_OUT, N_WQ, N_KEYS = 3, 18, 4, 8, 2
N_U = N_V = EXPERTS // P // 2
OUT0 = N_PROJ
WQ0 = OUT0 + N_OUT
KEY0 = WQ0 + N_WQ
U0 = KEY0 + N_KEYS
V0 = U0 + N_U
PIECES = V0 + N_V
assert PIECES % SLOTS == 0 and U0 % SLOTS == 0
Y_BLOCK = {3: 1, 4: 0, 5: 2, 6: 3, 11: 4, 12: 5, 13: 6, 14: 7, 15: 8, 16: 9, 17: 10}
W1 = (7, 8, 9, 10)
GATE, DT, K_WIN, V_WIN, K_CMP, V_CMP, K_SLC, V_SLC = 0, 12, 128, 192, 256, 320, 384, 448
NSA_Q, MOBA_Q, MOBA_K, MOBA_V, RET_Q, RET_K, RET_V, RET_G, SSM_Z = (256 * i for i in range(2, 11))
YW = 11 * 256

CONSTS = {}
_at = 0
for _name, _width in (("ident", 128), ("tri", 384), ("negk", 384), ("negq", 384), ("dret", 4 * 384),
                      ("cr", 128), ("sr", 128), ("c16", 32), ("s16", 32), ("cmpneg", 64), ("any", 2),
                      ("blkd", 4), ("iota", 128)):
    CONSTS[_name] = (_at, _at + _width)
    _at += _width
NCONST = _at
PARAMS = {}
_at = 0
for _name, _width in (("norm_mix", 8), ("norm_ffn", 8), ("conv_w", 24), ("conv_b", 6), ("ret_norm", 2),
                      ("ssm_norm", 2), ("pe_k", 16), ("pe_v", 16), ("w2k", 256), ("w2v", 128),
                      ("dt_bias", 4), ("a_log", 4), ("ssm_d", 4), ("norm_final", 8)):
    PARAMS[_name] = (_at, _at + _width)
    _at += _width
NPARAM = _at


def shape_constants():
    c = np.zeros((P, NCONST), np.float32)

    def put(name, a):
        lo, hi = CONSTS[name]
        c[:, lo:hi] = np.asarray(a, np.float32).reshape(P, hi - lo)

    p = np.arange(P)[:, None]
    t = np.arange(SEQ)
    put("ident", np.eye(P))
    age = np.concatenate([t[None, :] - p, t[None, P:] - (p + P)], 1)
    put("tri", age >= 0)
    put("negk", np.where(age >= 0, 0.0, NEG))
    ageq = np.concatenate([p - t[None, :P], p + P - t[None, :]], 1)
    put("negq", np.where(ageq >= 0, 0.0, NEG))
    lg = np.log1p(-np.exp2(-5.0 - np.arange(NH)))
    put("dret", np.stack([np.where(age >= 0, np.exp(lg[h] * np.maximum(age, 0)) * HD ** -0.5, 0.0)
                          for h in range(NH)], 1))

    def rope(n, theta):
        inv = (1.0 / (np.float32(theta) ** (np.arange(0, n, 2, dtype=np.float32) / np.float32(n)))).astype(np.float32)
        ang = (t.astype(np.float32)[:, None] * inv[None, :]).astype(np.float32).astype(np.float64)
        co, si = np.cos(ang), np.sin(ang)
        both = [np.concatenate([co, co], 1), np.concatenate([-si, si], 1)]
        return [b.reshape(TT, P, n).transpose(1, 0, 2) for b in both]

    cr, sr = rope(HD, 10000.0)
    put("cr", cr)
    put("sr", sr)
    c16, s16 = rope(ROPE16, 500000.0)
    put("c16", c16)
    put("s16", s16)
    tok = t.reshape(TT, P).T[:, :, None]
    j = np.arange(CPAD)[None, None, :]
    ok = (j * CMP_STRIDE + CMP_LEN - 1 <= tok) & (j < NCMP)
    put("cmpneg", np.where(ok, 0.0, NEG))
    put("any", ok.any(-1))
    put("blkd", p // CPAD == np.arange(NH)[None, :])
    put("iota", np.broadcast_to(np.arange(P)[None, :], (P, P)))
    return c


def bc(ap, axis, n):
    u = ap.unsqueeze(axis)
    shape = list(u.shape)
    shape[axis] = n
    return u.broadcast_to(shape)


def program(nc, x_t, stream, params, consts, out_t):
    ctx = ExitStack()
    with ctx:
        def sb(name, shape, dt=F32):
            return ctx.enter_context(nc.sbuf_tensor(name, shape, dt))

        sems = []

        def sem(name):
            s = ctx.enter_context(nc.semaphore(name))
            sems.append(s)
            return s

        ld0 = ctx.enter_context(nc.semaphore("ld0"))
        stored = ctx.enter_context(nc.semaphore("stored"))
        f_sq = ctx.enter_context(nc.semaphore("f_sq"))
        f_ssq = ctx.enter_context(nc.semaphore("f_ssq"))
        f_var = ctx.enter_context(nc.semaphore("f_var"))
        f_rs = ctx.enter_context(nc.semaphore("f_rs"))
        f_step = ctx.enter_context(nc.semaphore("f_step"))
        f_out = ctx.enter_context(nc.semaphore("f_out"))
        s_ones = ctx.enter_context(nc.semaphore("s_ones"))

        s_par = sem("s_par")
        landed = [sem(f"landed{i}") for i in range(SLOTS)]
        piece_done = sem("piece_done")
        sq_ready = sem("sq_ready")
        ssq_done = sem("ssq_done")
        var_ready = sem("var_ready")
        rs_ready = sem("rs_ready")
        h_ready = sem("h_ready")
        act_step = sem("act_step")
        dve_step = sem("dve_step")
        evac = sem("evac")
        padded = sem("padded")
        conv_ready = sem("conv_ready")
        conv_exp = sem("conv_exp")
        xc_ready = sem("xc_ready")
        roped = sem("roped")
        dup_ready = sem("dup_ready")
        dt_abs = sem("dt_abs")
        dt_exp = sem("dt_exp")
        dt_one = sem("dt_one")
        dt_ln = sem("dt_ln")
        da_ready = sem("da_ready")
        tr_done = sem("tr_done")
        tr_evac = sem("tr_evac")
        blocks_ready = sem("blocks_ready")
        hid_ready = sem("hid_ready")
        kcvc_done = sem("kcvc_done")
        kc_ready = sem("kc_ready")
        vb_ready = sem("vb_ready")
        sc_done = sem("sc_done")
        sc_evac = sem("sc_evac")
        negm_ready = sem("negm_ready")
        exp_done = sem("exp_done")
        acs_done = sem("acs_done")
        b6_free = sem("b6_free")
        cs_ready = sem("cs_ready")
        cs_exp = sem("cs_exp")
        acr_done = sem("acr_done")
        seg_ready = sem("seg_ready")
        seg_exp = sem("seg_exp")
        ps_ready = sem("ps_ready")
        pv_done = sem("pv_done")
        pv_evac = sem("pv_evac")
        m_ready = sem("m_ready")
        z_exp = sem("z_exp")
        g_var = sem("g_var")
        g_rs = sem("g_rs")
        x_added = sem("x_added")
        qt_evac = sem("qt_evac")
        key_done = sem("key_done")
        key_evac = sem("key_evac")
        rt_sub = sem("rt_sub")
        rt_exp = sem("rt_exp")
        rt_ready = sem("rt_ready")
        rt_tr = sem("rt_tr")
        rt_free = sem("rt_free")
        gelu_done = sem("gelu_done")
        d_ready = sem("d_ready")
        d2_ready = sem("d2_ready")
        o2_ready = sem("o2_ready")
        o1_ready = sem("o1_ready")
        w_done = sem("w_done")
        w_used = sem("w_used")
        acc_done = sem("acc_done")

        X = sb("X", [P, DC, SEQ])
        H = sb("H", [P, DC, SEQ])
        ring = sb("ring", [P, SLOTS, PIECE])
        G = sb("G", [P, KEYS, SEQ])
        CN = sb("CN", [P, NCONST])
        PR = sb("PR", [P, NPARAM])
        ones = sb("ones", [P, P])
        var = sb("var", [P, SEQ])
        rs = sb("rs", [P, SEQ])
        nt = sb("nt", [P, SEQ])
        slotT = sb("slotT", [P, 3, SEQ])
        PS = ctx.enter_context(nc.psum_tensor("PS", [P, 8, 512], F32))

        def cn(name, lo=0, hi=None):
            a, b = CONSTS[name]
            return CN[:, a + lo:(b if hi is None else a + hi)]

        def pr(name, lo=0, hi=None):
            a, b = PARAMS[name]
            return PR[:, a + lo:(b if hi is None else a + hi)]

        ident = cn("ident")
        Gf = G[:, :, :].rearrange("p e t -> p (e t)")
        used = [0]

        def region(width):
            lo = used[0]
            used[0] += width
            assert used[0] <= KEYS * SEQ
            return Gf[:, lo:lo + width]

        Y = region(TT * YW).rearrange("p (t n) -> p t n", t=TT)
        XBW = SEQ + CONV - 1
        XB = region(6 * XBW).rearrange("p (b n) -> p b n", b=6)
        XC = region(6 * SEQ).rearrange("p (b n) -> p b n", b=6)
        XS = region(TT * GW).rearrange("p (t n) -> p t n", t=TT)
        XDT = region(TT * GW).rearrange("p (t n) -> p t n", t=TT)
        T = region(12 * SEQ).rearrange("p (b n) -> p b n", b=12)
        TQ_NSA, TQ_MOBA, TK_MOBA, TQ_RET, TK_RET, TK_WIN, TK_SLC = 0, 2, 4, 6, 8, 10, 11
        SC4 = [region(NH * 384).rearrange("p (h n) -> p h n", h=NH) for _ in range(2)]
        PT = [region(NH * 384).rearrange("p (h n) -> p h n", h=NH) for _ in range(2)]
        SEG = region(NH * 384).rearrange("p (h n) -> p h n", h=NH)
        GS = region(2 * 384).rearrange("p (g n) -> p g n", g=2)
        DA = region(TT * NH * P).rearrange("p (t h n) -> p t h n", t=TT, h=NH)
        Mf = region(TT * D)
        M = Mf.rearrange("p (t n) -> p t n", t=TT)
        CE = Mf[:, 0:6 * SEQ].rearrange("p (b n) -> p b n", b=6)
        MTf = region(DC * SEQ)
        MT = MTf.rearrange("p (c n) -> p c n", c=DC)
        DUP = MTf[:, 0:TT * 6 * P].rearrange("p (t b e n) -> p t b e n", t=TT, b=6, e=2)
        TA = region(1024)
        TB = region(2048)
        K2 = region(2 * SEQ).rearrange("p (s n) -> p s n", s=2)
        BL = region(2 * CHUNKS * NCMP).rearrange("p (s j c) -> p s j c", s=2, j=CHUNKS)
        HV = region(2 * 2 * P).rearrange("p (s b h c) -> p s b h c", s=2, b=2, h=NH)
        KC = region(CPAD)
        VB = region(GW).rearrange("p (h n) -> p h n", h=NH)
        CS = region(TT * NH * CPAD).rearrange("p (t h c) -> p t h c", t=TT, h=NH)
        CP = region(TT * P).rearrange("p (t n) -> p t n", t=TT)
        SM = region(256)
        _s = [0]

        def small(n):
            lo = _s[0]
            _s[0] += n
            assert _s[0] <= 256
            return SM[:, lo:lo + n]

        mx = small(8)
        negm = [small(8) for _ in range(3)]
        rsum = [small(8) for _ in range(3)]
        rinv = [small(8) for _ in range(3)]
        cmx, csum, cinv = small(8), small(8), small(8)
        gate = small(24)
        dtx, dte, dtu, dtl, dtd, dtz, dta = (small(8) for _ in range(7))
        avec = small(4)
        acs = small(8)
        gvar, grs, gnt = small(8), small(8), small(8)

        rbase = 64 * SEQ

        def late(lo, width):
            return Gf[:, rbase + lo:rbase + lo + width]

        QT = late(0, 4096).rearrange("p (b n) -> p b n", b=16)
        S = late(4096, 4096).rearrange("p (t b n) -> p t b n", t=TT, b=16)
        CAND = [late(8192 + 2048 * t, 2048).rearrange("p (h n) -> p h n", h=HEADS) for t in range(TT)]
        EQ = late(0, 2048).rearrange("p (h k a) -> p h k a", h=HEADS, k=TOPK)
        EQ2 = late(2048, 2048).rearrange("p (h k a) -> p h k a", h=HEADS, k=TOPK)
        SQ = late(12288, 2048).rearrange("p (c n) -> p c n", c=DC)
        V16 = late(14336, 512).rearrange("p (t b k) -> p t b k", t=TT, b=16)
        I16 = late(14848, 512).rearrange("p (t b k) -> p t b k", t=TT, b=16).bitcast(U32)
        VC = late(15360, 256).rearrange("p (t h k) -> p t h k", t=TT, h=HEADS)
        PC = late(15616, 256).rearrange("p (t h k) -> p t h k", t=TT, h=HEADS).bitcast(U32)
        late_s = late(15872, 512)
        PAB = late_s[:, 0:128].bitcast(U32).rearrange("p (h k) -> p h k", h=HEADS)
        esum = late_s[:, 128:144]
        D2 = sb("D2", [P, 8, P])
        RT = sb("RT", [P, TT, 3, P])

        Hf = H[:, :, :].rearrange("p c n -> p (c n)")
        O1 = Hf[:, 0:1024].rearrange("p (s n) -> p s n", s=8)
        O2 = Hf[:, 1024:2048].rearrange("p (s n) -> p s n", s=8)

        bank = [PS[:, b, :] for b in range(8)]

        with nc.Block() as block:
            @block.sync
            def _(sp):
                sp.dma_start(CN[:, :], consts).then_inc(ld0, 16)
                sp.dma_start(X[:, :, :], x_t).then_inc(ld0, 16)
                sp.wait_ge(ld0, 32)

            @block.vector
            def _(dve):
                nc.vector.memset(ones[:, :], 1.0).then_inc(s_ones, 1)
                dve.wait_ge(s_ones, 1)

        with nc.Fori(0, DEPTH) as layer:
            with nc.Block() as block:
                @block.sync
                def _(sp):
                    sp.dma_start(PR[:, :], params[layer]).then_inc(s_par, 16)
                    for s in range(SLOTS):
                        sp.dma_start(ring[:, s, :], stream[layer, s]).then_inc(landed[s], 16)
                    with sp.Fori(1, PIECES // SLOTS) as r:
                        for s in range(SLOTS):
                            sp.wait_ge(piece_done, r * SLOTS + (s - SLOTS + 1))
                            sp.dma_start(ring[:, s, :], stream[layer, r * SLOTS + s]).then_inc(landed[s], 16)

                @block.gpsimd
                def _(pool):
                    pool.wait_ge(ssq_done, 1)
                    nc.gpsimd.memset(XB[:, :, 0:CONV - 1], 0.0).then_inc(padded, 1)
                    nc.gpsimd.memset(HV[:, :, :, :, :], 0.0).then_inc(padded, 1)
                    pool.wait_ge(roped, 1)
                    for e in range(2):
                        nc.gpsimd.tensor_copy(
                            DUP[:, :, :, e, :],
                            Y[:, :, K_WIN:K_WIN + 384].rearrange("p t (b n) -> p t b n", n=HD)).then_inc(dup_ready, 1)
                    pool.wait_ge(rt_free, 3)
                    def distance(t0, g, value):
                        d = D2[:, 4 * g:4 * g + 4, :]
                        nc.gpsimd.tensor_tensor(d, bc(cn("iota"), 1, 4), bc(slotT[:, 1, bass.ds(t0, 4)], 2, P),
                                                ALU.subtract).then_inc(d_ready, 1)
                        pool.wait_ge(d_ready, value)
                        nc.gpsimd.tensor_tensor(d, d, d, ALU.mult).then_inc(d2_ready, 1)

                    for g in range(2):
                        distance(4 * g, g, g + 1)
                    with pool.Fori(1, SEQ // 8) as r:
                        for g in range(2):
                            pool.wait_ge(o2_ready, r * 2 + (g - 1))
                            distance(r * 8 + 4 * g, g, r * 2 + (g + 1))

                @block.tensor
                def _(pe):
                    def piece(n):
                        pe.wait_ge(landed[n % SLOTS], 16 * (n // SLOTS + 1))
                        return ring[:, n % SLOTS, :]

                    def sum_squares(k):
                        pe.wait_ge(sq_ready, k + 1)
                        for c in range(DC):
                            mm = nc.tensor.matmul(bank[7][:, 0:SEQ], ones[:, :], SQ[:, c, :],
                                                  start=(c == 0), stop=(c == DC - 1))
                        mm.then_inc(ssq_done, 1)

                    def by_column(n, b, rhs):
                        w = piece(n).rearrange("p (c m) -> p c m", c=DC)
                        for k in range(2):
                            for c in range(DC):
                                mm = nc.tensor.matmul(bank[b][:, k * SEQ:(k + 1) * SEQ], w[:, c, k * P:(k + 1) * P],
                                                      rhs[:, c, :], start=(c == 0), stop=(c == DC - 1))
                        mm.then_inc(piece_done, 1)

                    def by_token(n, b):
                        w = piece(n).rearrange("p (c m) -> p c m", c=DC)
                        for t in range(TT):
                            for c in range(DC):
                                mm = nc.tensor.matmul(bank[b][:, t * 256:(t + 1) * 256], H[:, c, t * P:(t + 1) * P],
                                                      w[:, c, :], start=(c == 0), stop=(c == DC - 1))
                        mm.then_inc(piece_done, 1)

                    order = [0, 1, 2, 3, 4, 5, 6, 11, 12, 13, 14, 15, 16, 17]

                    def project(n):
                        j = order.index(n)
                        if j >= 2:
                            pe.wait_ge(evac, j - 1)
                        if n < N_XBC:
                            by_column(n, j % 2, H)
                        else:
                            by_token(n, j % 2)

                    sets = [0]

                    def turn(blocks):
                        k = sets[0]
                        if k >= 2:
                            pe.wait_ge(tr_evac, k - 1)
                        for i, b in enumerate(blocks):
                            mm = nc.tensor.transpose(bank[2 + k % 2][:, i * P:(i + 1) * P], b, ident)
                        mm.then_inc(tr_done, 1)
                        sets[0] += 1

                    def columns(c):
                        return [Y[:, t, c + i * P:c + (i + 1) * P] for i in range(2) for t in range(TT)]

                    scored = [0]

                    def scores(a, b, a_first):
                        k = scored[0]
                        if k >= 2:
                            pe.wait_ge(sc_evac, k - 1)
                        o = bank[4 + k % 2]
                        if a_first:
                            nc.tensor.matmul(o[:, 0:128], a[:, 0:P], b[:, 0:P], start=True, stop=True)
                            mm = nc.tensor.matmul(o[:, 128:384], a[:, P:SEQ], b[:, 0:SEQ], start=True, stop=True)
                        else:
                            nc.tensor.matmul(o[:, 0:256], a[:, 0:P], b[:, 0:SEQ], start=True, stop=True)
                            mm = nc.tensor.matmul(o[:, 256:384], a[:, P:SEQ], b[:, P:SEQ], start=True, stop=True)
                        mm.then_inc(sc_done, 1)
                        scored[0] += 1

                    def half(block, h):
                        return T[(h % 2) * HD:(h % 2) * HD + HD, block, :]

                    def values(weights, v):
                        for h in range(NH):
                            w, vh = weights(h), v(h)
                            nc.tensor.matmul(bank[6][:, h * HD:(h + 1) * HD], w[:, 0:P], vh[0], start=True, stop=True)
                            o = bank[6][:, 256 + h * HD:256 + (h + 1) * HD]
                            nc.tensor.matmul(o, w[:, P:2 * P], vh[0], start=True, stop=False)
                            mm = nc.tensor.matmul(o, w[:, 2 * P:3 * P], vh[1], start=False, stop=True)
                        mm.then_inc(pv_done, 1)

                    def y_values(c, step):
                        return lambda h: [Y[:, t, c + h * step:c + h * step + HD] for t in range(TT)]

                    def turn_group(buf, g):
                        for h in range(NH):
                            pe.wait_ge(exp_done, 8 * g + 2 * h + 2)
                            turn([buf[:, h, i * P:(i + 1) * P] for i in range(3)])

                    sum_squares(0)
                    pe.wait_ge(s_par, 16)
                    pe.wait_ge(h_ready, DC)
                    for n in (0, 1, 2, 3, 4, 5):
                        project(n)
                    pe.wait_ge(dup_ready, 2)
                    turn([DUP[:, t, b, :, :].rearrange("p e n -> p (e n)") for b in (2, 3) for t in range(TT)])
                    turn([DUP[:, t, b, :, :].rearrange("p e n -> p (e n)") for b in (0, 4) for t in range(TT)])
                    project(6)
                    pe.wait_ge(xc_ready, 1)
                    turn([XC[:, b, t * P:(t + 1) * P] for t in range(TT) for b in range(2)])
                    for i, n in enumerate(W1):
                        w = piece(n).rearrange("p (j m) -> p j m", j=CHUNKS)
                        pe.wait_ge(blocks_ready, i // 2 + 1)
                        for j in range(CHUNKS):
                            mm = nc.tensor.matmul(bank[7][:, 16 * i:16 * i + NCMP], w[:, j, :], BL[:, i // 2, j, :],
                                                  start=(j == 0), stop=(j == CHUNKS - 1))
                        mm.then_inc(piece_done, 1)
                    for g in range(2):
                        scores(XC[:, 2 + g, :], XC[:, 4 + g, :], False)
                    pe.wait_ge(roped, 2)
                    turn(columns(NSA_Q))
                    pe.wait_ge(tr_evac, 4)
                    for h in range(NH):
                        scores(half(TQ_NSA + h // 2, h), half(TK_WIN, h), True)
                    project(11)
                    pe.wait_ge(hid_ready, 4)
                    for b in range(2):
                        nc.tensor.matmul(bank[7][:, 64:96], pr("w2k", b * P, (b + 1) * P), HV[:, 0, b, 0, :],
                                         start=(b == 0), stop=(b == 1))
                    for b in range(2):
                        mm = nc.tensor.matmul(bank[7][:, 96:160], HV[:, 1, b, :, :].rearrange("p h c -> p (h c)"),
                                              pr("w2v", b * HD, (b + 1) * HD), start=(b == 0), stop=(b == 1))
                    mm.then_inc(kcvc_done, 1)
                    for h in range(NH):
                        scores(half(TQ_NSA + h // 2, h), half(TK_SLC, h), True)
                    project(12)
                    turn_group(SC4[0], 0)
                    pe.wait_ge(kc_ready, 1)
                    pe.wait_ge(vb_ready, 1)
                    for h in range(NH):
                        for t in range(TT):
                            at = 256 + (2 * t + h // 2) * CPAD
                            nc.tensor.matmul(bank[7 - h % 2][:, at:at + CPAD], half(TQ_NSA + h // 2, h)[:, t * P:(t + 1) * P],
                                                  KC[(h % 2) * HD:(h % 2) * HD + HD, :], start=True, stop=True)
                    pe.wait_ge(da_ready, 2)
                    dta_t = dta.rearrange("p (t h) -> p t h", t=TT)
                    tri = cn("tri")
                    nc.tensor.matmul(bank[6][:, 0:4], tri[:, 0:P], dta_t[:, 0, :], start=True, stop=True)
                    nc.tensor.matmul(bank[6][:, 4:8], tri[:, P:2 * P], dta_t[:, 0, :], start=True, stop=False)
                    nc.tensor.matmul(bank[6][:, 4:8], tri[:, 2 * P:3 * P], dta_t[:, 1, :], start=False,
                                     stop=True).then_inc(acs_done, 1)

                    def acr(pair):
                        for i in range(2):
                            h = 2 * pair + i
                            nc.tensor.matmul(bank[7][:, i * SEQ:(i + 1) * SEQ], DA[:, 0, h, :], tri[:, 0:SEQ],
                                             start=True, stop=False)
                            mm = nc.tensor.matmul(bank[7][:, i * SEQ + P:(i + 1) * SEQ], DA[:, 1, h, :],
                                                  tri[:, SEQ:SEQ + P], start=False, stop=True)
                        mm.then_inc(acr_done, 1)

                    project(13)
                    pe.wait_ge(tr_evac, 8)
                    pe.wait_ge(b6_free, 3)
                    values(lambda h: PT[0][:, h, :], y_values(V_WIN, 0))
                    acr(0)
                    project(14)
                    turn_group(SC4[1], 1)
                    pe.wait_ge(tr_evac, 12)
                    pe.wait_ge(pv_evac, 1)
                    values(lambda h: PT[1][:, h, :], y_values(V_SLC, 0))
                    pe.wait_ge(seg_ready, 2)
                    acr(1)
                    pe.wait_ge(roped, 3)
                    turn(columns(MOBA_Q))
                    turn(columns(MOBA_K))
                    project(15)
                    pe.wait_ge(tr_evac, 14)
                    for h in range(NH):
                        scores(half(TQ_MOBA + h // 2, h), half(TK_MOBA + h // 2, h), True)
                    pe.wait_ge(cs_exp, 1)
                    turn([CS[:, t, :, :].rearrange("p h c -> p (h c)") for t in range(TT)])
                    project(16)
                    pe.wait_ge(tr_evac, 15)
                    pe.wait_ge(pv_evac, 2)
                    for t in range(TT):
                        mm = nc.tensor.matmul(bank[6][:, t * GW:(t + 1) * GW], CP[:, t, :],
                                              VB[:, :, :].rearrange("p h n -> p (h n)"), start=True, stop=True)
                    mm.then_inc(pv_done, 1)
                    pe.wait_ge(roped, 4)
                    turn(columns(RET_Q))
                    turn(columns(RET_K))
                    pe.wait_ge(ps_ready, 2)
                    pe.wait_ge(pv_evac, 3)
                    values(lambda h: SEG[:, h, :], lambda h: [XDT[:, t, h * HD:(h + 1) * HD] for t in range(TT)])
                    project(17)
                    pe.wait_ge(tr_evac, 17)
                    for h in range(NH):
                        scores(half(TK_RET + h // 2, h), half(TQ_RET + h // 2, h), False)
                    turn_group(SC4[0], 2)
                    pe.wait_ge(tr_evac, 21)
                    pe.wait_ge(pv_evac, 4)
                    values(lambda h: PT[0][:, h, :], y_values(MOBA_V, HD))
                    pe.wait_ge(sc_evac, 18)
                    pe.wait_ge(pv_evac, 5)
                    values(lambda h: SC4[1][:, h, :], y_values(RET_V, HD))
                    for c, ready, n in ((6, m_ready, 1), (2, pv_evac, 5), (4, m_ready, 2), (0, m_ready, 3)):
                        pe.wait_ge(ready, n)
                        turn([M[:, t, (c + i) * P:(c + i + 1) * P] for i in range(2) for t in range(TT)])
                    pe.wait_ge(tr_evac, 25)
                    pe.wait_ge(evac, len(order))
                    for k in range(N_OUT):
                        if k >= 2:
                            pe.wait_ge(x_added, k - 1)
                        by_column(OUT0 + k, k % 2, MT)

                    sum_squares(1)
                    pe.wait_ge(h_ready, 2 * DC)
                    pe.wait_ge(x_added, N_OUT)
                    for k in range(N_WQ):
                        if k >= 2:
                            pe.wait_ge(qt_evac, k - 1)
                        by_column(WQ0 + k, k % 2, H)
                    pe.wait_ge(qt_evac, N_WQ)
                    sets_k = 0
                    for kp in range(N_KEYS):
                        w = piece(KEY0 + kp)[:, 0:8 * KEYS].rearrange("p (b n) -> p b n", b=8)
                        for t in range(TT):
                            for quad in range(2):
                                if sets_k >= 4:
                                    pe.wait_ge(key_evac, sets_k - 3)
                                for i in range(4):
                                    b = quad * 4 + i
                                    mm = nc.tensor.matmul(bank[sets_k % 4][:, i * P:(i + 1) * P],
                                                          QT[:, 8 * kp + b, t * P:(t + 1) * P], w[:, b, :],
                                                          start=True, stop=True)
                                mm.then_inc(piece_done if t == TT - 1 and quad == 1 else key_done, 1)
                                sets_k += 1

                    def experts_in(w, b):
                        u = w.rearrange("p (e c m) -> p e c m", e=2, c=DC)
                        for e in range(2):
                            for c in range(DC):
                                mm = nc.tensor.matmul(bank[b][:, e * SEQ:(e + 1) * SEQ], u[:, e, c, :], H[:, c, :],
                                                      start=(c == 0), stop=(c == DC - 1))
                        mm.then_inc(piece_done, 1)

                    R0 = U0 // SLOTS
                    for s in range(SLOTS):
                        experts_in(piece(U0 + s), 4 + s)

                    def rounds_in(lo, hi):
                        with pe.Fori(lo, hi) as r:
                            for s in range(SLOTS):
                                pe.wait_ge(landed[s], (r + (R0 + 1)) * 16)
                                pe.wait_ge(gelu_done, r * SLOTS + (s - SLOTS + 1))
                                experts_in(ring[:, s, :], 4 + s)

                    rounds_in(1, 12)
                    pe.wait_ge(key_evac, 8)
                    for k in range(3):
                        pe.wait_ge(rt_ready, 3 * TT)
                        for t in range(TT):
                            mm = nc.tensor.transpose(bank[k][:, t * P:(t + 1) * P], RT[:, t, k, :], ident)
                        mm.then_inc(rt_tr, 1)
                    rounds_in(12, N_U // SLOTS)

                    def place(b, g):
                        for i in range(4):
                            mm = nc.tensor.matmul(bank[b][:, i * P:(i + 1) * P], O2[:, 4 * g + i, :], O1[:, 4 * g + i, :],
                                                  start=True, stop=True)
                        mm.then_inc(w_done, 1)

                    pe.wait_ge(gelu_done, N_U)
                    for g in range(2):
                        pe.wait_ge(o1_ready, g + 1)
                        pe.wait_ge(o2_ready, g + 1)
                        place(4 + g, g)
                    with pe.Fori(1, SEQ // 8) as r:
                        for g in range(2):
                            pe.wait_ge(o1_ready, r * 2 + (g + 1))
                            pe.wait_ge(o2_ready, r * 2 + (g + 1))
                            pe.wait_ge(w_used, r * 2 + (g - 1))
                            place(4 + g, g)

                    def experts_out(w, e_first, first, last):
                        v = w.rearrange("p (e c m) -> p e c m", e=2, c=DC)
                        for e in range(2):
                            for c in range(DC):
                                mm = nc.tensor.matmul(bank[c // 2][:, (c % 2) * SEQ:(c % 2 + 1) * SEQ], v[:, e, c, :],
                                                      G[:, e_first + e, :],
                                                      start=(first and e == 0 and c % 2 == 0),
                                                      stop=(last and e == 1), skip_group_check=True)
                        mm.then_inc(piece_done, 1)

                    pe.wait_ge(w_used, SEQ // 4)
                    pe.wait_ge(rt_free, 3)
                    for s in range(SLOTS):
                        experts_out(piece(V0 + s), 2 * s, s == 0, False)
                    with pe.Fori(1, N_V // SLOTS - 1) as r:
                        for s in range(SLOTS):
                            pe.wait_ge(landed[s], (r + (V0 // SLOTS + 1)) * 16)
                            experts_out(ring[:, s, :], r * (2 * SLOTS) + 2 * s, False, False)
                    for s in range(SLOTS):
                        k = N_V - SLOTS + s
                        pe.wait_ge(landed[s], 16 * (PIECES // SLOTS))
                        experts_out(ring[:, s, :], 2 * k, False, s == SLOTS - 1)
                    nc.tensor.matmul(bank[7][:, 0:8], ones[:, :], ones[:, 0:8], start=True, stop=True).then_inc(acc_done, 1)

                @block.scalar
                def _(act):
                    def rough_root(src, dst, ready, done, n, steps):
                        act.wait_ge(ready, n)
                        nc.scalar.activation(dst, src, ACT.Ln).then_inc(act_step, 1)
                        act.wait_ge(act_step, steps)
                        nc.scalar.activation(dst, dst, ACT.Exp, scale=-0.5).then_inc(done, 1)

                    order = [0, 1, 2, 3, 4, 5, 6, 11, 12, 13, 14, 15, 16, 17]

                    def take(n):
                        act.wait_ge(piece_done, n + 1)
                        b = order.index(n) % 2
                        if n < N_XBC:
                            dst = XB[:, 2 * n:2 * n + 2, CONV - 1:]
                        else:
                            c = 256 * Y_BLOCK[n]
                            dst = Y[:, :, c:c + 256]
                        nc.scalar.copy(dst, bank[b].rearrange("p (k m) -> p k m", k=2)).then_inc(evac, 1)

                    turned = [0]

                    def taken(dst, width=512):
                        k = turned[0]
                        act.wait_ge(tr_done, k + 1)
                        src = bank[2 + k % 2][:, 0:width]
                        turned[0] += 1
                        return nc.scalar.copy(dst, src if len(dst.shape) == 2 else
                                              src.rearrange("p (k m) -> p k m", k=dst.shape[1]))

                    def exps(g, buf):
                        act.wait_ge(negm_ready, g + 1)
                        for h in range(NH):
                            for t in range(TT):
                                s = buf[:, h, 0:P] if t == 0 else buf[:, h, P:3 * P]
                                k = t * NH + h
                                nc.scalar.activation(s, s, ACT.Exp, bias=negm[g][:, k:k + 1], scale=HD ** -0.5,
                                                     accum_out=rsum[g][:, k:k + 1]).then_inc(exp_done, 1)

                    def probabilities(buf):
                        for h in range(NH):
                            taken(buf[:, h, :], 384).then_inc(tr_evac, 1)

                    nc.scalar.activation(SQ[:, :, :], X[:, :, :], ACT.Square).then_inc(sq_ready, 1)
                    rough_root(var[:, :], rs[:, :], var_ready, rs_ready, 1, 1)
                    for n in (0, 1, 2, 3, 4):
                        take(n)
                    act.wait_ge(conv_ready, 6)
                    nc.scalar.activation(CE[:, :, :], XC[:, :, :], ACT.Exp, scale=-1.0).then_inc(conv_exp, 1)
                    take(5)
                    act.wait_ge(tr_done, 1)
                    for s in range(2):
                        nc.scalar.copy(K2[0:HD, s, :], bank[2][0:HD, s * SEQ:(s + 1) * SEQ])
                        cp = nc.scalar.copy(K2[HD:P, s, 0:SEQ - 1], bank[2][HD:P, s * SEQ + 1:(s + 1) * SEQ])
                    cp.then_inc(tr_evac, 1)
                    turned[0] += 1
                    taken(T[:, TK_WIN:TK_WIN + 2, :]).then_inc(tr_evac, 1)
                    take(6)
                    act.wait_ge(dt_abs, 1)
                    nc.scalar.activation(dte, dte, ACT.Exp).then_inc(dt_exp, 1)
                    act.wait_ge(s_par, 16)
                    nc.scalar.activation(avec, pr("a_log"), ACT.Exp).then_inc(dt_exp, 1)
                    act.wait_ge(evac, 5)
                    nc.scalar.activation(gate.rearrange("p (t k) -> p t k", t=TT), Y[:, :, GATE:GATE + 12],
                                         ACT.Exp, scale=-1.0).then_inc(z_exp, 1)
                    act.wait_ge(dt_one, 1)
                    nc.scalar.activation(dtl, dtu, ACT.Ln).then_inc(dt_ln, 1)
                    taken(XS[:, :, :]).then_inc(tr_evac, 1)
                    act.wait_ge(padded, 2)
                    act.wait_ge(piece_done, W1[-1] + 1)
                    for i in range(len(W1)):
                        s, b = i // 2, i % 2
                        heads = 1 if s == 0 else NH
                        nc.scalar.activation(HV[:, s, b, 0:heads, 0:NCMP],
                                             bc(bank[7][:, 16 * i:16 * i + NCMP], 1, heads),
                                             ACT.Gelu).then_inc(hid_ready, 1)
                    taken(T[:, TQ_NSA:TQ_NSA + 2, :]).then_inc(tr_evac, 1)
                    exps(0, SC4[0])
                    take(11)
                    exps(1, SC4[1])
                    take(12)
                    probabilities(PT[0])
                    act.wait_ge(cs_ready, 1)
                    nc.scalar.activation(CS[:, :, :, :], CS[:, :, :, :], ACT.Exp, scale=HD ** -0.5).then_inc(cs_exp, 1)
                    take(13)
                    take(14)
                    probabilities(PT[1])
                    taken(T[:, TQ_MOBA:TQ_MOBA + 2, :]).then_inc(tr_evac, 1)
                    taken(T[:, TK_MOBA:TK_MOBA + 2, :]).then_inc(tr_evac, 1)
                    take(15)
                    act.wait_ge(seg_ready, 4)
                    nc.scalar.activation(SEG[:, :, :], SEG[:, :, :], ACT.Exp).then_inc(seg_exp, 1)
                    taken(CP[:, :, :], 256).then_inc(tr_evac, 1)
                    take(16)
                    act.wait_ge(evac, 13)
                    nc.scalar.activation(TB[:, 0:512].rearrange("p (t n) -> p t n", t=TT),
                                         Y[:, :, RET_G:RET_G + GW], ACT.Exp, scale=-1.0).then_inc(z_exp, 1)
                    taken(T[:, TQ_RET:TQ_RET + 2, :]).then_inc(tr_evac, 1)
                    taken(T[:, TK_RET:TK_RET + 2, :]).then_inc(tr_evac, 1)
                    take(17)
                    act.wait_ge(evac, len(order))
                    nc.scalar.activation(TB[:, 512:1024].rearrange("p (t n) -> p t n", t=TT),
                                         Y[:, :, SSM_Z:SSM_Z + GW], ACT.Exp, scale=-1.0).then_inc(z_exp, 1)
                    exps(2, SC4[0])
                    probabilities(PT[0])
                    rough_root(gvar[:, 0:4], grs[:, 0:4], g_var, g_rs, 1, 2)
                    for c in (6, 2, 4):
                        if c == 4:
                            for i in range(2):
                                act.wait_ge(tr_done, 24)
                                cp = nc.scalar.mul(MT[:, c + i, :], bank[2 + 23 % 2][:, i * SEQ:(i + 1) * SEQ],
                                                   pr("ssm_norm", i, i + 1))
                            cp.then_inc(tr_evac, 1)
                            turned[0] += 1
                        else:
                            taken(MT[:, c:c + 2, :]).then_inc(tr_evac, 1)
                    rough_root(gvar[:, 0:8], grs[:, 0:8], g_var, g_rs, 2, 3)
                    act.wait_ge(tr_done, 25)
                    for i in range(2):
                        cp = nc.scalar.mul(MT[:, i, :], bank[2 + 24 % 2][:, i * SEQ:(i + 1) * SEQ],
                                           pr("ret_norm", i, i + 1))
                    cp.then_inc(tr_evac, 1)

                    act.wait_ge(x_added, N_OUT)
                    nc.scalar.activation(SQ[:, :, :], X[:, :, :], ACT.Square).then_inc(sq_ready, 1)
                    rough_root(var[:, :], rs[:, :], var_ready, rs_ready, 2, 4)
                    for k in range(N_WQ):
                        act.wait_ge(piece_done, WQ0 + k + 1)
                        nc.scalar.copy(QT[:, 2 * k:2 * k + 2, :],
                                       bank[k % 2].rearrange("p (k m) -> p k m", k=2)).then_inc(qt_evac, 1)
                    for k in range(8):
                        kp, t, quad = k // 4, k // 2 % 2, k % 2
                        if k % 4 == 3:
                            act.wait_ge(piece_done, KEY0 + kp + 1)
                        else:
                            act.wait_ge(key_done, 3 * kp + k % 4 + 1)
                        nc.scalar.copy(S[:, t, 8 * kp + 4 * quad:8 * kp + 4 * quad + 4, :],
                                       bank[k % 4].rearrange("p (b n) -> p b n", b=4)).then_inc(key_evac, 1)

                    def gelu(dst, b):
                        nc.scalar.activation(dst, bank[b].rearrange("p (e n) -> p e n", e=2),
                                             ACT.Gelu).then_inc(gelu_done, 1)

                    for s in range(SLOTS):
                        act.wait_ge(piece_done, U0 + s + 1)
                        gelu(G[:, 2 * s:2 * s + 2, :], 4 + s)

                    def rounds_gelu(lo, hi):
                        with act.Fori(lo, hi) as r:
                            for s in range(SLOTS):
                                act.wait_ge(piece_done, r * SLOTS + (U0 + s + 1))
                                act.wait_ge(s_par, 16)
                                gelu(G[:, bass.ds(r * (2 * SLOTS) + 2 * s, 2), :], 4 + s)

                    rounds_gelu(1, 8)
                    for t in range(TT):
                        act.wait_ge(rt_sub, t + 1)
                        nc.scalar.activation(VC[:, t, :, :], VC[:, t, :, :], ACT.Exp).then_inc(rt_exp, 1)
                    act.wait_ge(rt_ready, 3 * TT)
                    act.wait_ge(piece_done, U0 + 8 * SLOTS + 1)
                    gelu(G[:, 64:66, :], 4)
                    for s in range(1, SLOTS):
                        act.wait_ge(piece_done, U0 + 8 * SLOTS + s + 1)
                        gelu(G[:, 64 + 2 * s:66 + 2 * s, :], 4 + s)
                    rounds_gelu(9, N_U // SLOTS)

                    def one_hot(g):
                        nc.scalar.activation(O2[:, 4 * g:4 * g + 4, :], D2[:, 4 * g:4 * g + 4, :], ACT.Relu,
                                             bias=1.0, scale=-1.0).then_inc(o2_ready, 1)

                    act.wait_ge(piece_done, V0)
                    for g in range(2):
                        act.wait_ge(d2_ready, g + 1)
                        one_hot(g)
                    with act.Fori(1, SEQ // 8) as r:
                        for g in range(2):
                            act.wait_ge(d2_ready, r * 2 + (g + 1))
                            act.wait_ge(w_done, r * 2 + (g - 1))
                            one_hot(g)

                @block.vector
                def _(dve):
                    n = [0]

                    def step(ins):
                        n[0] += 1
                        ins.then_inc(dve_step, 1)
                        dve.wait_ge(dve_step, n[0])

                    V = nc.vector

                    def newton(v, r, t):
                        step(V.tensor_tensor(t, r, r, ALU.mult))
                        step(V.tensor_tensor(t, t, v, ALU.mult))
                        step(V.tensor_scalar(t, t, -0.5, 1.5, ALU.mult, ALU.add))
                        step(V.tensor_tensor(r, r, t, ALU.mult))

                    def norm(k, weight):
                        dve.wait_ge(ssq_done, k + 1)
                        V.tensor_scalar(var[:, :], bank[7][:, 0:SEQ], 1.0 / D, EPS, ALU.mult, ALU.add).then_inc(var_ready, 1)
                        dve.wait_ge(var_ready, k + 1)
                        dve.wait_ge(rs_ready, k + 1)
                        newton(var[:, :], rs[:, :], nt[:, :])
                        for c in range(DC):
                            V.scalar_tensor_tensor(out=H[:, c, :], in0=X[:, c, :], scalar=pr(weight, c, c + 1),
                                                   in1=rs[:, :], op0=ALU.mult, op1=ALU.mult).then_inc(h_ready, 1)

                    def rope(y, cos, sin, half, heads):
                        w = TT * heads * 2 * half
                        a = TA[:, 0:w].rearrange("p (t h d) -> p t h d", t=TT, h=heads)
                        b = TB[:, 1024:1024 + w].rearrange("p (t h d) -> p t h d", t=TT, h=heads)
                        c = bc(cos.rearrange("p (t d) -> p t d", t=TT), 2, heads)
                        s = bc(sin.rearrange("p (t d) -> p t d", t=TT), 2, heads)
                        V.tensor_tensor(a, y, c, ALU.mult)
                        V.tensor_tensor(b[:, :, :, 0:half], y[:, :, :, half:], s[:, :, :, 0:half], ALU.mult)
                        step(V.tensor_tensor(b[:, :, :, half:], y[:, :, :, 0:half], s[:, :, :, half:], ALU.mult))
                        return V.tensor_tensor(y, a, b, ALU.add)

                    def silu_factor(e):
                        step(V.tensor_scalar(e, e, 1.0, None, ALU.add))
                        step(V.reciprocal(e, e))

                    def attention_scores(g, buf, first):
                        for h in range(NH):
                            dve.wait_ge(sc_done, first + h + 1)
                            V.tensor_tensor(buf[:, h, :], bank[4 + h % 2][:, 0:384], cn("negq"), ALU.add).then_inc(sc_evac, 1)
                        dve.wait_ge(sc_evac, first + NH)
                        V.tensor_reduce(mx[:, 0:4], buf[:, :, 0:P], AX.X, ALU.max)
                        step(V.tensor_reduce(mx[:, 4:8], buf[:, :, P:3 * P], AX.X, ALU.max))
                        V.tensor_scalar(negm[g], mx, -(HD ** -0.5), None, ALU.mult).then_inc(negm_ready, 1)

                    def heads(flat):
                        return flat.rearrange("p (t h d) -> p t h d", t=TT, h=NH)

                    def columns(f8):
                        return bc(f8.rearrange("p (t h) -> p t h", t=TT), 3, HD)

                    def m_part(c):
                        return M[:, :, c:c + GW].rearrange("p t (h d) -> p t h d", h=NH)

                    def nsa_factor(g, kind):
                        dve.wait_ge(exp_done, 8 * g + 8)
                        step(V.reciprocal(rinv[g], rsum[g]))
                        if kind is not None:
                            step(V.tensor_tensor(rinv[g].rearrange("p (t h) -> p t h", t=TT),
                                                 rinv[g].rearrange("p (t h) -> p t h", t=TT),
                                                 gate.rearrange("p (t k h) -> p t k h", t=TT, k=3)[:, :, kind, :],
                                                 ALU.mult))

                    dve.wait_ge(s_par, 16)
                    norm(0, "norm_mix")

                    dve.wait_ge(padded, 1)
                    for b in range(6):
                        dve.wait_ge(evac, b // 2 + 1)
                        w = pr("conv_w").rearrange("p (b j) -> p b j", b=6)
                        step(V.tensor_scalar(XC[:, b, :], XB[:, b, 0:SEQ], w[:, b, 0:1], pr("conv_b", b, b + 1),
                                             ALU.mult, ALU.add))
                        for j in range(1, CONV):
                            ins = V.scalar_tensor_tensor(out=XC[:, b, :], in0=XB[:, b, j:j + SEQ], scalar=w[:, b, j:j + 1],
                                                         in1=XC[:, b, :], op0=ALU.mult, op1=ALU.add)
                            if j < CONV - 1:
                                step(ins)
                            else:
                                ins.then_inc(conv_ready, 1)

                    dve.wait_ge(evac, 5)
                    rope(Y[:, :, K_WIN:K_WIN + 384].rearrange("p t (b n) -> p t b n", n=P)[:, :, :, 0:ROPE16],
                         cn("c16"), cn("s16"), ROPE16 // 2, 3).then_inc(roped, 1)
                    x8 = dtx.rearrange("p (t h) -> p t h", t=TT)
                    step(V.tensor_tensor(x8, Y[:, :, DT:DT + NH], bc(pr("dt_bias"), 1, TT), ALU.add))
                    step(V.tensor_scalar(dtz, dtx, -1.0, None, ALU.mult))
                    V.tensor_tensor(dte, dtx, dtz, ALU.min).then_inc(dt_abs, 1)
                    dve.wait_ge(conv_exp, 1)
                    step(V.tensor_scalar(CE[:, :, :], CE[:, :, :], 1.0, None, ALU.add))
                    step(V.reciprocal(CE[:, :, :], CE[:, :, :]))
                    V.tensor_tensor(XC[:, :, :], XC[:, :, :], CE[:, :, :], ALU.mult).then_inc(xc_ready, 1)
                    dve.wait_ge(evac, 6)
                    rope(Y[:, :, NSA_Q:NSA_Q + GW].rearrange("p t (b n) -> p t b n", n=HD)[:, :, :, 0:ROPE16],
                         cn("c16"), cn("s16"), ROPE16 // 2, NH).then_inc(roped, 1)
                    dve.wait_ge(tr_evac, 1)
                    for s, pe_name in enumerate(("pe_k", "pe_v")):
                        k2 = K2[:, s, :].rearrange("p (c j e) -> p e j c", e=2, j=CMP_STRIDE // 2)
                        for hi in range(2):
                            src = k2[:, 0, :, hi:hi + NCMP]
                            ins = V.tensor_tensor(BL[:, s, 8 * hi:8 * hi + 8, :], src,
                                                  bc(pr(pe_name, 8 * hi, 8 * hi + 8), 2, NCMP), ALU.add)
                            if hi == 1:
                                ins.then_inc(blocks_ready, 1)
                    dve.wait_ge(dt_exp, 1)
                    V.tensor_scalar(dtu, dte, 1.0, None, ALU.add).then_inc(dt_one, 1)
                    dve.wait_ge(dt_one, 1)
                    step(V.tensor_scalar(dtd, dtu, -1.0, None, ALU.add))
                    step(V.tensor_scalar(dtz, dtd, 0.0, None, ALU.is_equal))
                    step(V.tensor_tensor(dtd, dtd, dtz, ALU.add))
                    step(V.reciprocal(dtd, dtd))
                    dve.wait_ge(dt_ln, 1)
                    step(V.tensor_tensor(dtl, dtl, dtz, ALU.add))
                    step(V.tensor_tensor(dtl, dtl, dtd, ALU.mult))
                    step(V.tensor_tensor(dtl, dtl, dte, ALU.mult))
                    step(V.tensor_scalar(dtx, dtx, 0.0, None, ALU.max))
                    step(V.tensor_tensor(dtx, dtx, dtl, ALU.add))
                    dve.wait_ge(dt_exp, 2)
                    step(V.tensor_scalar(avec, avec, -1.0, None, ALU.mult))
                    V.tensor_tensor(dta.rearrange("p (t h) -> p t h", t=TT), x8, bc(avec, 1, TT), ALU.mult).then_inc(da_ready, 1)
                    dve.wait_ge(da_ready, 1)
                    V.tensor_copy(DA[:, :, :, :], bc(dta.rearrange("p (t h) -> p t h", t=TT), 3, P)).then_inc(da_ready, 1)
                    dve.wait_ge(z_exp, 1)
                    silu_factor(gate)
                    for g in range(2):
                        dve.wait_ge(sc_done, g + 1)
                        V.tensor_copy(GS[:, g, :], bank[4 + g][:, 0:384]).then_inc(sc_evac, 1)
                    attention_scores(0, SC4[0], 2)
                    attention_scores(1, SC4[1], 6)
                    dve.wait_ge(kcvc_done, 1)
                    V.tensor_copy(KC, bank[7][:, 64:96]).then_inc(kc_ready, 1)
                    V.tensor_tensor(VB[:, :, :], bc(bank[7][:, 96:160], 1, NH), bc(cn("blkd"), 2, HD),
                                    ALU.mult).then_inc(vb_ready, 1)
                    dve.wait_ge(acs_done, 1)
                    cs_e = CS[:, :, :, :].rearrange("p t (i e) c -> p e t i c", e=2)
                    for e in range(2):
                        V.tensor_tensor(cs_e[:, e], bank[7 - e][:, 256:384].rearrange("p (t i c) -> p t i c", t=TT, i=2),
                                        bc(cn("cmpneg").rearrange("p (t c) -> p t c", t=TT), 2, 2), ALU.add).then_inc(b6_free, 1)
                    dve.wait_ge(b6_free, 2)
                    V.tensor_copy(acs, bank[6][:, 0:8]).then_inc(b6_free, 1)
                    cs8 = CS[:, :, :, :].rearrange("p t h c -> p (t h) c")
                    step(V.tensor_reduce(cmx, cs8, AX.X, ALU.max))
                    V.tensor_tensor(cs8, cs8, bc(cmx, 2, CPAD), ALU.subtract).then_inc(cs_ready, 1)
                    nsa_factor(0, 2)
                    dve.wait_ge(pv_done, 1)
                    V.tensor_tensor(m_part(768), heads(bank[6]), columns(rinv[0]), ALU.mult).then_inc(pv_evac, 1)

                    def decays(pair):
                        dve.wait_ge(acr_done, pair + 1)
                        for i in range(2):
                            h = 2 * pair + i
                            V.scalar_tensor_tensor(out=SEG[:, h, 0:256], in0=bank[7][:, i * SEQ:(i + 1) * SEQ],
                                                   scalar=acs[:, h:h + 1], in1=cn("negk", 0, 256),
                                                   op0=ALU.subtract, op1=ALU.add)
                            V.scalar_tensor_tensor(out=SEG[:, h, 256:384], in0=bank[7][:, i * SEQ + P:(i + 1) * SEQ],
                                                   scalar=acs[:, 4 + h:5 + h], in1=cn("negk", 256, 384),
                                                   op0=ALU.subtract, op1=ALU.add).then_inc(seg_ready, 1)

                    dve.wait_ge(b6_free, 3)
                    decays(0)
                    nsa_factor(1, 1)
                    dve.wait_ge(pv_done, 2)
                    V.tensor_tensor(heads(TA[:, 0:512]), heads(bank[6]), columns(rinv[1]), ALU.mult).then_inc(pv_evac, 1)
                    dve.wait_ge(pv_evac, 2)
                    step(V.tensor_tensor(m_part(768), m_part(768), heads(TA[:, 0:512]), ALU.add))
                    dve.wait_ge(evac, 8)
                    rope(Y[:, :, MOBA_Q:MOBA_Q + 2 * GW].rearrange("p t (b n) -> p t b n", n=HD)[:, :, :, 0:ROPE16],
                         cn("c16"), cn("s16"), ROPE16 // 2, 2 * NH).then_inc(roped, 1)
                    decays(1)
                    dve.wait_ge(cs_exp, 1)
                    step(V.tensor_reduce(csum, cs8, AX.X, ALU.add))
                    step(V.reciprocal(cinv, csum))
                    c8 = cinv.rearrange("p (t h) -> p t h", t=TT)
                    step(V.tensor_tensor(c8, c8, bc(cn("any"), 2, NH), ALU.mult))
                    step(V.tensor_tensor(c8, c8, gate.rearrange("p (t k h) -> p t k h", t=TT, k=3)[:, :, 0, :], ALU.mult))
                    dve.wait_ge(evac, 11)
                    dve.wait_ge(roped, 3)
                    rope(Y[:, :, RET_Q:RET_Q + 2 * GW].rearrange("p t (b n) -> p t b n", n=HD),
                         cn("cr"), cn("sr"), HD // 2, 2 * NH).then_inc(roped, 1)
                    attention_scores(2, SC4[0], 10)
                    dve.wait_ge(tr_evac, 3)
                    V.tensor_tensor(heads(XDT[:, :, :].rearrange("p t n -> p (t n)")),
                                    heads(XS[:, :, :].rearrange("p t n -> p (t n)")), columns(dtx), ALU.mult).then_inc(ps_ready, 1)
                    dve.wait_ge(seg_exp, 1)
                    V.tensor_tensor(SEG[:, :, :].rearrange("p (g h) n -> p g h n", g=2),
                                    SEG[:, :, :].rearrange("p (g h) n -> p g h n", g=2), bc(GS[:, :, :], 2, 2),
                                    ALU.mult).then_inc(ps_ready, 1)
                    dve.wait_ge(pv_done, 3)
                    V.tensor_tensor(heads(TA[:, 0:512]), heads(bank[6]), columns(cinv), ALU.mult).then_inc(pv_evac, 1)
                    dve.wait_ge(pv_evac, 3)
                    V.tensor_tensor(m_part(768), m_part(768), heads(TA[:, 0:512]), ALU.add).then_inc(m_ready, 1)
                    for h in range(NH):
                        dve.wait_ge(sc_done, 15 + h)
                        V.tensor_tensor(SC4[1][:, h, :], bank[4 + h % 2][:, 0:384], cn("dret", 384 * h, 384 * (h + 1)),
                                        ALU.mult).then_inc(sc_evac, 1)
                    ya = TA[:, 0:512]
                    yb = TA[:, 512:1024]
                    step(V.tensor_tensor(heads(yb), heads(XS[:, :, :].rearrange("p t n -> p (t n)")),
                                         bc(bc(pr("ssm_d"), 2, HD), 1, TT), ALU.mult))
                    dve.wait_ge(pv_done, 4)
                    V.tensor_tensor(ya, bank[6], yb, ALU.add).then_inc(pv_evac, 1)
                    dve.wait_ge(z_exp, 3)
                    silu_factor(TB[:, 0:1024])
                    dve.wait_ge(pv_evac, 4)
                    step(V.tensor_tensor(ya, ya, TB[:, 512:1024], ALU.mult))
                    yt = ya.rearrange("p (t n) -> p t n", t=TT)
                    step(V.tensor_tensor(yt, yt, Y[:, :, SSM_Z:SSM_Z + GW], ALU.mult))
                    step(V.tensor_tensor(yb, ya, ya, ALU.mult))
                    step(V.tensor_reduce(gvar[:, 0:4], yb.rearrange("p (k n) -> p k n", n=P), AX.X, ALU.add))
                    V.tensor_scalar(gvar[:, 0:4], gvar[:, 0:4], 1.0 / P, EPS, ALU.mult, ALU.add).then_inc(g_var, 1)
                    nsa_factor(2, None)
                    dve.wait_ge(pv_done, 5)
                    V.tensor_tensor(m_part(256), heads(bank[6]), columns(rinv[2]), ALU.mult).then_inc(pv_evac, 1)
                    dve.wait_ge(pv_evac, 5)
                    dve.wait_ge(g_rs, 1)
                    newton(gvar[:, 0:4], grs[:, 0:4], gnt[:, 0:4])
                    V.tensor_tensor(M[:, :, 512:768].rearrange("p t (g n) -> p t g n", g=2),
                                    ya.rearrange("p (t g n) -> p t g n", t=TT, g=2),
                                    bc(grs[:, 0:4].rearrange("p (t g) -> p t g", t=TT), 3, P), ALU.mult).then_inc(m_ready, 1)
                    dve.wait_ge(m_ready, 2)
                    dve.wait_ge(pv_done, 6)
                    V.tensor_copy(ya, bank[6]).then_inc(pv_evac, 1)
                    dve.wait_ge(pv_evac, 6)
                    step(V.tensor_tensor(yb, ya, ya, ALU.mult))
                    step(V.tensor_reduce(gvar, yb.rearrange("p (k n) -> p k n", n=HD), AX.X, ALU.add))
                    V.tensor_scalar(gvar, gvar, 1.0 / HD, EPS, ALU.mult, ALU.add).then_inc(g_var, 1)
                    step(V.tensor_tensor(ya, ya, TB[:, 0:512], ALU.mult))
                    step(V.tensor_tensor(yt, yt, Y[:, :, RET_G:RET_G + GW], ALU.mult))
                    dve.wait_ge(g_rs, 2)
                    newton(gvar, grs, gnt)
                    V.tensor_tensor(m_part(0), heads(ya), columns(grs), ALU.mult).then_inc(m_ready, 1)
                    for k in range(N_OUT):
                        dve.wait_ge(piece_done, OUT0 + k + 1)
                        V.tensor_tensor(X[:, 2 * k:2 * k + 2, :], X[:, 2 * k:2 * k + 2, :],
                                        bank[k % 2].rearrange("p (k m) -> p k m", k=2), ALU.add).then_inc(x_added, 1)

                    dve.wait_ge(x_added, N_OUT)
                    norm(1, "norm_ffn")

                    def top16(rows, vals, idxs):
                        for r, v in zip(rows, vals):
                            ins = V.max(v[:, 0:8], r)
                        step(ins)
                        for r, v, i in zip(rows, vals, idxs):
                            V.max_index(i[:, 0:8], v[:, 0:8], r)
                            ins = V.match_replace(r, v[:, 0:8], r, -3e38)
                        step(ins)
                        for r, v in zip(rows, vals):
                            ins = V.max(v[:, 8:16], r)
                        step(ins)
                        for r, v, i in zip(rows, vals, idxs):
                            ins = V.max_index(i[:, 8:16], v[:, 8:16], r)
                        step(ins)

                    for kp in range(N_KEYS):
                        for t in range(TT):
                            dve.wait_ge(key_evac, 4 * kp + 2 * t + 2)
                            bs = range(8 * kp, 8 * kp + 8)
                            top16([S[:, t, b, :] for b in bs], [V16[:, t, b, :] for b in bs],
                                  [I16[:, t, b, :] for b in bs])
                    for t in range(TT):
                        v = V16[:, t, :, :].rearrange("p (h e) k -> p e h k", e=2)
                        step(V.tensor_tensor(CAND[t].rearrange("p h (a b) -> p h a b", a=TOPK),
                                             bc(v[:, 0], 3, TOPK), bc(v[:, 1], 2, TOPK), ALU.add))
                        top16([CAND[t][:, h, :] for h in range(HEADS)], [VC[:, t, h, :] for h in range(HEADS)],
                              [PC[:, t, h, :] for h in range(HEADS)])
                        step(V.tensor_copy(esum[:, 0:8], VC[:, t, :, 0]))
                        V.tensor_tensor(VC[:, t, :, :], VC[:, t, :, :], bc(esum[:, 0:8], 2, TOPK),
                                        ALU.subtract).then_inc(rt_sub, 1)
                        for e in range(2):
                            if e == 0:
                                step(V.tensor_scalar(PAB, PC[:, t, :, :], 4, None, ALU.logical_shift_right))
                            else:
                                step(V.tensor_scalar(PAB, PC[:, t, :, :], TOPK - 1, None, ALU.bitwise_and))
                            step(V.tensor_tensor(EQ, bc(PAB, 3, TOPK), bc(bc(cn("iota", 0, TOPK), 1, TOPK), 1, HEADS),
                                                 ALU.is_equal))
                            step(V.tensor_tensor(EQ2, EQ, bc(I16[:, t, :, :].rearrange("p (h e) k -> p e h k", e=2)[:, e], 2, TOPK),
                                                 ALU.mult))
                            V.tensor_reduce(RT[:, t, e, :].rearrange("p (h k) -> p h k", h=HEADS), EQ2, AX.X,
                                            ALU.add).then_inc(rt_ready, 1)
                            dve.wait_ge(rt_ready, 3 * t + e + 1)
                        dve.wait_ge(rt_exp, t + 1)
                        step(V.tensor_reduce(esum[:, 0:8], VC[:, t, :, :], AX.X, ALU.add))
                        step(V.reciprocal(esum[:, 8:16], esum[:, 0:8]))
                        V.tensor_tensor(RT[:, t, 2, :].rearrange("p (h k) -> p h k", h=HEADS), VC[:, t, :, :],
                                        bc(esum[:, 8:16], 2, TOPK), ALU.mult).then_inc(rt_ready, 1)
                    for k in range(3):
                        dve.wait_ge(rt_tr, k + 1)
                        V.tensor_copy(slotT[:, k, :], bank[k][:, 0:SEQ]).then_inc(rt_free, 1)
                    dve.wait_ge(rt_free, 3)

                    def one_hot(t0, g):
                        for i in range(4):
                            ins = V.tensor_scalar(O1[:, 4 * g + i, :], cn("iota"), slotT[:, 0, bass.ds(t0 + i, 1)],
                                                  slotT[:, 2, bass.ds(t0 + i, 1)], ALU.is_equal, ALU.mult)
                        ins.then_inc(o1_ready, 1)

                    def weigh(t0, g):
                        V.tensor_tensor(G[:, :, bass.ds(t0, 4)], G[:, :, bass.ds(t0, 4)],
                                        bank[4 + g].rearrange("p (i e) -> p e i", i=4), ALU.mult).then_inc(w_used, 1)

                    dve.wait_ge(piece_done, V0)
                    for g in range(2):
                        one_hot(4 * g, g)
                    with dve.Fori(1, SEQ // 8) as r:
                        for g in range(2):
                            dve.wait_ge(w_done, r * 2 + (g - 1))
                            weigh(r * 8 + (4 * g - 8), g)
                            one_hot(r * 8 + 4 * g, g)
                    for g in range(2):
                        dve.wait_ge(w_done, SEQ // 4 - 1 + g)
                        weigh(SEQ - 8 + 4 * g, g)
                    dve.wait_ge(acc_done, 1)
                    for k in range(4):
                        V.tensor_tensor(X[:, 2 * k:2 * k + 2, :], X[:, 2 * k:2 * k + 2, :],
                                        bank[k].rearrange("p (k m) -> p k m", k=2), ALU.add).then_inc(x_added, 1)
                    dve.wait_ge(x_added, 8)

            ids = [s.num for s in sems]
            nc.gpsimd.sem_clear(range(min(ids), max(ids) + 1))
            nc.all_engine_barrier()

        with nc.Block() as block:
            @block.scalar
            def _(act):
                nc.scalar.activation(SQ[:, :, :], X[:, :, :], ACT.Square).then_inc(f_sq, 1)
                act.wait_ge(f_var, 1)
                nc.scalar.activation(rs[:, :], var[:, :], ACT.Ln).then_inc(f_rs, 1)
                act.wait_ge(f_rs, 1)
                nc.scalar.activation(rs[:, :], rs[:, :], ACT.Exp, scale=-0.5).then_inc(f_rs, 1)

            @block.tensor
            def _(pe):
                pe.wait_ge(f_sq, 1)
                for c in range(DC):
                    mm = nc.tensor.matmul(bank[0][:, 0:SEQ], ones[:, :], SQ[:, c, :], start=(c == 0), stop=(c == DC - 1))
                mm.then_inc(f_ssq, 1)

            @block.vector
            def _(dve):
                dve.wait_ge(f_ssq, 1)
                nc.vector.tensor_scalar(var[:, :], bank[0][:, 0:SEQ], 1.0 / D, EPS, ALU.mult, ALU.add).then_inc(f_var, 1)
                dve.wait_ge(f_var, 1)
                dve.wait_ge(f_rs, 2)
                nc.vector.tensor_tensor(nt[:, :], rs[:, :], rs[:, :], ALU.mult).then_inc(f_step, 1)
                dve.wait_ge(f_step, 1)
                nc.vector.tensor_tensor(nt[:, :], nt[:, :], var[:, :], ALU.mult).then_inc(f_step, 1)
                dve.wait_ge(f_step, 2)
                nc.vector.tensor_scalar(nt[:, :], nt[:, :], -0.5, 1.5, ALU.mult, ALU.add).then_inc(f_step, 1)
                dve.wait_ge(f_step, 3)
                nc.vector.tensor_tensor(rs[:, :], rs[:, :], nt[:, :], ALU.mult).then_inc(f_step, 1)
                dve.wait_ge(f_step, 4)
                for c in range(DC):
                    nc.vector.scalar_tensor_tensor(out=H[:, c, :], in0=X[:, c, :], scalar=pr("norm_final", c, c + 1),
                                                   in1=rs[:, :], op0=ALU.mult, op1=ALU.mult).then_inc(f_out, 1)

            @block.sync
            def _(sp):
                sp.wait_ge(f_out, DC)
                sp.dma_start(out_t, H[:, :, :]).then_inc(stored, 16)
                sp.wait_ge(stored, 16)


def chunked(w):
    L, k, n = w.shape
    return w.reshape(L, k // P, P, n // 256, 256).transpose(0, 3, 2, 1, 4).reshape(L, n // 256, P, PIECE)


def lay_out(inp):
    f = {k: np.asarray(v) for k, v in inp.items()}
    L = DEPTH
    w_in = f["w_in"]
    off, at = {}, 0
    for name, width in (("ret_q", GW), ("ret_k", GW), ("ret_v", GW), ("ret_g", GW), ("moba_q", GW), ("moba_k", GW),
                        ("moba_v", GW), ("z", GW), ("xbc", 768), ("dt", 4), ("nsa_q", GW), ("k_cmp", HD),
                        ("v_cmp", HD), ("k_slc", HD), ("v_slc", HD), ("k_win", HD), ("v_win", HD), ("gate", 12)):
        off[name] = slice(at, at + width)
        at += width
    col = {k: w_in[:, :, s] for k, s in off.items()}
    g2 = np.zeros((L, D, 256), np.float32)
    for name, c in (("gate", GATE), ("dt", DT), ("k_win", K_WIN), ("v_win", V_WIN)):
        g2[:, :, c:c + col[name].shape[2]] = col[name]
    g1 = np.concatenate([col[k] for k in ("k_cmp", "v_cmp", "k_slc", "v_slc")], 2)
    stream = np.zeros((L, PIECES, P, PIECE), np.float32)
    stream[:, 0:3] = chunked(col["xbc"])
    for n, w in ((3, g1), (4, g2), (5, col["nsa_q"]), (6, col["moba_q"]), (11, col["moba_k"]), (12, col["moba_v"]),
                 (13, col["ret_q"]), (14, col["ret_k"]), (15, col["ret_v"]), (16, col["ret_g"]), (17, col["z"])):
        stream[:, n:n + 1] = chunked(w)
    for n, name in ((7, "nsa_w1_k"), (9, "nsa_w1_v")):
        w = f[name].reshape(L, CHUNKS, P, 2, P).transpose(0, 3, 2, 1, 4)
        stream[:, n:n + 2] = w.reshape(L, 2, P, PIECE)
    stream[:, OUT0:OUT0 + N_OUT] = chunked(f["w_out"])
    stream[:, WQ0:WQ0 + N_WQ] = chunked(f["peer_wq"])
    keys = f["peer_keys"].reshape(L, N_KEYS, 8, KEYS, P).transpose(0, 1, 4, 2, 3)
    stream[:, KEY0:KEY0 + N_KEYS, :, 0:8 * KEYS] = keys.reshape(L, N_KEYS, P, 8 * KEYS)
    u = f["peer_u"].reshape(L, N_U, 2, P, DC, P).transpose(0, 1, 5, 2, 4, 3)
    stream[:, U0:U0 + N_U] = u.reshape(L, N_U, P, PIECE)
    v = f["peer_v"].reshape(L, N_V, 2, P, D).transpose(0, 1, 3, 2, 4)
    stream[:, V0:V0 + N_V] = v.reshape(L, N_V, P, PIECE)

    params = np.zeros((L, P, NPARAM), np.float32)

    def put(name, a):
        lo, hi = PARAMS[name]
        params[:, :, lo:hi] = a.reshape(a.shape[0], P, hi - lo)

    def on_partitions(a, n):
        return a.reshape(L, n, P).transpose(0, 2, 1)

    put("norm_mix", on_partitions(f["norm_mix"], DC))
    put("norm_ffn", on_partitions(f["norm_ffn"], DC))
    put("conv_w", f["ssm_conv_w"].reshape(L, CONV, 6, P).transpose(0, 3, 2, 1))
    put("conv_b", on_partitions(f["ssm_conv_b"], 6))
    put("ret_norm", on_partitions(f["ret_norm"], 2))
    put("ssm_norm", on_partitions(f["ssm_norm"], 2))
    put("pe_k", on_partitions(f["nsa_pe_k"], CHUNKS))
    put("pe_v", on_partitions(f["nsa_pe_v"], CHUNKS))
    w2k = f["nsa_w2_k"].reshape(L, 2, P, 1, HD)
    put("w2k", np.broadcast_to(w2k, (L, 2, P, 2, HD)).transpose(0, 2, 1, 3, 4))
    put("w2v", f["nsa_w2_v"].reshape(L, 2, P, HD).transpose(0, 2, 1, 3))
    for name, src in (("dt_bias", "ssm_dt_bias"), ("a_log", "ssm_a_log"), ("ssm_d", "ssm_d")):
        put(name, np.broadcast_to(f[src][:, None, :], (L, P, NH)))
    put("norm_final", np.broadcast_to(f["norm_final"].reshape(1, DC, P).transpose(0, 2, 1), (L, P, DC)))
    x_t = np.ascontiguousarray(f["x"].reshape(SEQ, DC, P).transpose(2, 1, 0))
    return {"x_t": x_t, "stream": stream, "params": params, "consts": shape_constants()}


def kernel(**inputs):
    import concourse.bacc as bacc
    from concourse.bass_utils import run_bass_kernel_spmd as run

    nc = bacc.Bacc("TRN2", target_bir_lowering=False, num_devices=1)
    arrays = lay_out(inputs)
    args = [nc.dram_tensor(k, a.shape, F32, kind="ExternalInput").ap() for k, a in arrays.items()]
    args.append(nc.dram_tensor("out_t", (P, DC, SEQ), F32, kind="ExternalOutput").ap())
    program(nc, *args)
    r = run(nc, [arrays], core_ids=[0])
    out = r.results[0]["out_t"]
    return out.transpose(2, 1, 0).reshape(1, SEQ, D)
```

```python
from contextlib import ExitStack

import numpy as np

import concourse.bass as bass
from concourse import mybir

F32 = mybir.dt.float32
F32R = mybir.dt.float32r
BF16 = mybir.dt.bfloat16
U32 = mybir.dt.uint32
ALU = mybir.AluOpType
ACT = mybir.ActivationFunctionType
AX = mybir.AxisListType

P = 128
DEPTH, SEQ, D = 2, 256, 1024
TT = SEQ // P
DC = D // P
HD, NH = 64, 4
GW = HD * NH
NEG = -1e30
EPS = 1e-6
CONV = 4
CMP_LEN, CMP_STRIDE = 32, 16
NCMP = (SEQ - CMP_LEN) // CMP_STRIDE + 1
CPAD = 32
CHUNKS = CMP_LEN * HD // P
ROPE16 = 16
HEADS, KEYS, TOPK = 8, 128, 16
EXPERTS = KEYS * KEYS

SLOTS = 4
PIECE = 1024
N_XBC, N_PROJ, N_OUT, N_WQ = 3, 18, 4, 8
OUT0 = N_PROJ
WQ0 = OUT0 + N_OUT
KEY0 = 2 * (WQ0 + N_WQ)
N_KEYS = 2
U0 = KEY0 + N_KEYS
HK = KEYS // 2
EXP_ROUND, TURN_ROUND = 10, 13
TILES = EXPERTS // P
V0 = U0 + TILES
PIECES = V0 + TILES
Y_BLOCK = {3: 1, 4: 0, 5: 2, 6: 3, 11: 4, 12: 5, 13: 6, 14: 7, 15: 8, 16: 9, 17: 10}
W1 = (7, 8, 9, 10)
GATE, DT, K_WIN, V_WIN, K_CMP, V_CMP, K_SLC, V_SLC = 0, 12, 128, 192, 256, 320, 384, 448
NSA_Q, MOBA_Q, MOBA_K, MOBA_V, RET_Q, RET_K, RET_V, RET_G, SSM_Z = (256 * i for i in range(2, 11))
YW = 11 * 256

CONSTS = {}
_at = 0
for _name, _width in (("ident", 128), ("tri", 384), ("negk", 384), ("negq", 384), ("gamma", 16),
                      ("cr", 128), ("sr", 128), ("c16", 32), ("s16", 32), ("cmpneg", 64), ("any", 2),
                      ("blkd", 4), ("iota", 128)):
    CONSTS[_name] = (_at, _at + _width)
    _at += _width
NCONST = _at
PARAMS = {}
_at = 0
for _name, _width in (("norm_mix", 8), ("norm_ffn", 8), ("conv_w", 24), ("conv_b", 6), ("ret_norm", 2),
                      ("ssm_norm", 2), ("pe_k", 16), ("pe_v", 16), ("w2k", 256), ("w2v", 128),
                      ("dt_bias", 4), ("a_log", 4), ("ssm_d", 4), ("norm_final", 8)):
    PARAMS[_name] = (_at, _at + _width)
    _at += _width
NPARAM = _at


def shape_constants():
    c = np.zeros((P, NCONST), np.float32)

    def put(name, a):
        lo, hi = CONSTS[name]
        c[:, lo:hi] = np.asarray(a, np.float32).reshape(P, hi - lo)

    p = np.arange(P)[:, None]
    t = np.arange(SEQ)
    put("ident", np.eye(P))
    age = np.concatenate([t[None, :] - p, t[None, P:] - (p + P)], 1)
    put("tri", age >= 0)
    put("negk", np.where(age >= 0, 0.0, NEG))
    ageq = np.concatenate([p - t[None, :P], p + P - t[None, :]], 1)
    put("negq", np.where(ageq >= 0, 0.0, NEG))
    lg = np.log1p(-np.exp2(-5.0 - np.arange(NH)))
    rise = (t.reshape(TT, P).T)[:, :, None] * lg
    put("gamma", np.concatenate([np.exp(rise), np.exp(-rise) * HD ** -0.5], 2))

    def rope(n, theta):
        inv = (1.0 / (np.float32(theta) ** (np.arange(0, n, 2, dtype=np.float32) / np.float32(n)))).astype(np.float32)
        ang = (t.astype(np.float32)[:, None] * inv[None, :]).astype(np.float32).astype(np.float64)
        co, si = np.cos(ang), np.sin(ang)
        both = [np.concatenate([co, co], 1), np.concatenate([-si, si], 1)]
        return [b.reshape(TT, P, n).transpose(1, 0, 2) for b in both]

    cr, sr = rope(HD, 10000.0)
    put("cr", cr)
    put("sr", sr)
    c16, s16 = rope(ROPE16, 500000.0)
    put("c16", c16)
    put("s16", s16)
    tok = t.reshape(TT, P).T[:, :, None]
    j = np.arange(CPAD)[None, None, :]
    ok = (j * CMP_STRIDE + CMP_LEN - 1 <= tok) & (j < NCMP)
    put("cmpneg", np.where(ok, 0.0, NEG))
    put("any", ok.any(-1))
    put("blkd", p // CPAD == np.arange(NH)[None, :])
    put("iota", np.broadcast_to(np.arange(P)[None, :], (P, P)))
    return c


def bc(ap, axis, n):
    u = ap.unsqueeze(axis)
    shape = list(u.shape)
    shape[axis] = n
    return u.broadcast_to(shape)


def program(nc, x_t, stream, params, consts, out_t):
    ctx = ExitStack()
    with ctx:
        def sb(name, shape, dt=F32):
            return ctx.enter_context(nc.sbuf_tensor(name, shape, dt))

        sems = []

        def sem(name):
            s = ctx.enter_context(nc.semaphore(name))
            sems.append(s)
            return s

        ld0 = ctx.enter_context(nc.semaphore("ld0"))
        stored = ctx.enter_context(nc.semaphore("stored"))
        f_sq = ctx.enter_context(nc.semaphore("f_sq"))
        f_ssq = ctx.enter_context(nc.semaphore("f_ssq"))
        f_var = ctx.enter_context(nc.semaphore("f_var"))
        f_rs = ctx.enter_context(nc.semaphore("f_rs"))
        f_step = ctx.enter_context(nc.semaphore("f_step"))
        f_out = ctx.enter_context(nc.semaphore("f_out"))
        s_ones = ctx.enter_context(nc.semaphore("s_ones"))

        s_par = sem("s_par")
        landed = [sem(f"landed{i}") for i in range(SLOTS)]
        piece_done = sem("piece_done")
        hi_ready = sem("hi_ready")
        hi_used = sem("hi_used")
        lo_ready = sem("lo_ready")
        gh_ready = sem("gh_ready")
        gl_ready = sem("gl_ready")
        hh_ready = sem("hh_ready")
        hl_ready = sem("hl_ready")
        sq_ready = sem("sq_ready")
        ssq_done = sem("ssq_done")
        var_ready = sem("var_ready")
        rs_ready = sem("rs_ready")
        h_ready = sem("h_ready")
        act_step = sem("act_step")
        dve_step = sem("dve_step")
        evac = sem("evac")
        padded = sem("padded")
        conv_ready = sem("conv_ready")
        conv_exp = sem("conv_exp")
        xc_ready = sem("xc_ready")
        roped = sem("roped")
        dup_ready = sem("dup_ready")
        dt_abs = sem("dt_abs")
        dt_exp = sem("dt_exp")
        dt_one = sem("dt_one")
        dt_ln = sem("dt_ln")
        da_ready = sem("da_ready")
        tr_done = sem("tr_done")
        tr_evac = sem("tr_evac")
        blocks_ready = sem("blocks_ready")
        hid_ready = sem("hid_ready")
        kcvc_done = sem("kcvc_done")
        kc_ready = sem("kc_ready")
        vb_ready = sem("vb_ready")
        sc_done = sem("sc_done")
        sc_evac = sem("sc_evac")
        negm_ready = sem("negm_ready")
        exp_done = sem("exp_done")
        acs_done = sem("acs_done")
        b6_free = sem("b6_free")
        cs_ready = sem("cs_ready")
        cs_exp = sem("cs_exp")
        acr_done = sem("acr_done")
        seg_ready = sem("seg_ready")
        seg_exp = sem("seg_exp")
        ps_ready = sem("ps_ready")
        pv_done = sem("pv_done")
        pv_evac = sem("pv_evac")
        m_ready = sem("m_ready")
        z_exp = sem("z_exp")
        g_var = sem("g_var")
        g_rs = sem("g_rs")
        x_added = sem("x_added")
        qt_evac = sem("qt_evac")
        key_done = sem("key_done")
        key_evac = sem("key_evac")
        rt_sub = sem("rt_sub")
        rt_exp = sem("rt_exp")
        rt_ready = sem("rt_ready")
        rt_tr = sem("rt_tr")
        rt_free = sem("rt_free")
        gelu_done = sem("gelu_done")
        o_ready = sem("o_ready")
        w_done = sem("w_done")
        w_used = sem("w_used")

        X = sb("X", [P, DC, SEQ])
        H = sb("H", [P, DC, SEQ])
        ring = sb("ring", [P, SLOTS, PIECE])
        HH = sb("HH", [P, DC, SEQ], F32R)
        HL = sb("HL", [P, DC, SEQ], F32R)
        WH = sb("WH", [P, 2, PIECE], F32R)
        WL = sb("WL", [P, 2, PIECE], F32R)
        G = sb("G", [P, KEYS, SEQ])
        CN = sb("CN", [P, NCONST])
        PR = sb("PR", [P, NPARAM])
        ones = sb("ones", [P, P])
        VR = sb("VR", [P, 3, SEQ])
        var, rs = VR[:, 0, :], VR[:, 1, :]
        slotT = sb("slotT", [P, 2, SEQ])
        slotW = VR[:, :, :]
        PS = ctx.enter_context(nc.psum_tensor("PS", [P, 8, 512], F32))

        def cn(name, lo=0, hi=None):
            a, b = CONSTS[name]
            return CN[:, a + lo:(b if hi is None else a + hi)]

        def pr(name, lo=0, hi=None):
            a, b = PARAMS[name]
            return PR[:, a + lo:(b if hi is None else a + hi)]

        ident = cn("ident")
        Gf = G[:, :, :].rearrange("p e t -> p (e t)")
        used = [0]

        def region(width):
            lo = used[0]
            used[0] += width
            assert used[0] <= KEYS * SEQ
            return Gf[:, lo:lo + width]

        Y = region(TT * YW).rearrange("p (t n) -> p t n", t=TT)
        XBW = SEQ + CONV - 1
        XB = region(6 * XBW).rearrange("p (b n) -> p b n", b=6)
        XC = region(6 * SEQ).rearrange("p (b n) -> p b n", b=6)
        XS = region(TT * GW).rearrange("p (t n) -> p t n", t=TT)
        XDT = region(TT * GW).rearrange("p (t n) -> p t n", t=TT)
        T = region(12 * SEQ).rearrange("p (b n) -> p b n", b=12)
        TQ_NSA, TQ_MOBA, TK_MOBA, TQ_RET, TK_RET, TK_WIN, TK_SLC = 0, 2, 4, 6, 8, 10, 11
        SC4 = [region(NH * 384).rearrange("p (h n) -> p h n", h=NH) for _ in range(2)]
        PT = [region(NH * 384).rearrange("p (h n) -> p h n", h=NH) for _ in range(2)]
        SEG = region(NH * 384).rearrange("p (h n) -> p h n", h=NH)
        GS = region(2 * 384).rearrange("p (g n) -> p g n", g=2)
        DA = region(TT * NH * P).rearrange("p (t h n) -> p t h n", t=TT, h=NH)
        Mf = region(TT * D)
        M = Mf.rearrange("p (t n) -> p t n", t=TT)
        CE = Mf[:, 0:6 * SEQ].rearrange("p (b n) -> p b n", b=6)
        MTf = region(DC * SEQ)
        MT = MTf.rearrange("p (c n) -> p c n", c=DC)
        DUP = MTf[:, 0:TT * 6 * P].rearrange("p (t b e n) -> p t b e n", t=TT, b=6, e=2)
        TA = region(1024)
        TB = region(2048)
        K2 = region(2 * SEQ).rearrange("p (s n) -> p s n", s=2)
        BL = region(2 * CHUNKS * NCMP).rearrange("p (s j c) -> p s j c", s=2, j=CHUNKS)
        HV = region(2 * 2 * P).rearrange("p (s b h c) -> p s b h c", s=2, b=2, h=NH)
        KC = region(CPAD)
        VB = region(GW).rearrange("p (h n) -> p h n", h=NH)
        CS = region(TT * NH * CPAD).rearrange("p (t h c) -> p t h c", t=TT, h=NH)
        CP = region(TT * P).rearrange("p (t n) -> p t n", t=TT)
        SM = region(256)
        _s = [0]

        def small(n):
            lo = _s[0]
            _s[0] += n
            assert _s[0] <= 256
            return SM[:, lo:lo + n]

        mx = small(8)
        negm = [small(8) for _ in range(3)]
        rsum = [small(8) for _ in range(3)]
        rinv = [small(8) for _ in range(3)]
        cmx, csum, cinv = small(8), small(8), small(8)
        gate = small(24)
        dtx, dte, dtu, dtl, dtd, dtz, dta = (small(8) for _ in range(7))
        avec = small(4)
        acs = small(8)
        gvar, grs, gnt = small(8), small(8), small(8)

        rbase = 64 * SEQ

        def late(lo, width):
            return Gf[:, rbase + lo:rbase + lo + width]

        QT = late(0, 4096).rearrange("p (b n) -> p b n", b=16)
        S = late(4096, 4096).rearrange("p (t b n) -> p t b n", t=TT, b=16)
        CAND = [late(8192 + 2048 * t, 2048).rearrange("p (h n) -> p h n", h=HEADS) for t in range(TT)]
        EQ = late(0, 2048).rearrange("p (h k a) -> p h k a", h=HEADS, k=TOPK)
        EQ2 = late(2048, 2048).rearrange("p (h k a) -> p h k a", h=HEADS, k=TOPK)
        SQ = late(12288, 2048).rearrange("p (c n) -> p c n", c=DC)
        V16 = late(14336, 512).rearrange("p (t b k) -> p t b k", t=TT, b=16)
        I16 = late(14848, 512).rearrange("p (t b k) -> p t b k", t=TT, b=16).bitcast(U32)
        VC = late(15360, 256).rearrange("p (t h k) -> p t h k", t=TT, h=HEADS)
        PC = late(15616, 256).rearrange("p (t h k) -> p t h k", t=TT, h=HEADS).bitcast(U32)
        late_s = late(15872, 512)
        PAB = late_s[:, 0:128].bitcast(U32).rearrange("p (h k) -> p h k", h=HEADS)
        esum = late_s[:, 128:144]
        nt = late(12288, 256)
        RT = late(12544, 768).rearrange("p (t k n) -> p t k n", t=TT, k=3)

        Hf = H[:, :, :].rearrange("p c n -> p (c n)")
        O1 = Hf[:, 0:768].bitcast(BF16).rearrange("p (s k n) -> p s k n", s=8, k=3)
        O2 = Hf[:, 768:1280].bitcast(BF16).rearrange("p (s n) -> p s n", s=8)
        PART = Hf[:, 1280:1536].bitcast(BF16).rearrange("p (s n) -> p s n", s=2)
        GH, GL = HH, HL

        bank = [PS[:, b, :] for b in range(8)]

        with nc.Block() as block:
            @block.sync
            def _(sp):
                sp.dma_start(CN[:, :], consts).then_inc(ld0, 16)
                sp.dma_start(X[:, :, :], x_t).then_inc(ld0, 16)
                sp.wait_ge(ld0, 32)

            @block.vector
            def _(dve):
                nc.vector.memset(ones[:, :], 1.0).then_inc(s_ones, 1)
                dve.wait_ge(s_ones, 1)

        with nc.Fori(0, DEPTH) as layer:
            with nc.Block() as block:
                @block.sync
                def _(sp):
                    sp.dma_start(PR[:, :], params[layer]).then_inc(s_par, 16)
                    for s in range(SLOTS):
                        sp.dma_start(ring[:, s, :], stream[layer, s]).then_inc(landed[s], 16)
                    with sp.Fori(1, U0 // SLOTS + 1) as r:
                        for s in range(SLOTS):
                            sp.wait_ge(piece_done, r * SLOTS + (s - SLOTS + 1))
                            sp.dma_start(ring[:, s, :], stream[layer, r * SLOTS + s]).then_inc(landed[s], 16)
                    for n in range(SLOTS * (U0 // SLOTS + 1), U0 + SLOTS):
                        sp.wait_ge(piece_done, n - SLOTS + 1)
                        sp.dma_start(ring[:, n % SLOTS, :], stream[layer, n]).then_inc(landed[n % SLOTS], 16)
                    with sp.Fori(0, (PIECES - U0) // SLOTS - 1) as r:
                        for s in range(SLOTS):
                            sp.wait_ge(lo_ready, r * SLOTS + (s + 1))
                            n = U0 + SLOTS + s
                            sp.dma_start(ring[:, n % SLOTS, :], stream[layer, r * SLOTS + n]).then_inc(landed[n % SLOTS], 16)

                @block.gpsimd
                def _(pool):
                    pool.wait_ge(ssq_done, 1)
                    nc.gpsimd.memset(XB[:, :, 0:CONV - 1], 0.0).then_inc(padded, 1)
                    nc.gpsimd.memset(HV[:, :, :, :, :], 0.0).then_inc(padded, 1)
                    pool.wait_ge(roped, 1)
                    for e in range(2):
                        nc.gpsimd.tensor_copy(
                            DUP[:, :, :, e, :],
                            Y[:, :, K_WIN:K_WIN + 384].rearrange("p t (b n) -> p t b n", n=HD)).then_inc(dup_ready, 1)
                    def low(b, slot):
                        nc.gpsimd.tensor_tensor(WL[:, b, :], ring[:, slot, :], WH[:, b, :].bitcast(F32),
                                                ALU.subtract).then_inc(lo_ready, 1)

                    for k in range(SLOTS):
                        pool.wait_ge(hi_ready, k + 1)
                        if k >= 2:
                            pool.wait_ge(piece_done, U0 + k - 1)
                        low(k % 2, (U0 + k) % SLOTS)
                    with pool.Fori(1, 2 * TILES // SLOTS) as r:
                        for s in range(SLOTS):
                            pool.wait_ge(hi_ready, r * SLOTS + (s + 1))
                            pool.wait_ge(piece_done, r * SLOTS + (U0 + s - 1))
                            low(s % 2, (U0 + s) % SLOTS)

                @block.tensor
                def _(pe):
                    def piece(n):
                        pe.wait_ge(landed[n % SLOTS], 16 * (n // SLOTS + 1))
                        return ring[:, n % SLOTS, :]

                    def sum_squares(k):
                        pe.wait_ge(sq_ready, k + 1)
                        for c in range(DC):
                            mm = nc.tensor.matmul(bank[7][:, 0:SEQ], ones[:, :], SQ[:, c, :],
                                                  start=(c == 0), stop=(c == DC - 1))
                        mm.then_inc(ssq_done, 1)

                    def by_column(u, b, rhs):
                        for k in range(2):
                            w = piece(2 * u + k).rearrange("p (c m) -> p c m", c=DC)
                            for c in range(DC):
                                mm = nc.tensor.matmul(bank[b][:, k * SEQ:(k + 1) * SEQ], w[:, c, :],
                                                      rhs[:, c, :], start=(c == 0), stop=(c == DC - 1))
                            mm.then_inc(piece_done, 1)

                    def by_token(u, b):
                        for k in range(2):
                            w = piece(2 * u + k).rearrange("p (c m) -> p c m", c=DC // 2)
                            for c in range(DC // 2):
                                for t in range(TT):
                                    mm = nc.tensor.matmul(bank[b][:, t * 256:(t + 1) * 256],
                                                          H[:, 4 * k + c, t * P:(t + 1) * P], w[:, c, :],
                                                          start=(k == 0 and c == 0 and t == 0),
                                                          stop=(k == 1 and c == DC // 2 - 1), skip_group_check=True)
                            mm.then_inc(piece_done, 1)

                    order = [0, 1, 2, 3, 4, 5, 6, 11, 12, 13, 14, 15, 16, 17]

                    def project(n):
                        j = order.index(n)
                        if j >= 2:
                            pe.wait_ge(evac, j - 1)
                        if n < N_XBC:
                            by_column(n, j % 2, H)
                        else:
                            by_token(n, j % 2)

                    sets = [0]

                    def turn(blocks):
                        k = sets[0]
                        if k >= 2:
                            pe.wait_ge(tr_evac, k - 1)
                        for i, b in enumerate(blocks):
                            mm = nc.tensor.transpose(bank[2 + k % 2][:, i * P:(i + 1) * P], b, ident)
                        mm.then_inc(tr_done, 1)
                        sets[0] += 1

                    def columns(c):
                        return [Y[:, t, c + i * P:c + (i + 1) * P] for i in range(2) for t in range(TT)]

                    scored = [0]

                    def scores(a, b, a_first):
                        k = scored[0]
                        if k >= 2:
                            pe.wait_ge(sc_evac, k - 1)
                        o = bank[4 + k % 2]
                        if a_first:
                            nc.tensor.matmul(o[:, 0:128], a[:, 0:P], b[:, 0:P], start=True, stop=True)
                            mm = nc.tensor.matmul(o[:, 128:384], a[:, P:SEQ], b[:, 0:SEQ], start=True, stop=True)
                        else:
                            nc.tensor.matmul(o[:, 0:256], a[:, 0:P], b[:, 0:SEQ], start=True, stop=True)
                            mm = nc.tensor.matmul(o[:, 256:384], a[:, P:SEQ], b[:, P:SEQ], start=True, stop=True)
                        mm.then_inc(sc_done, 1)
                        scored[0] += 1

                    def half(block, h):
                        return T[(h % 2) * HD:(h % 2) * HD + HD, block, :]

                    def values(weights, v):
                        for h in range(NH):
                            w, vh = weights(h), v(h)
                            nc.tensor.matmul(bank[6][:, h * HD:(h + 1) * HD], w[:, 0:P], vh[0], start=True, stop=True)
                            o = bank[6][:, 256 + h * HD:256 + (h + 1) * HD]
                            nc.tensor.matmul(o, w[:, P:2 * P], vh[0], start=True, stop=False)
                            mm = nc.tensor.matmul(o, w[:, 2 * P:3 * P], vh[1], start=False, stop=True)
                        mm.then_inc(pv_done, 1)

                    def y_values(c, step):
                        return lambda h: [Y[:, t, c + h * step:c + h * step + HD] for t in range(TT)]

                    def turn_group(buf, g):
                        for h in range(NH):
                            pe.wait_ge(exp_done, 8 * g + 2 * h + 2)
                            turn([buf[:, h, i * P:(i + 1) * P] for i in range(3)])

                    sum_squares(0)
                    pe.wait_ge(s_par, 16)
                    pe.wait_ge(h_ready, DC)
                    for n in (0, 1, 2, 3, 4, 5):
                        project(n)
                    pe.wait_ge(dup_ready, 2)
                    turn([DUP[:, t, b, :, :].rearrange("p e n -> p (e n)") for b in (2, 3) for t in range(TT)])
                    turn([DUP[:, t, b, :, :].rearrange("p e n -> p (e n)") for b in (0, 4) for t in range(TT)])
                    project(6)
                    pe.wait_ge(xc_ready, 1)
                    turn([XC[:, b, t * P:(t + 1) * P] for t in range(TT) for b in range(2)])
                    for i, u in enumerate(W1):
                        pe.wait_ge(blocks_ready, i // 2 + 1)
                        for k in range(2):
                            w = piece(2 * u + k).rearrange("p (j m) -> p j m", j=CHUNKS // 2)
                            for j in range(CHUNKS // 2):
                                mm = nc.tensor.matmul(bank[7][:, 16 * i:16 * i + NCMP], w[:, j, :],
                                                      BL[:, i // 2, CHUNKS // 2 * k + j, :],
                                                      start=(k == 0 and j == 0), stop=(k == 1 and j == CHUNKS // 2 - 1))
                            mm.then_inc(piece_done, 1)
                    for g in range(2):
                        scores(XC[:, 2 + g, :], XC[:, 4 + g, :], False)
                    pe.wait_ge(roped, 2)
                    turn(columns(NSA_Q))
                    pe.wait_ge(tr_evac, 4)
                    for h in range(NH):
                        scores(half(TQ_NSA + h // 2, h), half(TK_WIN, h), True)
                    project(11)
                    pe.wait_ge(hid_ready, 4)
                    for b in range(2):
                        nc.tensor.matmul(bank[7][:, 64:96], pr("w2k", b * P, (b + 1) * P), HV[:, 0, b, 0, :],
                                         start=(b == 0), stop=(b == 1))
                    for b in range(2):
                        mm = nc.tensor.matmul(bank[7][:, 96:160], HV[:, 1, b, :, :].rearrange("p h c -> p (h c)"),
                                              pr("w2v", b * HD, (b + 1) * HD), start=(b == 0), stop=(b == 1))
                    mm.then_inc(kcvc_done, 1)
                    for h in range(NH):
                        scores(half(TQ_NSA + h // 2, h), half(TK_SLC, h), True)
                    project(12)
                    turn_group(SC4[0], 0)
                    pe.wait_ge(kc_ready, 1)
                    pe.wait_ge(vb_ready, 1)
                    for h in range(NH):
                        for t in range(TT):
                            at = 256 + (2 * t + h // 2) * CPAD
                            nc.tensor.matmul(bank[7 - h % 2][:, at:at + CPAD], half(TQ_NSA + h // 2, h)[:, t * P:(t + 1) * P],
                                                  KC[(h % 2) * HD:(h % 2) * HD + HD, :], start=True, stop=True)
                    pe.wait_ge(da_ready, 2)
                    dta_t = dta.rearrange("p (t h) -> p t h", t=TT)
                    tri = cn("tri")
                    nc.tensor.matmul(bank[6][:, 0:4], tri[:, 0:P], dta_t[:, 0, :], start=True, stop=True)
                    nc.tensor.matmul(bank[6][:, 4:8], tri[:, P:2 * P], dta_t[:, 0, :], start=True, stop=False)
                    nc.tensor.matmul(bank[6][:, 4:8], tri[:, 2 * P:3 * P], dta_t[:, 1, :], start=False,
                                     stop=True).then_inc(acs_done, 1)

                    def acr(pair):
                        for i in range(2):
                            h = 2 * pair + i
                            nc.tensor.matmul(bank[7][:, i * SEQ:(i + 1) * SEQ], DA[:, 0, h, :], tri[:, 0:SEQ],
                                             start=True, stop=False)
                            mm = nc.tensor.matmul(bank[7][:, i * SEQ + P:(i + 1) * SEQ], DA[:, 1, h, :],
                                                  tri[:, SEQ:SEQ + P], start=False, stop=True)
                        mm.then_inc(acr_done, 1)

                    project(13)
                    pe.wait_ge(tr_evac, 8)
                    pe.wait_ge(b6_free, 3)
                    values(lambda h: PT[0][:, h, :], y_values(V_WIN, 0))
                    acr(0)
                    project(14)
                    turn_group(SC4[1], 1)
                    pe.wait_ge(tr_evac, 12)
                    pe.wait_ge(pv_evac, 1)
                    values(lambda h: PT[1][:, h, :], y_values(V_SLC, 0))
                    pe.wait_ge(seg_ready, 2)
                    acr(1)
                    pe.wait_ge(roped, 3)
                    turn(columns(MOBA_Q))
                    turn(columns(MOBA_K))
                    project(15)
                    pe.wait_ge(tr_evac, 14)
                    for h in range(NH):
                        scores(half(TQ_MOBA + h // 2, h), half(TK_MOBA + h // 2, h), True)
                    pe.wait_ge(cs_exp, 1)
                    turn([CS[:, t, :, :].rearrange("p h c -> p (h c)") for t in range(TT)])
                    project(16)
                    pe.wait_ge(tr_evac, 15)
                    pe.wait_ge(pv_evac, 2)
                    for t in range(TT):
                        mm = nc.tensor.matmul(bank[6][:, t * GW:(t + 1) * GW], CP[:, t, :],
                                              VB[:, :, :].rearrange("p h n -> p (h n)"), start=True, stop=True)
                    mm.then_inc(pv_done, 1)
                    pe.wait_ge(roped, 4)
                    turn(columns(RET_Q))
                    turn(columns(RET_K))
                    pe.wait_ge(ps_ready, 2)
                    pe.wait_ge(pv_evac, 3)
                    values(lambda h: SEG[:, h, :], lambda h: [XDT[:, t, h * HD:(h + 1) * HD] for t in range(TT)])
                    project(17)
                    pe.wait_ge(tr_evac, 17)
                    for h in range(NH):
                        scores(half(TK_RET + h // 2, h), half(TQ_RET + h // 2, h), False)
                    turn_group(SC4[0], 2)
                    pe.wait_ge(tr_evac, 21)
                    pe.wait_ge(pv_evac, 4)
                    values(lambda h: PT[0][:, h, :], y_values(MOBA_V, HD))
                    pe.wait_ge(sc_evac, 18)
                    pe.wait_ge(pv_evac, 5)
                    values(lambda h: SC4[1][:, h, :], y_values(RET_V, HD))
                    for c, ready, n in ((6, m_ready, 1), (2, pv_evac, 5), (4, m_ready, 2), (0, m_ready, 3)):
                        pe.wait_ge(ready, n)
                        turn([M[:, t, (c + i) * P:(c + i + 1) * P] for i in range(2) for t in range(TT)])
                    pe.wait_ge(tr_evac, 25)
                    pe.wait_ge(evac, len(order))
                    for k in range(N_OUT):
                        if k >= 2:
                            pe.wait_ge(x_added, k - 1)
                        by_column(OUT0 + k, k % 2, MT)

                    sum_squares(1)
                    pe.wait_ge(h_ready, 2 * DC)
                    pe.wait_ge(x_added, N_OUT)
                    for k in range(N_WQ):
                        if k >= 2:
                            pe.wait_ge(qt_evac, k - 1)
                        by_column(WQ0 + k, k % 2, H)
                    pe.wait_ge(qt_evac, N_WQ)
                    sets_k = 0
                    for kp in range(N_KEYS):
                        w = piece(KEY0 + kp).rearrange("p (b n) -> p b n", b=8)
                        for t in range(TT):
                            for quad in range(2):
                                if sets_k >= 4:
                                    pe.wait_ge(key_evac, sets_k - 3)
                                for i in range(4):
                                    b = quad * 4 + i
                                    mm = nc.tensor.matmul(bank[sets_k % 4][:, i * P:(i + 1) * P],
                                                          QT[:, 8 * kp + b, t * P:(t + 1) * P], w[:, b, :],
                                                          start=True, stop=True)
                                mm.then_inc(piece_done if t == TT - 1 and quad == 1 else key_done, 1)
                                sets_k += 1

                    pe.wait_ge(hl_ready, DC)

                    def parts(s):
                        return [W[:, s % 2, :].rearrange("p (c m) -> p c m", c=DC) for W in (WH, WL)]

                    def experts_in(s, ready):
                        o = bank[4 + s // 2][:, s % 2 * SEQ:(s % 2 + 1) * SEQ]
                        wh, wl = parts(s)
                        pe.wait_ge(hi_ready, ready)
                        for c in range(DC):
                            nc.tensor.matmul(o, wh[:, c, :], HH[:, c, :], start=(c == 0), stop=False)
                            mm = nc.tensor.matmul(o, wh[:, c, :], HL[:, c, :], start=False, stop=False)
                        mm.then_inc(hi_used, 1)
                        pe.wait_ge(lo_ready, ready)
                        for c in range(DC):
                            mm = nc.tensor.matmul(o, wl[:, c, :], HH[:, c, :], start=False, stop=(c == DC - 1))
                        mm.then_inc(piece_done, 1)

                    def place(g):
                        for i in range(4):
                            o = bank[6 + g][:, i * HK:(i + 1) * HK]
                            for k in range(3):
                                mm = nc.tensor.matmul(o, O2[:, 4 * g + i, :], O1[:, 4 * g + i, k, :],
                                                      start=(k == 0), stop=(k == 2))
                        mm.then_inc(w_done, 1)

                    for s in range(SLOTS):
                        experts_in(s, s + 1)

                    def rounds_in(lo, hi):
                        with pe.Fori(lo, hi) as r:
                            for s in range(SLOTS):
                                if s % 2 == 0:
                                    pe.wait_ge(gelu_done, r * 2 + (s // 2 - 1))
                                experts_in(s, r * SLOTS + (s + 1))

                    rounds_in(1, TURN_ROUND)
                    pe.wait_ge(key_evac, 8)
                    pe.wait_ge(rt_ready, 3 * TT)
                    for k in range(3):
                        for t in range(TT):
                            mm = nc.tensor.transpose(bank[k][:, t * P:(t + 1) * P], RT[:, t, k, :], ident)
                        mm.then_inc(rt_tr, 1)
                    rounds_in(TURN_ROUND, HK // SLOTS)
                    for s in range(SLOTS):
                        if s % 2 == 0:
                            pe.wait_ge(gelu_done, HK // 2 + (s // 2 - 1))
                        pe.wait_ge(o_ready, s + 1)
                        if s >= 2:
                            pe.wait_ge(w_used, s - 1)
                        place(s % 2)
                        experts_in(s, HK + s + 1)
                    with pe.Fori(1, HK // SLOTS) as r:
                        for s in range(SLOTS):
                            if s % 2 == 0:
                                pe.wait_ge(gelu_done, r * 2 + (HK // 2 + s // 2 - 1))
                            pe.wait_ge(o_ready, r * SLOTS + (s + 1))
                            pe.wait_ge(w_used, r * SLOTS + (s - 1))
                            place(s % 2)
                            experts_in(s, r * SLOTS + (HK + s + 1))

                    def experts_out(s, ready, first, last):
                        wh, wl = parts(s)
                        gh, gl = GH[:, s, :], GL[:, s, :]
                        pe.wait_ge(gl_ready, ready)
                        pe.wait_ge(hi_ready, ready + TILES)
                        for c in range(DC):
                            o = bank[c // 2][:, (c % 2) * SEQ:(c % 2 + 1) * SEQ]
                            nc.tensor.matmul(o, wh[:, c, :], gh, start=(first and c % 2 == 0), stop=False,
                                             skip_group_check=True)
                            mm = nc.tensor.matmul(o, wh[:, c, :], gl, start=False, stop=False, skip_group_check=True)
                        mm.then_inc(hi_used, 1)
                        pe.wait_ge(lo_ready, ready + TILES)
                        for c in range(DC):
                            o = bank[c // 2][:, (c % 2) * SEQ:(c % 2 + 1) * SEQ]
                            mm = nc.tensor.matmul(o, wl[:, c, :], gh, start=False, stop=last, skip_group_check=True)
                        mm.then_inc(piece_done, 1)

                    pe.wait_ge(rt_free, 3)
                    for s in range(SLOTS):
                        pe.wait_ge(o_ready, HK + s + 1)
                        pe.wait_ge(w_used, HK + s - 1)
                        place(s % 2)
                        experts_out(s, s + 1, s == 0, False)
                    with pe.Fori(1, HK // SLOTS) as r:
                        for s in range(SLOTS):
                            pe.wait_ge(o_ready, r * SLOTS + (HK + s + 1))
                            pe.wait_ge(w_used, r * SLOTS + (HK + s - 1))
                            place(s % 2)
                            experts_out(s, r * SLOTS + (s + 1), False, False)
                    with pe.Fori(HK // SLOTS, TILES // SLOTS - 1) as r:
                        for s in range(SLOTS):
                            experts_out(s, r * SLOTS + (s + 1), False, False)
                    for s in range(SLOTS):
                        experts_out(s, TILES - SLOTS + s + 1, False, s == SLOTS - 1)

                @block.scalar
                def _(act):
                    def rough_root(src, dst, ready, done, n, steps):
                        act.wait_ge(ready, n)
                        nc.scalar.activation(dst, src, ACT.Ln).then_inc(act_step, 1)
                        act.wait_ge(act_step, steps)
                        nc.scalar.activation(dst, dst, ACT.Exp, scale=-0.5).then_inc(done, 1)

                    order = [0, 1, 2, 3, 4, 5, 6, 11, 12, 13, 14, 15, 16, 17]

                    def take(n):
                        act.wait_ge(piece_done, 2 * n + 2)
                        b = order.index(n) % 2
                        if n < N_XBC:
                            dst = XB[:, 2 * n:2 * n + 2, CONV - 1:]
                        else:
                            c = 256 * Y_BLOCK[n]
                            dst = Y[:, :, c:c + 256]
                        nc.scalar.copy(dst, bank[b].rearrange("p (k m) -> p k m", k=2)).then_inc(evac, 1)

                    turned = [0]

                    def taken(dst, width=512):
                        k = turned[0]
                        act.wait_ge(tr_done, k + 1)
                        src = bank[2 + k % 2][:, 0:width]
                        turned[0] += 1
                        return nc.scalar.copy(dst, src if len(dst.shape) == 2 else
                                              src.rearrange("p (k m) -> p k m", k=dst.shape[1]))

                    def exps(g, buf):
                        act.wait_ge(negm_ready, g + 1)
                        for h in range(NH):
                            for t in range(TT):
                                s = buf[:, h, 0:P] if t == 0 else buf[:, h, P:3 * P]
                                k = t * NH + h
                                nc.scalar.activation(s, s, ACT.Exp, bias=negm[g][:, k:k + 1], scale=HD ** -0.5,
                                                     accum_out=rsum[g][:, k:k + 1]).then_inc(exp_done, 1)

                    def probabilities(buf):
                        for h in range(NH):
                            taken(buf[:, h, :], 384).then_inc(tr_evac, 1)

                    nc.scalar.activation(SQ[:, :, :], X[:, :, :], ACT.Square).then_inc(sq_ready, 1)
                    rough_root(var, rs, var_ready, rs_ready, 1, 1)
                    for n in (0, 1, 2, 3, 4):
                        take(n)
                    act.wait_ge(conv_ready, 6)
                    nc.scalar.activation(CE[:, :, :], XC[:, :, :], ACT.Exp, scale=-1.0).then_inc(conv_exp, 1)
                    take(5)
                    act.wait_ge(tr_done, 1)
                    for s in range(2):
                        nc.scalar.copy(K2[0:HD, s, :], bank[2][0:HD, s * SEQ:(s + 1) * SEQ])
                        cp = nc.scalar.copy(K2[HD:P, s, 0:SEQ - 1], bank[2][HD:P, s * SEQ + 1:(s + 1) * SEQ])
                    cp.then_inc(tr_evac, 1)
                    turned[0] += 1
                    taken(T[:, TK_WIN:TK_WIN + 2, :]).then_inc(tr_evac, 1)
                    take(6)
                    act.wait_ge(dt_abs, 1)
                    nc.scalar.activation(dte, dte, ACT.Exp).then_inc(dt_exp, 1)
                    act.wait_ge(s_par, 16)
                    nc.scalar.activation(avec, pr("a_log"), ACT.Exp).then_inc(dt_exp, 1)
                    act.wait_ge(evac, 5)
                    nc.scalar.activation(gate.rearrange("p (t k) -> p t k", t=TT), Y[:, :, GATE:GATE + 12],
                                         ACT.Exp, scale=-1.0).then_inc(z_exp, 1)
                    act.wait_ge(dt_one, 1)
                    nc.scalar.activation(dtl, dtu, ACT.Ln).then_inc(dt_ln, 1)
                    taken(XS[:, :, :]).then_inc(tr_evac, 1)
                    act.wait_ge(padded, 2)
                    act.wait_ge(piece_done, 2 * W1[-1] + 2)
                    for i in range(len(W1)):
                        s, b = i // 2, i % 2
                        heads = 1 if s == 0 else NH
                        nc.scalar.activation(HV[:, s, b, 0:heads, 0:NCMP],
                                             bc(bank[7][:, 16 * i:16 * i + NCMP], 1, heads),
                                             ACT.Gelu).then_inc(hid_ready, 1)
                    taken(T[:, TQ_NSA:TQ_NSA + 2, :]).then_inc(tr_evac, 1)
                    exps(0, SC4[0])
                    take(11)
                    exps(1, SC4[1])
                    take(12)
                    probabilities(PT[0])
                    act.wait_ge(cs_ready, 1)
                    nc.scalar.activation(CS[:, :, :, :], CS[:, :, :, :], ACT.Exp, scale=HD ** -0.5).then_inc(cs_exp, 1)
                    take(13)
                    take(14)
                    probabilities(PT[1])
                    taken(T[:, TQ_MOBA:TQ_MOBA + 2, :]).then_inc(tr_evac, 1)
                    taken(T[:, TK_MOBA:TK_MOBA + 2, :]).then_inc(tr_evac, 1)
                    take(15)
                    act.wait_ge(seg_ready, 4)
                    nc.scalar.activation(SEG[:, :, :], SEG[:, :, :], ACT.Exp).then_inc(seg_exp, 1)
                    taken(CP[:, :, :], 256).then_inc(tr_evac, 1)
                    take(16)
                    act.wait_ge(evac, 13)
                    nc.scalar.activation(TB[:, 0:512].rearrange("p (t n) -> p t n", t=TT),
                                         Y[:, :, RET_G:RET_G + GW], ACT.Exp, scale=-1.0).then_inc(z_exp, 1)
                    taken(T[:, TQ_RET:TQ_RET + 2, :]).then_inc(tr_evac, 1)
                    taken(T[:, TK_RET:TK_RET + 2, :]).then_inc(tr_evac, 1)
                    take(17)
                    act.wait_ge(evac, len(order))
                    nc.scalar.activation(TB[:, 512:1024].rearrange("p (t n) -> p t n", t=TT),
                                         Y[:, :, SSM_Z:SSM_Z + GW], ACT.Exp, scale=-1.0).then_inc(z_exp, 1)
                    exps(2, SC4[0])
                    probabilities(PT[0])
                    rough_root(gvar[:, 0:4], grs[:, 0:4], g_var, g_rs, 1, 2)
                    for c in (6, 2, 4):
                        if c == 4:
                            for i in range(2):
                                act.wait_ge(tr_done, 24)
                                cp = nc.scalar.mul(MT[:, c + i, :], bank[2 + 23 % 2][:, i * SEQ:(i + 1) * SEQ],
                                                   pr("ssm_norm", i, i + 1))
                            cp.then_inc(tr_evac, 1)
                            turned[0] += 1
                        else:
                            taken(MT[:, c:c + 2, :]).then_inc(tr_evac, 1)
                    rough_root(gvar[:, 0:8], grs[:, 0:8], g_var, g_rs, 2, 3)
                    act.wait_ge(tr_done, 25)
                    for i in range(2):
                        cp = nc.scalar.mul(MT[:, i, :], bank[2 + 24 % 2][:, i * SEQ:(i + 1) * SEQ],
                                           pr("ret_norm", i, i + 1))
                    cp.then_inc(tr_evac, 1)

                    act.wait_ge(x_added, N_OUT)
                    nc.scalar.activation(SQ[:, :, :], X[:, :, :], ACT.Square).then_inc(sq_ready, 1)
                    rough_root(var, rs, var_ready, rs_ready, 2, 4)
                    for c in range(DC):
                        act.wait_ge(h_ready, DC + c + 1)
                        nc.scalar.copy(HH[:, c, :], H[:, c, :]).then_inc(hh_ready, 1)
                    for k in range(N_WQ):
                        act.wait_ge(piece_done, 2 * (WQ0 + k) + 2)
                        nc.scalar.copy(QT[:, 2 * k:2 * k + 2, :],
                                       bank[k % 2].rearrange("p (k m) -> p k m", k=2)).then_inc(qt_evac, 1)
                    for k in range(8):
                        kp, t, quad = k // 4, k // 2 % 2, k % 2
                        if k % 4 == 3:
                            act.wait_ge(piece_done, KEY0 + kp + 1)
                        else:
                            act.wait_ge(key_done, 3 * kp + k % 4 + 1)
                        nc.scalar.copy(S[:, t, 8 * kp + 4 * quad:8 * kp + 4 * quad + 4, :],
                                       bank[k % 4].rearrange("p (b n) -> p b n", b=4)).then_inc(key_evac, 1)

                    def high(b, slot):
                        nc.scalar.copy(WH[:, b, :], ring[:, slot, :]).then_inc(hi_ready, 1)

                    def gelu(dst, b):
                        nc.scalar.activation(dst, bank[4 + b].rearrange("p (e n) -> p e n", e=2),
                                             ACT.Gelu).then_inc(gelu_done, 1)

                    def arrival(n):
                        return landed[n % SLOTS], 16 * (n // SLOTS + 1)

                    def high_k(k):
                        act.wait_ge(*arrival(U0 + k))
                        if k >= 2:
                            act.wait_ge(hi_used, k - 1)
                            act.wait_ge(lo_ready, k - 1)
                        high(k % 2, (U0 + k) % SLOTS)

                    def high_r(r, s, k0=0):
                        q, n = arrival(U0 + k0 + s)
                        act.wait_ge(q, r * 16 + n)
                        act.wait_ge(hi_used, r * SLOTS + (k0 + s - 1))
                        act.wait_ge(lo_ready, r * SLOTS + (k0 + s - 1))
                        high(s % 2, (U0 + s) % SLOTS)

                    for k in (0, 1, 2, 3):
                        high_k(k)
                    act.wait_ge(piece_done, U0 + 2)
                    gelu(G[:, 0:2, :], 0)

                    def rounds_gelu(lo, hi):
                        with act.Fori(lo, hi) as r:
                            for s in range(SLOTS):
                                high_r(r, s)
                                if s == 1:
                                    act.wait_ge(piece_done, r * SLOTS + U0)
                                    gelu(G[:, bass.ds(r * SLOTS - 2, 2), :], 1)
                                if s == 3:
                                    act.wait_ge(piece_done, r * SLOTS + (U0 + 2))
                                    gelu(G[:, bass.ds(r * SLOTS, 2), :], 0)

                    rounds_gelu(1, EXP_ROUND)
                    act.wait_ge(rt_sub, TT)
                    nc.scalar.activation(VC[:, :, :, :], VC[:, :, :, :], ACT.Exp).then_inc(rt_exp, 1)
                    rounds_gelu(EXP_ROUND, HK // SLOTS)
                    act.wait_ge(rt_free, 3)
                    rounds_gelu(HK // SLOTS, TILES // SLOTS)

                    def high_g(s, tile):
                        nc.scalar.copy(GH[:, s, :], G[:, tile, :]).then_inc(gh_ready, 1)

                    high_k(TILES)
                    act.wait_ge(w_used, HK)
                    act.wait_ge(piece_done, V0)
                    high_g(0, 0)
                    gelu(G[:, TILES - 2:TILES, :], 1)
                    high_g(1, 1)
                    for s in range(1, SLOTS):
                        high_k(TILES + s)
                        high_g((s + 1) % SLOTS, s + 1)

                    def rounds_out(lo, hi, last):
                        with act.Fori(lo, hi) as r:
                            for s in range(last):
                                high_r(r, s, TILES)
                                high_g((s + 1) % SLOTS, r * SLOTS + (s + 1))

                    rounds_out(1, HK // SLOTS - 1, SLOTS)
                    for s in range(SLOTS):
                        high_k(TILES + HK - SLOTS + s)
                        if s == SLOTS - 1:
                            act.wait_ge(w_used, 2 * HK)
                        high_g((s + 1) % SLOTS, HK - SLOTS + s + 1)
                    rounds_out(HK // SLOTS, TILES // SLOTS - 1, SLOTS)
                    for s in range(SLOTS):
                        high_k(2 * TILES - SLOTS + s)
                        if s < SLOTS - 1:
                            high_g(s + 1, TILES - SLOTS + s + 1)

                @block.vector
                def _(dve):
                    n = [0]

                    def step(ins):
                        n[0] += 1
                        ins.then_inc(dve_step, 1)
                        dve.wait_ge(dve_step, n[0])

                    V = nc.vector

                    def newton(v, r, t):
                        step(V.tensor_tensor(t, r, r, ALU.mult))
                        step(V.tensor_tensor(t, t, v, ALU.mult))
                        step(V.tensor_scalar(t, t, -0.5, 1.5, ALU.mult, ALU.add))
                        step(V.tensor_tensor(r, r, t, ALU.mult))

                    def norm(k, weight):
                        dve.wait_ge(ssq_done, k + 1)
                        V.tensor_scalar(var, bank[7][:, 0:SEQ], 1.0 / D, EPS, ALU.mult, ALU.add).then_inc(var_ready, 1)
                        dve.wait_ge(var_ready, k + 1)
                        dve.wait_ge(rs_ready, k + 1)
                        newton(var, rs, nt[:, :])
                        for c in range(DC):
                            V.scalar_tensor_tensor(out=H[:, c, :], in0=X[:, c, :], scalar=pr(weight, c, c + 1),
                                                   in1=rs, op0=ALU.mult, op1=ALU.mult).then_inc(h_ready, 1)

                    def rope(y, cos, sin, half, heads):
                        w = TT * heads * 2 * half
                        a = TA[:, 0:w].rearrange("p (t h d) -> p t h d", t=TT, h=heads)
                        b = TB[:, 1024:1024 + w].rearrange("p (t h d) -> p t h d", t=TT, h=heads)
                        c = bc(cos.rearrange("p (t d) -> p t d", t=TT), 2, heads)
                        s = bc(sin.rearrange("p (t d) -> p t d", t=TT), 2, heads)
                        V.tensor_tensor(a, y, c, ALU.mult)
                        V.tensor_tensor(b[:, :, :, 0:half], y[:, :, :, half:], s[:, :, :, 0:half], ALU.mult)
                        step(V.tensor_tensor(b[:, :, :, half:], y[:, :, :, 0:half], s[:, :, :, half:], ALU.mult))
                        return V.tensor_tensor(y, a, b, ALU.add)

                    def silu_factor(e):
                        step(V.tensor_scalar(e, e, 1.0, None, ALU.add))
                        step(V.reciprocal(e, e))

                    def attention_scores(g, buf, first):
                        for h in range(NH):
                            dve.wait_ge(sc_done, first + h + 1)
                            V.tensor_tensor(buf[:, h, :], bank[4 + h % 2][:, 0:384], cn("negq"), ALU.add).then_inc(sc_evac, 1)
                        dve.wait_ge(sc_evac, first + NH)
                        V.tensor_reduce(mx[:, 0:4], buf[:, :, 0:P], AX.X, ALU.max)
                        step(V.tensor_reduce(mx[:, 4:8], buf[:, :, P:3 * P], AX.X, ALU.max))
                        V.tensor_scalar(negm[g], mx, -(HD ** -0.5), None, ALU.mult).then_inc(negm_ready, 1)

                    def heads(flat):
                        return flat.rearrange("p (t h d) -> p t h d", t=TT, h=NH)

                    def columns(f8):
                        return bc(f8.rearrange("p (t h) -> p t h", t=TT), 3, HD)

                    def m_part(c):
                        return M[:, :, c:c + GW].rearrange("p t (h d) -> p t h d", h=NH)

                    def nsa_factor(g, kind):
                        dve.wait_ge(exp_done, 8 * g + 8)
                        step(V.reciprocal(rinv[g], rsum[g]))
                        if kind is not None:
                            step(V.tensor_tensor(rinv[g].rearrange("p (t h) -> p t h", t=TT),
                                                 rinv[g].rearrange("p (t h) -> p t h", t=TT),
                                                 gate.rearrange("p (t k h) -> p t k h", t=TT, k=3)[:, :, kind, :],
                                                 ALU.mult))

                    dve.wait_ge(s_par, 16)
                    norm(0, "norm_mix")

                    dve.wait_ge(padded, 1)
                    for b in range(6):
                        dve.wait_ge(evac, b // 2 + 1)
                        w = pr("conv_w").rearrange("p (b j) -> p b j", b=6)
                        step(V.tensor_scalar(XC[:, b, :], XB[:, b, 0:SEQ], w[:, b, 0:1], pr("conv_b", b, b + 1),
                                             ALU.mult, ALU.add))
                        for j in range(1, CONV):
                            ins = V.scalar_tensor_tensor(out=XC[:, b, :], in0=XB[:, b, j:j + SEQ], scalar=w[:, b, j:j + 1],
                                                         in1=XC[:, b, :], op0=ALU.mult, op1=ALU.add)
                            if j < CONV - 1:
                                step(ins)
                            else:
                                ins.then_inc(conv_ready, 1)

                    dve.wait_ge(evac, 5)
                    rope(Y[:, :, K_WIN:K_WIN + 384].rearrange("p t (b n) -> p t b n", n=P)[:, :, :, 0:ROPE16],
                         cn("c16"), cn("s16"), ROPE16 // 2, 3).then_inc(roped, 1)
                    x8 = dtx.rearrange("p (t h) -> p t h", t=TT)
                    step(V.tensor_tensor(x8, Y[:, :, DT:DT + NH], bc(pr("dt_bias"), 1, TT), ALU.add))
                    step(V.tensor_scalar(dtz, dtx, -1.0, None, ALU.mult))
                    V.tensor_tensor(dte, dtx, dtz, ALU.min).then_inc(dt_abs, 1)
                    dve.wait_ge(conv_exp, 1)
                    step(V.tensor_scalar(CE[:, :, :], CE[:, :, :], 1.0, None, ALU.add))
                    step(V.reciprocal(CE[:, :, :], CE[:, :, :]))
                    V.tensor_tensor(XC[:, :, :], XC[:, :, :], CE[:, :, :], ALU.mult).then_inc(xc_ready, 1)
                    dve.wait_ge(evac, 6)
                    rope(Y[:, :, NSA_Q:NSA_Q + GW].rearrange("p t (b n) -> p t b n", n=HD)[:, :, :, 0:ROPE16],
                         cn("c16"), cn("s16"), ROPE16 // 2, NH).then_inc(roped, 1)
                    dve.wait_ge(tr_evac, 1)
                    for s, pe_name in enumerate(("pe_k", "pe_v")):
                        k2 = K2[:, s, :].rearrange("p (c j e) -> p e j c", e=2, j=CMP_STRIDE // 2)
                        for hi in range(2):
                            src = k2[:, 0, :, hi:hi + NCMP]
                            ins = V.tensor_tensor(BL[:, s, 8 * hi:8 * hi + 8, :], src,
                                                  bc(pr(pe_name, 8 * hi, 8 * hi + 8), 2, NCMP), ALU.add)
                            if hi == 1:
                                ins.then_inc(blocks_ready, 1)
                    dve.wait_ge(dt_exp, 1)
                    V.tensor_scalar(dtu, dte, 1.0, None, ALU.add).then_inc(dt_one, 1)
                    dve.wait_ge(dt_one, 1)
                    step(V.tensor_scalar(dtd, dtu, -1.0, None, ALU.add))
                    step(V.tensor_scalar(dtz, dtd, 0.0, None, ALU.is_equal))
                    step(V.tensor_tensor(dtd, dtd, dtz, ALU.add))
                    step(V.reciprocal(dtd, dtd))
                    dve.wait_ge(dt_ln, 1)
                    step(V.tensor_tensor(dtl, dtl, dtz, ALU.add))
                    step(V.tensor_tensor(dtl, dtl, dtd, ALU.mult))
                    step(V.tensor_tensor(dtl, dtl, dte, ALU.mult))
                    step(V.tensor_scalar(dtx, dtx, 0.0, None, ALU.max))
                    step(V.tensor_tensor(dtx, dtx, dtl, ALU.add))
                    dve.wait_ge(dt_exp, 2)
                    step(V.tensor_scalar(avec, avec, -1.0, None, ALU.mult))
                    V.tensor_tensor(dta.rearrange("p (t h) -> p t h", t=TT), x8, bc(avec, 1, TT), ALU.mult).then_inc(da_ready, 1)
                    dve.wait_ge(da_ready, 1)
                    V.tensor_copy(DA[:, :, :, :], bc(dta.rearrange("p (t h) -> p t h", t=TT), 3, P)).then_inc(da_ready, 1)
                    dve.wait_ge(z_exp, 1)
                    silu_factor(gate)
                    for g in range(2):
                        dve.wait_ge(sc_done, g + 1)
                        V.tensor_copy(GS[:, g, :], bank[4 + g][:, 0:384]).then_inc(sc_evac, 1)
                    attention_scores(0, SC4[0], 2)
                    attention_scores(1, SC4[1], 6)
                    dve.wait_ge(kcvc_done, 1)
                    V.tensor_copy(KC, bank[7][:, 64:96]).then_inc(kc_ready, 1)
                    V.tensor_tensor(VB[:, :, :], bc(bank[7][:, 96:160], 1, NH), bc(cn("blkd"), 2, HD),
                                    ALU.mult).then_inc(vb_ready, 1)
                    dve.wait_ge(acs_done, 1)
                    cs_e = CS[:, :, :, :].rearrange("p t (i e) c -> p e t i c", e=2)
                    for e in range(2):
                        V.tensor_tensor(cs_e[:, e], bank[7 - e][:, 256:384].rearrange("p (t i c) -> p t i c", t=TT, i=2),
                                        bc(cn("cmpneg").rearrange("p (t c) -> p t c", t=TT), 2, 2), ALU.add).then_inc(b6_free, 1)
                    dve.wait_ge(b6_free, 2)
                    V.tensor_copy(acs, bank[6][:, 0:8]).then_inc(b6_free, 1)
                    cs8 = CS[:, :, :, :].rearrange("p t h c -> p (t h) c")
                    step(V.tensor_reduce(cmx, cs8, AX.X, ALU.max))
                    V.tensor_tensor(cs8, cs8, bc(cmx, 2, CPAD), ALU.subtract).then_inc(cs_ready, 1)
                    nsa_factor(0, 2)
                    dve.wait_ge(pv_done, 1)
                    V.tensor_tensor(m_part(768), heads(bank[6]), columns(rinv[0]), ALU.mult).then_inc(pv_evac, 1)

                    def decays(pair):
                        dve.wait_ge(acr_done, pair + 1)
                        for i in range(2):
                            h = 2 * pair + i
                            V.scalar_tensor_tensor(out=SEG[:, h, 0:256], in0=bank[7][:, i * SEQ:(i + 1) * SEQ],
                                                   scalar=acs[:, h:h + 1], in1=cn("negk", 0, 256),
                                                   op0=ALU.subtract, op1=ALU.add)
                            V.scalar_tensor_tensor(out=SEG[:, h, 256:384], in0=bank[7][:, i * SEQ + P:(i + 1) * SEQ],
                                                   scalar=acs[:, 4 + h:5 + h], in1=cn("negk", 256, 384),
                                                   op0=ALU.subtract, op1=ALU.add).then_inc(seg_ready, 1)

                    dve.wait_ge(b6_free, 3)
                    decays(0)
                    nsa_factor(1, 1)
                    dve.wait_ge(pv_done, 2)
                    V.tensor_tensor(heads(TA[:, 0:512]), heads(bank[6]), columns(rinv[1]), ALU.mult).then_inc(pv_evac, 1)
                    dve.wait_ge(pv_evac, 2)
                    step(V.tensor_tensor(m_part(768), m_part(768), heads(TA[:, 0:512]), ALU.add))
                    dve.wait_ge(evac, 8)
                    rope(Y[:, :, MOBA_Q:MOBA_Q + 2 * GW].rearrange("p t (b n) -> p t b n", n=HD)[:, :, :, 0:ROPE16],
                         cn("c16"), cn("s16"), ROPE16 // 2, 2 * NH).then_inc(roped, 1)
                    decays(1)
                    dve.wait_ge(cs_exp, 1)
                    step(V.tensor_reduce(csum, cs8, AX.X, ALU.add))
                    step(V.reciprocal(cinv, csum))
                    c8 = cinv.rearrange("p (t h) -> p t h", t=TT)
                    step(V.tensor_tensor(c8, c8, bc(cn("any"), 2, NH), ALU.mult))
                    step(V.tensor_tensor(c8, c8, gate.rearrange("p (t k h) -> p t k h", t=TT, k=3)[:, :, 0, :], ALU.mult))
                    dve.wait_ge(evac, 11)
                    dve.wait_ge(roped, 3)
                    qk = Y[:, :, RET_Q:RET_Q + 2 * GW].rearrange("p t (b n) -> p t b n", n=HD)
                    step(rope(qk, cn("cr"), cn("sr"), HD // 2, 2 * NH))
                    V.tensor_tensor(qk, qk, bc(cn("gamma").rearrange("p (t b) -> p t b", t=TT), 3, HD),
                                    ALU.mult).then_inc(roped, 1)
                    attention_scores(2, SC4[0], 10)
                    dve.wait_ge(tr_evac, 3)
                    V.tensor_tensor(heads(XDT[:, :, :].rearrange("p t n -> p (t n)")),
                                    heads(XS[:, :, :].rearrange("p t n -> p (t n)")), columns(dtx), ALU.mult).then_inc(ps_ready, 1)
                    dve.wait_ge(seg_exp, 1)
                    V.tensor_tensor(SEG[:, :, :].rearrange("p (g h) n -> p g h n", g=2),
                                    SEG[:, :, :].rearrange("p (g h) n -> p g h n", g=2), bc(GS[:, :, :], 2, 2),
                                    ALU.mult).then_inc(ps_ready, 1)
                    dve.wait_ge(pv_done, 3)
                    V.tensor_tensor(heads(TA[:, 0:512]), heads(bank[6]), columns(cinv), ALU.mult).then_inc(pv_evac, 1)
                    dve.wait_ge(pv_evac, 3)
                    V.tensor_tensor(m_part(768), m_part(768), heads(TA[:, 0:512]), ALU.add).then_inc(m_ready, 1)
                    for h in range(NH):
                        dve.wait_ge(sc_done, 15 + h)
                        V.tensor_tensor(SC4[1][:, h, :], bank[4 + h % 2][:, 0:384], cn("tri"),
                                        ALU.mult).then_inc(sc_evac, 1)
                    ya = TA[:, 0:512]
                    yb = TA[:, 512:1024]
                    step(V.tensor_tensor(heads(yb), heads(XS[:, :, :].rearrange("p t n -> p (t n)")),
                                         bc(bc(pr("ssm_d"), 2, HD), 1, TT), ALU.mult))
                    dve.wait_ge(pv_done, 4)
                    V.tensor_tensor(ya, bank[6], yb, ALU.add).then_inc(pv_evac, 1)
                    dve.wait_ge(z_exp, 3)
                    silu_factor(TB[:, 0:1024])
                    dve.wait_ge(pv_evac, 4)
                    step(V.tensor_tensor(ya, ya, TB[:, 512:1024], ALU.mult))
                    yt = ya.rearrange("p (t n) -> p t n", t=TT)
                    step(V.tensor_tensor(yt, yt, Y[:, :, SSM_Z:SSM_Z + GW], ALU.mult))
                    step(V.tensor_tensor(yb, ya, ya, ALU.mult))
                    step(V.tensor_reduce(gvar[:, 0:4], yb.rearrange("p (k n) -> p k n", n=P), AX.X, ALU.add))
                    V.tensor_scalar(gvar[:, 0:4], gvar[:, 0:4], 1.0 / P, EPS, ALU.mult, ALU.add).then_inc(g_var, 1)
                    nsa_factor(2, None)
                    dve.wait_ge(pv_done, 5)
                    V.tensor_tensor(m_part(256), heads(bank[6]), columns(rinv[2]), ALU.mult).then_inc(pv_evac, 1)
                    dve.wait_ge(pv_evac, 5)
                    dve.wait_ge(g_rs, 1)
                    newton(gvar[:, 0:4], grs[:, 0:4], gnt[:, 0:4])
                    V.tensor_tensor(M[:, :, 512:768].rearrange("p t (g n) -> p t g n", g=2),
                                    ya.rearrange("p (t g n) -> p t g n", t=TT, g=2),
                                    bc(grs[:, 0:4].rearrange("p (t g) -> p t g", t=TT), 3, P), ALU.mult).then_inc(m_ready, 1)
                    dve.wait_ge(m_ready, 2)
                    dve.wait_ge(pv_done, 6)
                    V.tensor_copy(ya, bank[6]).then_inc(pv_evac, 1)
                    dve.wait_ge(pv_evac, 6)
                    step(V.tensor_tensor(yb, ya, ya, ALU.mult))
                    step(V.tensor_reduce(gvar, yb.rearrange("p (k n) -> p k n", n=HD), AX.X, ALU.add))
                    V.tensor_scalar(gvar, gvar, 1.0 / HD, EPS, ALU.mult, ALU.add).then_inc(g_var, 1)
                    step(V.tensor_tensor(ya, ya, TB[:, 0:512], ALU.mult))
                    step(V.tensor_tensor(yt, yt, Y[:, :, RET_G:RET_G + GW], ALU.mult))
                    dve.wait_ge(g_rs, 2)
                    newton(gvar, grs, gnt)
                    V.tensor_tensor(m_part(0), heads(ya), columns(grs), ALU.mult).then_inc(m_ready, 1)
                    for k in range(N_OUT):
                        dve.wait_ge(piece_done, 2 * (OUT0 + k) + 2)
                        V.tensor_tensor(X[:, 2 * k:2 * k + 2, :], X[:, 2 * k:2 * k + 2, :],
                                        bank[k % 2].rearrange("p (k m) -> p k m", k=2), ALU.add).then_inc(x_added, 1)

                    dve.wait_ge(x_added, N_OUT)
                    norm(1, "norm_ffn")
                    for c in range(DC):
                        dve.wait_ge(hh_ready, c + 1)
                        V.tensor_tensor(HL[:, c, :], H[:, c, :], HH[:, c, :].bitcast(F32),
                                        ALU.subtract).then_inc(hl_ready, 1)

                    def top16(rows, vals, idxs):
                        for r, v in zip(rows, vals):
                            ins = V.max(v[:, 0:8], r)
                        step(ins)
                        for r, v, i in zip(rows, vals, idxs):
                            V.max_index(i[:, 0:8], v[:, 0:8], r)
                            ins = V.match_replace(r, v[:, 0:8], r, -3e38)
                        step(ins)
                        for r, v in zip(rows, vals):
                            ins = V.max(v[:, 8:16], r)
                        step(ins)
                        for r, v, i in zip(rows, vals, idxs):
                            ins = V.max_index(i[:, 8:16], v[:, 8:16], r)
                        step(ins)

                    for kp in range(N_KEYS):
                        for t in range(TT):
                            dve.wait_ge(key_evac, 4 * kp + 2 * t + 2)
                            bs = range(8 * kp, 8 * kp + 8)
                            top16([S[:, t, b, :] for b in bs], [V16[:, t, b, :] for b in bs],
                                  [I16[:, t, b, :] for b in bs])
                    for t in range(TT):
                        v = V16[:, t, :, :].rearrange("p (h e) k -> p e h k", e=2)
                        step(V.tensor_tensor(CAND[t].rearrange("p h (a b) -> p h a b", a=TOPK),
                                             bc(v[:, 0], 3, TOPK), bc(v[:, 1], 2, TOPK), ALU.add))
                        top16([CAND[t][:, h, :] for h in range(HEADS)], [VC[:, t, h, :] for h in range(HEADS)],
                              [PC[:, t, h, :] for h in range(HEADS)])
                        step(V.tensor_copy(esum[:, 0:8], VC[:, t, :, 0]))
                        V.tensor_tensor(VC[:, t, :, :], VC[:, t, :, :], bc(esum[:, 0:8], 2, TOPK),
                                        ALU.subtract).then_inc(rt_sub, 1)
                        for e in range(2):
                            if e == 0:
                                step(V.tensor_scalar(PAB, PC[:, t, :, :], 4, None, ALU.logical_shift_right))
                            else:
                                step(V.tensor_scalar(PAB, PC[:, t, :, :], TOPK - 1, None, ALU.bitwise_and))
                            step(V.tensor_tensor(EQ, bc(PAB, 3, TOPK), bc(bc(cn("iota", 0, TOPK), 1, TOPK), 1, HEADS),
                                                 ALU.is_equal))
                            step(V.tensor_tensor(EQ2, EQ, bc(I16[:, t, :, :].rearrange("p (h e) k -> p e h k", e=2)[:, e], 2, TOPK),
                                                 ALU.mult))
                            V.tensor_reduce(RT[:, t, e, :].rearrange("p (h k) -> p h k", h=HEADS), EQ2, AX.X,
                                            ALU.add).then_inc(rt_ready, 1)
                            dve.wait_ge(rt_ready, 2 * t + e + 1)
                    dve.wait_ge(rt_exp, 1)
                    for t in range(TT):
                        step(V.tensor_reduce(esum[:, 0:8], VC[:, t, :, :], AX.X, ALU.add))
                        step(V.reciprocal(esum[:, 8:16], esum[:, 0:8]))
                        V.tensor_tensor(RT[:, t, 2, :].rearrange("p (h k) -> p h k", h=HEADS), VC[:, t, :, :],
                                        bc(esum[:, 8:16], 2, TOPK), ALU.mult).then_inc(rt_ready, 1)
                    for k in range(2):
                        dve.wait_ge(rt_tr, k + 1)
                        V.tensor_copy(slotT[:, k, :], bank[k][:, 0:SEQ]).then_inc(rt_free, 1)
                    dve.wait_ge(rt_tr, 3)
                    step(V.tensor_copy(PART[:, 0, :], bank[2][:, 0:SEQ]))
                    step(V.tensor_copy(slotW[:, 0, :], PART[:, 0, :]))
                    step(V.tensor_tensor(slotW[:, 2, :], bank[2][:, 0:SEQ], slotW[:, 0, :], ALU.subtract))
                    step(V.tensor_copy(PART[:, 1, :], slotW[:, 2, :]))
                    step(V.tensor_copy(slotW[:, 1, :], PART[:, 1, :]))
                    V.tensor_tensor(slotW[:, 2, :], slotW[:, 2, :], slotW[:, 1, :], ALU.subtract).then_inc(rt_free, 1)
                    dve.wait_ge(rt_free, 3)

                    def one_hot(t0, g, half):
                        V.tensor_tensor(O2[:, 4 * g:4 * g + 4, :], bc(cn("iota"), 1, 4),
                                        bc(slotT[:, 1, bass.ds(t0, 4)], 2, P), ALU.is_equal)
                        for i in range(4):
                            ins = V.scalar_tensor_tensor(out=O1[:, 4 * g + i, :, :],
                                                         in0=bc(cn("iota", half * HK, (half + 1) * HK), 1, 3),
                                                         scalar=slotT[:, 0, bass.ds(t0 + i, 1)],
                                                         in1=slotW[:, :, bass.ds(t0 + i, 1)].broadcast_to([P, 3, HK]),
                                                         op0=ALU.is_equal, op1=ALU.mult)
                        ins.then_inc(o_ready, 1)

                    def weigh(t0, g, half):
                        acts = G[:, half * HK:(half + 1) * HK, bass.ds(t0, 4)]
                        V.tensor_tensor(acts, acts, bank[6 + g][:, 0:4 * HK].rearrange("p (i e) -> p e i", i=4),
                                        ALU.mult).then_inc(w_used, 1)

                    for g in range(2):
                        one_hot(4 * g, g, 0)
                    dve.wait_ge(gelu_done, HK // 2)
                    with dve.Fori(0, HK // SLOTS - 1) as r:
                        for s in range(SLOTS):
                            dve.wait_ge(w_done, r * SLOTS + (s + 1))
                            weigh(r * 16 + 4 * s, s % 2, 0)
                            one_hot(r * 16 + (4 * s + 8), s % 2, 0)
                    for s in range(SLOTS):
                        dve.wait_ge(w_done, HK - SLOTS + s + 1)
                        weigh(SEQ - 16 + 4 * s, s % 2, 0)
                        one_hot((SEQ - 8 + 4 * s) % SEQ, s % 2, s // 2)

                    def low_g(s, tile, value):
                        dve.wait_ge(gh_ready, value)
                        V.tensor_tensor(GL[:, s, :], G[:, tile, :], GH[:, s, :].bitcast(F32),
                                        ALU.subtract).then_inc(gl_ready, 1)

                    low_g(0, 0, 1)
                    dve.wait_ge(gelu_done, TILES // 2)
                    with dve.Fori(0, HK // SLOTS - 1) as r:
                        for s in range(SLOTS):
                            dve.wait_ge(w_done, r * SLOTS + (HK + s + 1))
                            weigh(r * 16 + 4 * s, s % 2, 1)
                            low_g((s + 1) % SLOTS, r * SLOTS + (s + 1), r * SLOTS + (s + 2))
                            one_hot(r * 16 + (4 * s + 8), s % 2, 1)
                    for s in range(SLOTS):
                        dve.wait_ge(w_done, 2 * HK - SLOTS + s + 1)
                        weigh(SEQ - 16 + 4 * s, s % 2, 1)
                        low_g((s + 1) % SLOTS, HK - SLOTS + s + 1, HK - SLOTS + s + 2)
                        if s < 2:
                            one_hot(SEQ - 8 + 4 * s, s, 1)
                    with dve.Fori(HK // SLOTS, TILES // SLOTS - 1) as r:
                        for s in range(SLOTS):
                            low_g((s + 1) % SLOTS, r * SLOTS + (s + 1), r * SLOTS + (s + 2))
                    for s in range(SLOTS - 1):
                        low_g(s + 1, TILES - SLOTS + s + 1, TILES - SLOTS + s + 2)
                    dve.wait_ge(piece_done, PIECES)
                    for k in range(4):
                        V.tensor_tensor(X[:, 2 * k:2 * k + 2, :], X[:, 2 * k:2 * k + 2, :],
                                        bank[k].rearrange("p (k m) -> p k m", k=2), ALU.add).then_inc(x_added, 1)
                    dve.wait_ge(x_added, 8)

            ids = [s.num for s in sems]
            nc.gpsimd.sem_clear(range(min(ids), max(ids) + 1))
            nc.all_engine_barrier()

        with nc.Block() as block:
            @block.scalar
            def _(act):
                nc.scalar.activation(SQ[:, :, :], X[:, :, :], ACT.Square).then_inc(f_sq, 1)
                act.wait_ge(f_var, 1)
                nc.scalar.activation(rs, var, ACT.Ln).then_inc(f_rs, 1)
                act.wait_ge(f_rs, 1)
                nc.scalar.activation(rs, rs, ACT.Exp, scale=-0.5).then_inc(f_rs, 1)

            @block.tensor
            def _(pe):
                pe.wait_ge(f_sq, 1)
                for c in range(DC):
                    mm = nc.tensor.matmul(bank[0][:, 0:SEQ], ones[:, :], SQ[:, c, :], start=(c == 0), stop=(c == DC - 1))
                mm.then_inc(f_ssq, 1)

            @block.vector
            def _(dve):
                dve.wait_ge(f_ssq, 1)
                nc.vector.tensor_scalar(var, bank[0][:, 0:SEQ], 1.0 / D, EPS, ALU.mult, ALU.add).then_inc(f_var, 1)
                dve.wait_ge(f_var, 1)
                dve.wait_ge(f_rs, 2)
                nc.vector.tensor_tensor(nt[:, :], rs, rs, ALU.mult).then_inc(f_step, 1)
                dve.wait_ge(f_step, 1)
                nc.vector.tensor_tensor(nt[:, :], nt[:, :], var, ALU.mult).then_inc(f_step, 1)
                dve.wait_ge(f_step, 2)
                nc.vector.tensor_scalar(nt[:, :], nt[:, :], -0.5, 1.5, ALU.mult, ALU.add).then_inc(f_step, 1)
                dve.wait_ge(f_step, 3)
                nc.vector.tensor_tensor(rs, rs, nt[:, :], ALU.mult).then_inc(f_step, 1)
                dve.wait_ge(f_step, 4)
                for c in range(DC):
                    nc.vector.scalar_tensor_tensor(out=H[:, c, :], in0=X[:, c, :], scalar=pr("norm_final", c, c + 1),
                                                   in1=rs, op0=ALU.mult, op1=ALU.mult).then_inc(f_out, 1)

            @block.sync
            def _(sp):
                sp.wait_ge(f_out, DC)
                sp.dma_start(out_t, H[:, :, :]).then_inc(stored, 16)
                sp.wait_ge(stored, 16)


def by_column(w):
    L, k, n = w.shape
    return w.reshape(L, DC, P, n // P, P).transpose(0, 3, 2, 1, 4).reshape(L, n // P, P, PIECE)


def by_token(w):
    L = w.shape[0]
    return w.reshape(L, 2, DC // 2, P, 256).transpose(0, 1, 3, 2, 4).reshape(L, 2, P, PIECE)


def lay_out(inp):
    f = {k: np.asarray(v) for k, v in inp.items()}
    L = DEPTH
    w_in = f["w_in"]
    off, at = {}, 0
    for name, width in (("ret_q", GW), ("ret_k", GW), ("ret_v", GW), ("ret_g", GW), ("moba_q", GW), ("moba_k", GW),
                        ("moba_v", GW), ("z", GW), ("xbc", 768), ("dt", 4), ("nsa_q", GW), ("k_cmp", HD),
                        ("v_cmp", HD), ("k_slc", HD), ("v_slc", HD), ("k_win", HD), ("v_win", HD), ("gate", 12)):
        off[name] = slice(at, at + width)
        at += width
    col = {k: w_in[:, :, s] for k, s in off.items()}
    g2 = np.zeros((L, D, 256), np.float32)
    for name, c in (("gate", GATE), ("dt", DT), ("k_win", K_WIN), ("v_win", V_WIN)):
        g2[:, :, c:c + col[name].shape[2]] = col[name]
    g1 = np.concatenate([col[k] for k in ("k_cmp", "v_cmp", "k_slc", "v_slc")], 2)
    stream = np.zeros((L, PIECES, P, PIECE), np.float32)
    stream[:, 0:2 * N_XBC] = by_column(col["xbc"])
    for n, w in ((3, g1), (4, g2), (5, col["nsa_q"]), (6, col["moba_q"]), (11, col["moba_k"]), (12, col["moba_v"]),
                 (13, col["ret_q"]), (14, col["ret_k"]), (15, col["ret_v"]), (16, col["ret_g"]), (17, col["z"])):
        stream[:, 2 * n:2 * n + 2] = by_token(w)
    for n, name in ((7, "nsa_w1_k"), (9, "nsa_w1_v")):
        w = f[name].reshape(L, 2, CHUNKS // 2, P, 2, P).transpose(0, 4, 1, 3, 2, 5)
        stream[:, 2 * n:2 * n + 4] = w.reshape(L, 4, P, PIECE)
    stream[:, 2 * OUT0:2 * (OUT0 + N_OUT)] = by_column(f["w_out"])
    stream[:, 2 * WQ0:2 * (WQ0 + N_WQ)] = by_column(f["peer_wq"])
    keys = f["peer_keys"].reshape(L, N_KEYS, 8, KEYS, P).transpose(0, 1, 4, 2, 3)
    stream[:, KEY0:KEY0 + N_KEYS] = keys.reshape(L, N_KEYS, P, PIECE)
    u = f["peer_u"].reshape(L, TILES, P, DC, P).transpose(0, 1, 4, 3, 2)
    stream[:, U0:V0] = u.reshape(L, TILES, P, PIECE)
    stream[:, V0:] = f["peer_v"].reshape(L, TILES, P, PIECE)

    params = np.zeros((L, P, NPARAM), np.float32)

    def put(name, a):
        lo, hi = PARAMS[name]
        params[:, :, lo:hi] = a.reshape(a.shape[0], P, hi - lo)

    def on_partitions(a, n):
        return a.reshape(L, n, P).transpose(0, 2, 1)

    put("norm_mix", on_partitions(f["norm_mix"], DC))
    put("norm_ffn", on_partitions(f["norm_ffn"], DC))
    put("conv_w", f["ssm_conv_w"].reshape(L, CONV, 6, P).transpose(0, 3, 2, 1))
    put("conv_b", on_partitions(f["ssm_conv_b"], 6))
    put("ret_norm", on_partitions(f["ret_norm"], 2))
    put("ssm_norm", on_partitions(f["ssm_norm"], 2))
    put("pe_k", on_partitions(f["nsa_pe_k"], CHUNKS))
    put("pe_v", on_partitions(f["nsa_pe_v"], CHUNKS))
    w2k = f["nsa_w2_k"].reshape(L, 2, P, 1, HD)
    put("w2k", np.broadcast_to(w2k, (L, 2, P, 2, HD)).transpose(0, 2, 1, 3, 4))
    put("w2v", f["nsa_w2_v"].reshape(L, 2, P, HD).transpose(0, 2, 1, 3))
    for name, src in (("dt_bias", "ssm_dt_bias"), ("a_log", "ssm_a_log"), ("ssm_d", "ssm_d")):
        put(name, np.broadcast_to(f[src][:, None, :], (L, P, NH)))
    put("norm_final", np.broadcast_to(f["norm_final"].reshape(1, DC, P).transpose(0, 2, 1), (L, P, DC)))
    x_t = np.ascontiguousarray(f["x"].reshape(SEQ, DC, P).transpose(2, 1, 0))
    return {"x_t": x_t, "stream": stream, "params": params, "consts": shape_constants()}


def kernel(**inputs):
    import concourse.bacc as bacc
    from concourse.bass_utils import run_bass_kernel_spmd as run

    nc = bacc.Bacc("TRN2", target_bir_lowering=False, num_devices=1)
    arrays = lay_out(inputs)
    args = [nc.dram_tensor(k, a.shape, F32, kind="ExternalInput").ap() for k, a in arrays.items()]
    args.append(nc.dram_tensor("out_t", (P, DC, SEQ), F32, kind="ExternalOutput").ap())
    program(nc, *args)
    r = run(nc, [arrays], core_ids=[0])
    out = r.results[0]["out_t"]
    return out.transpose(2, 1, 0).reshape(1, SEQ, D)
```

```python
from contextlib import ExitStack

import numpy as np

import concourse.bass as bass
from concourse import mybir

F32 = mybir.dt.float32
F32R = mybir.dt.float32r
BF16 = mybir.dt.bfloat16
U32 = mybir.dt.uint32
ALU = mybir.AluOpType
ACT = mybir.ActivationFunctionType
AX = mybir.AxisListType

P = 128
DEPTH, SEQ, D = 2, 256, 1024
TT = SEQ // P
DC = D // P
HD, NH = 64, 4
GW = HD * NH
NEG = -1e30
EPS = 1e-6
CONV = 4
CMP_LEN, CMP_STRIDE = 32, 16
NCMP = (SEQ - CMP_LEN) // CMP_STRIDE + 1
CPAD = 32
CHUNKS = CMP_LEN * HD // P
ROPE16 = 16
HEADS, KEYS, TOPK = 8, 128, 16
EXPERTS = KEYS * KEYS

SLOTS = 4
PIECE = 1024
N_XBC, N_PROJ, N_OUT, N_WQ = 3, 18, 4, 8
OUT0 = N_PROJ
WQ0 = OUT0 + N_OUT
PROJ = [0, 1, 2, 3, 4, 5, 6, 11, 12, 13, 14, 15, 16, 17]
SPLIT = PROJ + [OUT0 + k for k in range(N_OUT)] + [WQ0 + k for k in range(N_WQ)]
KEY0 = 2 * (WQ0 + N_WQ)
N_KEYS = 2
U0 = KEY0 + N_KEYS
HK = KEYS // 2
EXP_ROUND, TURN_ROUND = 10, 13
TILES = EXPERTS // P
V0 = U0 + TILES
PIECES = V0 + TILES
Y_BLOCK = {3: 1, 4: 0, 5: 2, 6: 3, 11: 4, 12: 5, 13: 6, 14: 7, 15: 8, 16: 9, 17: 10}
W1 = 7
M_ORDER = (6, 7, 2, 3, 0, 1, 4, 5)
GATE, DT, K_WIN, V_WIN, K_CMP, V_CMP, K_SLC, V_SLC = 0, 12, 128, 192, 256, 320, 384, 448
NSA_Q, MOBA_Q, MOBA_K, MOBA_V, RET_Q, RET_K, RET_V, RET_G, SSM_Z = (256 * i for i in range(2, 11))
YW = 11 * 256

CONSTS = {}
_at = 0
for _name, _width in (("ident", 128), ("tri", 384), ("negk", 384), ("negq", 384), ("gamma", 16),
                      ("cr", 128), ("sr", 128), ("c16", 32), ("s16", 32), ("cmpneg", 64), ("any", 2),
                      ("blkd", 4), ("iota", 128)):
    CONSTS[_name] = (_at, _at + _width)
    _at += _width
NCONST = _at
PARAMS = {}
_at = 0
for _name, _width in (("norm_mix", 8), ("norm_ffn", 8), ("conv_w", 24), ("conv_b", 6), ("ret_norm", 2),
                      ("ssm_norm", 2), ("pe_k", 16), ("pe_v", 16), ("w2k", 256), ("w2v", 128),
                      ("dt_bias", 4), ("a_log", 4), ("ssm_d", 4), ("norm_final", 8)):
    PARAMS[_name] = (_at, _at + _width)
    _at += _width
NPARAM = _at


def shape_constants():
    c = np.zeros((P, NCONST), np.float32)

    def put(name, a):
        lo, hi = CONSTS[name]
        c[:, lo:hi] = np.asarray(a, np.float32).reshape(P, hi - lo)

    p = np.arange(P)[:, None]
    t = np.arange(SEQ)
    put("ident", np.eye(P))
    age = np.concatenate([t[None, :] - p, t[None, P:] - (p + P)], 1)
    put("tri", age >= 0)
    put("negk", np.where(age >= 0, 0.0, NEG))
    ageq = np.concatenate([p - t[None, :P], p + P - t[None, :]], 1)
    put("negq", np.where(ageq >= 0, 0.0, NEG))
    lg = np.log1p(-np.exp2(-5.0 - np.arange(NH)))
    rise = (t.reshape(TT, P).T)[:, :, None] * lg
    put("gamma", np.concatenate([np.exp(rise), np.exp(-rise) * HD ** -0.5], 2))

    def rope(n, theta):
        inv = (1.0 / (np.float32(theta) ** (np.arange(0, n, 2, dtype=np.float32) / np.float32(n)))).astype(np.float32)
        ang = (t.astype(np.float32)[:, None] * inv[None, :]).astype(np.float32).astype(np.float64)
        co, si = np.cos(ang), np.sin(ang)
        both = [np.concatenate([co, co], 1), np.concatenate([-si, si], 1)]
        return [b.reshape(TT, P, n).transpose(1, 0, 2) for b in both]

    cr, sr = rope(HD, 10000.0)
    put("cr", cr)
    put("sr", sr)
    c16, s16 = rope(ROPE16, 500000.0)
    put("c16", c16)
    put("s16", s16)
    tok = t.reshape(TT, P).T[:, :, None]
    j = np.arange(CPAD)[None, None, :]
    ok = (j * CMP_STRIDE + CMP_LEN - 1 <= tok) & (j < NCMP)
    put("cmpneg", np.where(ok, 0.0, NEG))
    put("any", ok.any(-1))
    put("blkd", p // CPAD == np.arange(NH)[None, :])
    put("iota", np.broadcast_to(np.arange(P)[None, :], (P, P)))
    return c


def bc(ap, axis, n):
    u = ap.unsqueeze(axis)
    shape = list(u.shape)
    shape[axis] = n
    return u.broadcast_to(shape)


def program(nc, x_t, stream, params, consts, out_t):
    ctx = ExitStack()
    with ctx:
        def sb(name, shape, dt=F32):
            return ctx.enter_context(nc.sbuf_tensor(name, shape, dt))

        sems = []

        def sem(name):
            s = ctx.enter_context(nc.semaphore(name))
            sems.append(s)
            return s

        x_in = [ctx.enter_context(nc.semaphore(f"x_in{k}")) for k in range(4)]
        cn_in = ctx.enter_context(nc.semaphore("cn_in"))
        stored = ctx.enter_context(nc.semaphore("stored"))
        p_sq = ctx.enter_context(nc.semaphore("p_sq"))
        p_ssq = ctx.enter_context(nc.semaphore("p_ssq"))
        f_var = ctx.enter_context(nc.semaphore("f_var"))
        f_rs = ctx.enter_context(nc.semaphore("f_rs"))
        f_step = ctx.enter_context(nc.semaphore("f_step"))
        f_out = ctx.enter_context(nc.semaphore("f_out"))
        s_ones = ctx.enter_context(nc.semaphore("s_ones"))

        s_par = sem("s_par")
        landed = [sem(f"landed{i}") for i in range(SLOTS)]
        piece_done = sem("piece_done")
        mix_hi = sem("mix_hi")
        mix_used = sem("mix_used")
        mix_lo = sem("mix_lo")
        hi_ready = sem("hi_ready")
        hi_used = sem("hi_used")
        lo_ready = sem("lo_ready")
        gh_ready = sem("gh_ready")
        gl_ready = sem("gl_ready")
        hh_ready = sem("hh_ready")
        hl_ready = sem("hl_ready")
        sq_ready = sem("sq_ready")
        ssq_done = sem("ssq_done")
        var_ready = sem("var_ready")
        rs_ready = sem("rs_ready")
        h_ready = sem("h_ready")
        act_step = sem("act_step")
        dve_step = sem("dve_step")
        evac = sem("evac")
        padded = sem("padded")
        conv_ready = sem("conv_ready")
        conv_exp = sem("conv_exp")
        xc_ready = sem("xc_ready")
        roped = sem("roped")
        dup_ready = sem("dup_ready")
        dt_abs = sem("dt_abs")
        dt_exp = sem("dt_exp")
        dt_one = sem("dt_one")
        dt_ln = sem("dt_ln")
        da_ready = sem("da_ready")
        tr_done = sem("tr_done")
        tr_evac = sem("tr_evac")
        blocks_ready = sem("blocks_ready")
        hid_ready = sem("hid_ready")
        hid_tr = sem("hid_tr")
        kcvc_done = sem("kcvc_done")
        kc_ready = sem("kc_ready")
        vb_ready = sem("vb_ready")
        sc_done = sem("sc_done")
        sc_evac = sem("sc_evac")
        negm_ready = sem("negm_ready")
        exp_done = sem("exp_done")
        acs_done = sem("acs_done")
        b6_free = sem("b6_free")
        cs_ready = sem("cs_ready")
        cs_exp = sem("cs_exp")
        acr_done = sem("acr_done")
        seg_ready = sem("seg_ready")
        seg_exp = sem("seg_exp")
        ps_ready = sem("ps_ready")
        pv_done = sem("pv_done")
        pv_evac = sem("pv_evac")
        m_ready = sem("m_ready")
        z_exp = sem("z_exp")
        g_var = sem("g_var")
        g_rs = sem("g_rs")
        x_added = sem("x_added")
        qt_evac = sem("qt_evac")
        key_done = sem("key_done")
        key_evac = sem("key_evac")
        rt_sub = sem("rt_sub")
        rt_exp = sem("rt_exp")
        rt_ready = sem("rt_ready")
        rt_tr = sem("rt_tr")
        rt_free = sem("rt_free")
        gelu_done = sem("gelu_done")
        o_ready = sem("o_ready")
        w_done = sem("w_done")
        w_used = sem("w_used")

        X = sb("X", [P, DC, SEQ])
        H = sb("H", [P, DC, SEQ])
        ring = sb("ring", [P, SLOTS, PIECE])
        HH = sb("HH", [P, DC, SEQ], F32R)
        HL = sb("HL", [P, DC, SEQ], F32R)
        WH = sb("WH", [P, 2, PIECE], F32R)
        WL = sb("WL", [P, 2, PIECE], F32R)
        G = sb("G", [P, KEYS, SEQ])
        CN = sb("CN", [P, NCONST])
        PR = sb("PR", [P, NPARAM])
        ones = sb("ones", [P, P])
        VR = sb("VR", [P, 3, SEQ])
        var, rs = VR[:, 0, :], VR[:, 1, :]
        slotT = sb("slotT", [P, 2, SEQ])
        slotW = VR[:, :, :]
        PS = ctx.enter_context(nc.psum_tensor("PS", [P, 8, 512], F32))

        def cn(name, lo=0, hi=None):
            a, b = CONSTS[name]
            return CN[:, a + lo:(b if hi is None else a + hi)]

        def pr(name, lo=0, hi=None):
            a, b = PARAMS[name]
            return PR[:, a + lo:(b if hi is None else a + hi)]

        ident = cn("ident")
        Gf = G[:, :, :].rearrange("p e t -> p (e t)")
        used = [0]

        def region(width):
            lo = used[0]
            used[0] += width
            assert used[0] <= KEYS * SEQ
            return Gf[:, lo:lo + width]

        Y = region(TT * YW).rearrange("p (t n) -> p t n", t=TT)
        XBW = SEQ + CONV - 1
        XB = region(6 * XBW).rearrange("p (b n) -> p b n", b=6)
        XC = region(6 * SEQ).rearrange("p (b n) -> p b n", b=6)
        XS = region(TT * GW).rearrange("p (t n) -> p t n", t=TT)
        XDT = region(TT * GW).rearrange("p (t n) -> p t n", t=TT)
        T = region(12 * SEQ).rearrange("p (b n) -> p b n", b=12)
        TQ_NSA, TQ_MOBA, TK_MOBA, TQ_RET, TK_RET, TK_WIN, TK_SLC = 0, 2, 4, 6, 8, 10, 11
        SC4 = [region(NH * 384).rearrange("p (h n) -> p h n", h=NH) for _ in range(2)]
        PT = [region(NH * 384).rearrange("p (h n) -> p h n", h=NH) for _ in range(2)]
        SEG = region(NH * 384).rearrange("p (h n) -> p h n", h=NH)
        GS = region(2 * 384).rearrange("p (g n) -> p g n", g=2)
        DA = region(TT * NH * P).rearrange("p (t h n) -> p t h n", t=TT, h=NH)
        Mf = region(TT * D)
        M = Mf.rearrange("p (t n) -> p t n", t=TT)
        CE = Mf[:, 0:6 * SEQ].rearrange("p (b n) -> p b n", b=6)
        MTf = region(DC * SEQ)
        MT = MTf.rearrange("p (c n) -> p c n", c=DC)
        DUP = MTf[:, 0:TT * 6 * P].rearrange("p (t b e n) -> p t b e n", t=TT, b=6, e=2)
        TA = region(1024)
        TB = region(2048)
        K2 = region(2 * SEQ).rearrange("p (s n) -> p s n", s=2)
        BL = region(2 * CHUNKS * NCMP).rearrange("p (s j c) -> p s j c", s=2, j=CHUNKS)
        HV = region(2 * 2 * P).rearrange("p (s b h c) -> p s b h c", s=2, b=2, h=NH)
        HID = region(2 * 2 * P).rearrange("p (s n) -> p s n", s=2)
        KC = region(CPAD)
        VB = region(GW).rearrange("p (h n) -> p h n", h=NH)
        CS = region(TT * NH * CPAD).rearrange("p (t h c) -> p t h c", t=TT, h=NH)
        CP = region(TT * P).rearrange("p (t n) -> p t n", t=TT)
        SM = region(256)
        _s = [0]

        def small(n):
            lo = _s[0]
            _s[0] += n
            assert _s[0] <= 256
            return SM[:, lo:lo + n]

        mx = small(8)
        negm = [small(8) for _ in range(3)]
        rsum = [small(8) for _ in range(3)]
        rinv = [small(8) for _ in range(3)]
        cmx, csum, cinv = small(8), small(8), small(8)
        gate = small(24)
        dtx, dte, dtu, dtl, dtd, dtz, dta = (small(8) for _ in range(7))
        avec = small(4)
        acs = small(8)
        gvar, grs = small(4), small(4)
        rvar, rrs, gnt = small(8), small(8), small(8)

        rbase = 64 * SEQ

        def late(lo, width):
            return Gf[:, rbase + lo:rbase + lo + width]

        QT = late(0, 4096).rearrange("p (b n) -> p b n", b=16)
        S = late(4096, 4096).rearrange("p (t b n) -> p t b n", t=TT, b=16)
        CAND = [late(8192 + 2048 * t, 2048).rearrange("p (h n) -> p h n", h=HEADS) for t in range(TT)]
        EQ = late(0, 2048).rearrange("p (h k a) -> p h k a", h=HEADS, k=TOPK)
        EQ2 = late(2048, 2048).rearrange("p (h k a) -> p h k a", h=HEADS, k=TOPK)
        SQ = late(12288, 2048).rearrange("p (c n) -> p c n", c=DC)
        V16 = late(14336, 512).rearrange("p (t b k) -> p t b k", t=TT, b=16)
        I16 = late(14848, 512).rearrange("p (t b k) -> p t b k", t=TT, b=16).bitcast(U32)
        VC = late(15360, 256).rearrange("p (t h k) -> p t h k", t=TT, h=HEADS)
        PC = late(15616, 256).rearrange("p (t h k) -> p t h k", t=TT, h=HEADS).bitcast(U32)
        late_s = late(15872, 512)
        PAB = late_s[:, 0:128].bitcast(U32).rearrange("p (h k) -> p h k", h=HEADS)
        esum = late_s[:, 128:144]
        nt = late(12288, 256)
        RT = late(12544, 768).rearrange("p (t k n) -> p t k n", t=TT, k=3)

        Hf = H[:, :, :].rearrange("p c n -> p (c n)")
        O1 = Hf[:, 0:768].bitcast(BF16).rearrange("p (s k n) -> p s k n", s=8, k=3)
        O2 = Hf[:, 768:1280].bitcast(BF16).rearrange("p (s n) -> p s n", s=8)
        PART = Hf[:, 1280:1536].bitcast(BF16).rearrange("p (s n) -> p s n", s=2)
        GH, GL = HH, HL

        bank = [PS[:, b, :] for b in range(8)]

        with nc.Block() as block:
            @block.sync
            def _(sp):
                for k in range(4):
                    sp.dma_start(X[:, 2 * k:2 * k + 2, :], x_t[:, 2 * k:2 * k + 2, :]).then_inc(x_in[k], 16)
                sp.dma_start(CN[:, :], consts).then_inc(cn_in, 16)
                sp.wait_ge(cn_in, 16)

            @block.vector
            def _(dve):
                nc.vector.memset(ones[:, :], 1.0).then_inc(s_ones, 1)
                dve.wait_ge(s_ones, 1)

            @block.scalar
            def _(act):
                for k in range(4):
                    act.wait_ge(x_in[k], 16)
                    nc.scalar.activation(SQ[:, 2 * k:2 * k + 2, :], X[:, 2 * k:2 * k + 2, :],
                                         ACT.Square).then_inc(p_sq, 1)

            @block.tensor
            def _(pe):
                pe.wait_ge(s_ones, 1)
                for c in range(DC):
                    if c % 2 == 0:
                        pe.wait_ge(p_sq, c // 2 + 1)
                    mm = nc.tensor.matmul(bank[7][:, 0:SEQ], ones[:, :], SQ[:, c, :], start=(c == 0), stop=(c == DC - 1))
                mm.then_inc(p_ssq, 1)
                pe.wait_ge(p_ssq, 1)

        with nc.Fori(0, DEPTH) as layer:
            with nc.Block() as block:
                @block.sync
                def _(sp):
                    sp.dma_start(PR[:, :], params[layer]).then_inc(s_par, 16)
                    for s in range(SLOTS):
                        sp.dma_start(ring[:, s, :], stream[layer, s]).then_inc(landed[s], 16)
                    with sp.Fori(1, U0 // SLOTS + 1) as r:
                        for s in range(SLOTS):
                            sp.wait_ge(piece_done, r * SLOTS + (s - SLOTS + 1))
                            sp.dma_start(ring[:, s, :], stream[layer, r * SLOTS + s]).then_inc(landed[s], 16)
                    for n in range(SLOTS * (U0 // SLOTS + 1), U0 + SLOTS):
                        sp.wait_ge(piece_done, n - SLOTS + 1)
                        sp.dma_start(ring[:, n % SLOTS, :], stream[layer, n]).then_inc(landed[n % SLOTS], 16)
                    with sp.Fori(0, (PIECES - U0) // SLOTS - 1) as r:
                        for s in range(SLOTS):
                            sp.wait_ge(lo_ready, r * SLOTS + (s + 1))
                            n = U0 + SLOTS + s
                            sp.dma_start(ring[:, n % SLOTS, :], stream[layer, r * SLOTS + n]).then_inc(landed[n % SLOTS], 16)

                @block.gpsimd
                def _(pool):
                    nc.gpsimd.memset(XB[:, :, 0:CONV - 1], 0.0).then_inc(padded, 1)
                    nc.gpsimd.memset(HV[:, :, :, :, :], 0.0).then_inc(padded, 1)
                    def low(b, slot, done):
                        nc.gpsimd.tensor_tensor(WL[:, b, :], ring[:, slot, :], WH[:, b, :].bitcast(F32),
                                                ALU.subtract).then_inc(done, 1)

                    pieces = [2 * u + k for u in SPLIT for k in range(2)]
                    for q, n in enumerate(pieces):
                        pool.wait_ge(mix_hi, q + 1)
                        if q >= 2:
                            pool.wait_ge(piece_done, pieces[q - 2] + 1)
                        low(q % 2, n % SLOTS, mix_lo)
                    for k in range(SLOTS):
                        pool.wait_ge(hi_ready, k + 1)
                        pool.wait_ge(piece_done, U0 + k - 1 if k >= 2 else KEY0 + k - 1)
                        low(k % 2, (U0 + k) % SLOTS, lo_ready)
                    with pool.Fori(1, 2 * TILES // SLOTS) as r:
                        for s in range(SLOTS):
                            pool.wait_ge(hi_ready, r * SLOTS + (s + 1))
                            pool.wait_ge(piece_done, r * SLOTS + (U0 + s - 1))
                            low(s % 2, (U0 + s) % SLOTS, lo_ready)

                @block.tensor
                def _(pe):
                    def piece(n):
                        pe.wait_ge(landed[n % SLOTS], 16 * (n // SLOTS + 1))
                        return ring[:, n % SLOTS, :]

                    def sum_squares(k, experts):
                        pe.wait_ge(sq_ready, 4 * experts + k + 1)
                        for c in (2 * k, 2 * k + 1):
                            mm = nc.tensor.matmul(bank[7][:, 0:SEQ], ones[:, :], SQ[:, c, :],
                                                  start=(c == 0), stop=(c == DC - 1))
                        if k == 3:
                            mm.then_inc(ssq_done, 1)

                    def parts(s):
                        return [W[:, s % 2, :].rearrange("p (c m) -> p c m", c=DC) for W in (WH, WL)]

                    def by_column(u, b, first=0):
                        for k in range(2):
                            q = 2 * SPLIT.index(u) + k
                            o = bank[b][:, k * SEQ:(k + 1) * SEQ]
                            wh, wl = parts(q)
                            pe.wait_ge(mix_hi, q + 1)
                            for i, c in enumerate(M_ORDER if OUT0 <= u < WQ0 else range(DC)):
                                if first and k == 0:
                                    pe.wait_ge(hl_ready, first - 1 + i + 1)
                                nc.tensor.matmul(o, wh[:, c, :], HH[:, c, :], start=(i == 0), stop=False)
                                mm = nc.tensor.matmul(o, wh[:, c, :], HL[:, c, :], start=False, stop=False)
                            mm.then_inc(mix_used, 1)
                            pe.wait_ge(mix_lo, q + 1)
                            for c in range(DC):
                                mm = nc.tensor.matmul(o, wl[:, c, :], HH[:, c, :], start=False, stop=(c == DC - 1))
                            mm.then_inc(piece_done, 1)

                    def by_token(u, b):
                        for k in range(2):
                            q = 2 * SPLIT.index(u) + k
                            wh, wl = [W[:, q % 2, :].rearrange("p (c m) -> p c m", c=DC // 2) for W in (WH, WL)]

                            def product(h, w, c, t):
                                return nc.tensor.matmul(bank[b][:, t * 256:(t + 1) * 256],
                                                        h[:, 4 * k + c, t * P:(t + 1) * P], w[:, c, :],
                                                        start=(k == 0 and c == 0 and t == 0 and h is HH and w is wh),
                                                        stop=(k == 1 and c == DC // 2 - 1 and w is wl),
                                                        skip_group_check=True)

                            pe.wait_ge(mix_hi, q + 1)
                            for c in range(DC // 2):
                                for t in range(TT):
                                    product(HH, wh, c, t)
                                    mm = product(HL, wh, c, t)
                            mm.then_inc(mix_used, 1)
                            pe.wait_ge(mix_lo, q + 1)
                            for c in range(DC // 2):
                                for t in range(TT):
                                    mm = product(HH, wl, c, t)
                            mm.then_inc(piece_done, 1)

                    def project(n):
                        j = PROJ.index(n)
                        if j >= 2:
                            pe.wait_ge(evac, j - 1)
                        if n < N_XBC:
                            by_column(n, j % 2, first=(n == 0))
                        else:
                            by_token(n, j % 2)

                    sets = [0]

                    def turn(blocks):
                        k = sets[0]
                        if k >= 2:
                            pe.wait_ge(tr_evac, k - 1)
                        for i, b in enumerate(blocks):
                            mm = nc.tensor.transpose(bank[2 + k % 2][:, i * P:(i + 1) * P], b, ident)
                        mm.then_inc(tr_done, 1)
                        sets[0] += 1

                    def columns(c):
                        return [Y[:, t, c + i * P:c + (i + 1) * P] for i in range(2) for t in range(TT)]

                    scored = [0]

                    def scores(a, b, a_first):
                        k = scored[0]
                        if k >= 2:
                            pe.wait_ge(sc_evac, k - 1)
                        o = bank[4 + k % 2]
                        if a_first:
                            nc.tensor.matmul(o[:, 0:128], a[:, 0:P], b[:, 0:P], start=True, stop=True)
                            mm = nc.tensor.matmul(o[:, 128:384], a[:, P:SEQ], b[:, 0:SEQ], start=True, stop=True)
                        else:
                            nc.tensor.matmul(o[:, 0:256], a[:, 0:P], b[:, 0:SEQ], start=True, stop=True)
                            mm = nc.tensor.matmul(o[:, 256:384], a[:, P:SEQ], b[:, P:SEQ], start=True, stop=True)
                        mm.then_inc(sc_done, 1)
                        scored[0] += 1

                    def half(block, h):
                        return T[(h % 2) * HD:(h % 2) * HD + HD, block, :]

                    def values(weights, v, b=6):
                        for h in range(NH):
                            w, vh = weights(h), v(h)
                            nc.tensor.matmul(bank[b][:, h * HD:(h + 1) * HD], w[:, 0:P], vh[0], start=True, stop=True)
                            o = bank[b][:, 256 + h * HD:256 + (h + 1) * HD]
                            nc.tensor.matmul(o, w[:, P:2 * P], vh[0], start=True, stop=False)
                            mm = nc.tensor.matmul(o, w[:, 2 * P:3 * P], vh[1], start=False, stop=True)
                        mm.then_inc(pv_done, 1)

                    def y_values(c, step):
                        return lambda h: [Y[:, t, c + h * step:c + h * step + HD] for t in range(TT)]

                    def turn_group(buf, g):
                        for h in range(NH):
                            pe.wait_ge(exp_done, 8 * g + 2 * h + 2)
                            turn([buf[:, h, i * P:(i + 1) * P] for i in range(3)])

                    for n in (0, 1, 2, 3, 4, 5):
                        project(n)
                    pe.wait_ge(dup_ready, 2)
                    turn([DUP[:, t, b, :, :].rearrange("p e n -> p (e n)") for b in (2, 3) for t in range(TT)])
                    turn([DUP[:, t, b, :, :].rearrange("p e n -> p (e n)") for b in (0, 4) for t in range(TT)])
                    project(6)
                    for i in range(2):
                        pe.wait_ge(blocks_ready, i + 1)
                        o = bank[7][0:NCMP, i * 256:(i + 1) * 256]
                        for k in range(4):
                            w = piece(2 * W1 + 4 * i + k).rearrange("p (j m) -> p j m", j=CHUNKS // 4)
                            for j in range(CHUNKS // 4):
                                mm = nc.tensor.matmul(o, BL[:, i, CHUNKS // 4 * k + j, :], w[:, j, :],
                                                      start=(k == 0 and j == 0), stop=(k == 3 and j == CHUNKS // 4 - 1))
                            mm.then_inc(piece_done, 1)
                    pe.wait_ge(xc_ready, 1)
                    turn([XC[:, b, t * P:(t + 1) * P] for t in range(TT) for b in range(2)])
                    for g in range(2):
                        scores(XC[:, 2 + g, :], XC[:, 4 + g, :], False)
                    pe.wait_ge(roped, 2)
                    turn(columns(NSA_Q))
                    pe.wait_ge(tr_evac, 4)
                    for h in range(NH):
                        scores(half(TQ_NSA + h // 2, h), half(TK_WIN, h), True)
                    pe.wait_ge(hid_ready, 1)
                    for i in range(4):
                        mm = nc.tensor.transpose(bank[7][:, 16 * i:16 * i + NCMP],
                                                 HID[0:NCMP, i // 2, i % 2 * P:(i % 2 + 1) * P], ident[0:NCMP, 0:NCMP])
                    mm.then_inc(hid_tr, 1)
                    project(11)
                    pe.wait_ge(hid_ready, 5)
                    for b in range(2):
                        nc.tensor.matmul(bank[7][:, 64:96], pr("w2k", b * P, (b + 1) * P), HV[:, 0, b, 0, :],
                                         start=(b == 0), stop=(b == 1))
                    for b in range(2):
                        mm = nc.tensor.matmul(bank[7][:, 96:160], HV[:, 1, b, :, :].rearrange("p h c -> p (h c)"),
                                              pr("w2v", b * HD, (b + 1) * HD), start=(b == 0), stop=(b == 1))
                    mm.then_inc(kcvc_done, 1)
                    for h in range(NH):
                        scores(half(TQ_NSA + h // 2, h), half(TK_SLC, h), True)
                    project(12)
                    turn_group(SC4[0], 0)
                    pe.wait_ge(kc_ready, 1)
                    pe.wait_ge(vb_ready, 1)
                    for h in range(NH):
                        for t in range(TT):
                            at = 256 + (2 * t + h // 2) * CPAD
                            nc.tensor.matmul(bank[7 - h % 2][:, at:at + CPAD], half(TQ_NSA + h // 2, h)[:, t * P:(t + 1) * P],
                                                  KC[(h % 2) * HD:(h % 2) * HD + HD, :], start=True, stop=True)
                    pe.wait_ge(da_ready, 2)
                    dta_t = dta.rearrange("p (t h) -> p t h", t=TT)
                    tri = cn("tri")
                    nc.tensor.matmul(bank[6][:, 0:4], tri[:, 0:P], dta_t[:, 0, :], start=True, stop=True)
                    nc.tensor.matmul(bank[6][:, 4:8], tri[:, P:2 * P], dta_t[:, 0, :], start=True, stop=False)
                    nc.tensor.matmul(bank[6][:, 4:8], tri[:, 2 * P:3 * P], dta_t[:, 1, :], start=False,
                                     stop=True).then_inc(acs_done, 1)

                    def acr(pair):
                        for i in range(2):
                            h = 2 * pair + i
                            nc.tensor.matmul(bank[7][:, i * SEQ:(i + 1) * SEQ], DA[:, 0, h, :], tri[:, 0:SEQ],
                                             start=True, stop=False)
                            mm = nc.tensor.matmul(bank[7][:, i * SEQ + P:(i + 1) * SEQ], DA[:, 1, h, :],
                                                  tri[:, SEQ:SEQ + P], start=False, stop=True)
                        mm.then_inc(acr_done, 1)

                    project(13)
                    pe.wait_ge(tr_evac, 8)
                    pe.wait_ge(b6_free, 3)
                    values(lambda h: PT[0][:, h, :], y_values(V_WIN, 0))
                    acr(0)
                    project(14)
                    turn_group(SC4[1], 1)
                    pe.wait_ge(tr_evac, 12)
                    pe.wait_ge(pv_evac, 1)
                    values(lambda h: PT[1][:, h, :], y_values(V_SLC, 0))
                    pe.wait_ge(seg_ready, 2)
                    acr(1)
                    pe.wait_ge(roped, 3)
                    turn(columns(MOBA_Q))
                    turn(columns(MOBA_K))
                    project(15)
                    pe.wait_ge(tr_evac, 14)
                    for h in range(NH):
                        scores(half(TQ_MOBA + h // 2, h), half(TK_MOBA + h // 2, h), True)
                    pe.wait_ge(cs_exp, 1)
                    turn([CS[:, t, :, :].rearrange("p h c -> p (h c)") for t in range(TT)])
                    project(16)
                    pe.wait_ge(tr_evac, 15)
                    pe.wait_ge(pv_evac, 2)
                    for t in range(TT):
                        mm = nc.tensor.matmul(bank[6][:, t * GW:(t + 1) * GW], CP[:, t, :],
                                              VB[:, :, :].rearrange("p h n -> p (h n)"), start=True, stop=True)
                    mm.then_inc(pv_done, 1)
                    pe.wait_ge(roped, 4)
                    turn(columns(RET_Q))
                    turn(columns(RET_K))
                    pe.wait_ge(ps_ready, 2)
                    pe.wait_ge(pv_evac, 3)
                    values(lambda h: SEG[:, h, :], lambda h: [XDT[:, t, h * HD:(h + 1) * HD] for t in range(TT)])
                    project(17)
                    pe.wait_ge(tr_evac, 17)
                    for h in range(NH):
                        scores(half(TK_RET + h // 2, h), half(TQ_RET + h // 2, h), False)
                    turn_group(SC4[0], 2)
                    pe.wait_ge(sc_evac, 18)
                    pe.wait_ge(seg_ready, 4)
                    values(lambda h: SC4[1][:, h, :], y_values(RET_V, HD), 7)
                    pe.wait_ge(tr_evac, 21)
                    pe.wait_ge(pv_evac, 4)
                    values(lambda h: PT[0][:, h, :], y_values(MOBA_V, HD))
                    for c, ready, n in ((6, m_ready, 1), (2, pv_evac, 6), (0, m_ready, 2), (4, m_ready, 3)):
                        pe.wait_ge(ready, n)
                        turn([M[:, t, (c + i) * P:(c + i + 1) * P] for i in range(2) for t in range(TT)])
                    pe.wait_ge(tr_evac, 25)
                    pe.wait_ge(evac, len(PROJ))
                    for k in range(N_OUT):
                        if k >= 2:
                            pe.wait_ge(x_added, k - 1)
                        by_column(OUT0 + k, k % 2, first=(DC + 1 if k == 0 else 0))
                        if k >= 1:
                            sum_squares(k - 1, 0)
                    sum_squares(3, 0)

                    pe.wait_ge(x_added, N_OUT)
                    for k in range(N_WQ):
                        if k >= 2:
                            pe.wait_ge(qt_evac, k - 1)
                        by_column(WQ0 + k, k % 2, first=(2 * DC + 1 if k == 0 else 0))
                    pe.wait_ge(qt_evac, N_WQ)
                    sets_k = 0
                    for kp in range(N_KEYS):
                        w = piece(KEY0 + kp).rearrange("p (b n) -> p b n", b=8)
                        for t in range(TT):
                            for quad in range(2):
                                if sets_k >= 4:
                                    pe.wait_ge(key_evac, sets_k - 3)
                                for i in range(4):
                                    b = quad * 4 + i
                                    mm = nc.tensor.matmul(bank[sets_k % 4][:, i * P:(i + 1) * P],
                                                          QT[:, 8 * kp + b, t * P:(t + 1) * P], w[:, b, :],
                                                          start=True, stop=True)
                                mm.then_inc(piece_done if t == TT - 1 and quad == 1 else key_done, 1)
                                sets_k += 1

                    def experts_in(s, ready):
                        o = bank[4 + s // 2][:, s % 2 * SEQ:(s % 2 + 1) * SEQ]
                        wh, wl = parts(s)
                        pe.wait_ge(hi_ready, ready)
                        for c in range(DC):
                            nc.tensor.matmul(o, wh[:, c, :], HH[:, c, :], start=(c == 0), stop=False)
                            mm = nc.tensor.matmul(o, wh[:, c, :], HL[:, c, :], start=False, stop=False)
                        mm.then_inc(hi_used, 1)
                        pe.wait_ge(lo_ready, ready)
                        for c in range(DC):
                            mm = nc.tensor.matmul(o, wl[:, c, :], HH[:, c, :], start=False, stop=(c == DC - 1))
                        mm.then_inc(piece_done, 1)

                    def place(g):
                        for i in range(4):
                            o = bank[6 + g][:, i * HK:(i + 1) * HK]
                            for k in range(3):
                                mm = nc.tensor.matmul(o, O2[:, 4 * g + i, :], O1[:, 4 * g + i, k, :],
                                                      start=(k == 0), stop=(k == 2))
                        mm.then_inc(w_done, 1)

                    for s in range(SLOTS):
                        experts_in(s, s + 1)

                    def rounds_in(lo, hi):
                        with pe.Fori(lo, hi) as r:
                            for s in range(SLOTS):
                                if s % 2 == 0:
                                    pe.wait_ge(gelu_done, r * 2 + (s // 2 - 1))
                                experts_in(s, r * SLOTS + (s + 1))

                    rounds_in(1, TURN_ROUND)
                    pe.wait_ge(key_evac, 8)
                    pe.wait_ge(rt_ready, 3 * TT)
                    for k in range(3):
                        for t in range(TT):
                            mm = nc.tensor.transpose(bank[k][:, t * P:(t + 1) * P], RT[:, t, k, :], ident)
                        mm.then_inc(rt_tr, 1)
                    rounds_in(TURN_ROUND, HK // SLOTS)
                    for s in range(SLOTS):
                        if s % 2 == 0:
                            pe.wait_ge(gelu_done, HK // 2 + (s // 2 - 1))
                        pe.wait_ge(o_ready, s + 1)
                        if s >= 2:
                            pe.wait_ge(w_used, s - 1)
                        place(s % 2)
                        experts_in(s, HK + s + 1)
                    with pe.Fori(1, HK // SLOTS) as r:
                        for s in range(SLOTS):
                            if s % 2 == 0:
                                pe.wait_ge(gelu_done, r * 2 + (HK // 2 + s // 2 - 1))
                            pe.wait_ge(o_ready, r * SLOTS + (s + 1))
                            pe.wait_ge(w_used, r * SLOTS + (s - 1))
                            place(s % 2)
                            experts_in(s, r * SLOTS + (HK + s + 1))

                    def experts_out(s, ready, first, last):
                        wh, wl = parts(s)
                        gh, gl = GH[:, s, :], GL[:, s, :]
                        pe.wait_ge(gl_ready, ready)
                        pe.wait_ge(hi_ready, ready + TILES)
                        for c in range(DC):
                            o = bank[c // 2][:, (c % 2) * SEQ:(c % 2 + 1) * SEQ]
                            nc.tensor.matmul(o, wh[:, c, :], gh, start=(first and c % 2 == 0), stop=False,
                                             skip_group_check=True)
                            mm = nc.tensor.matmul(o, wh[:, c, :], gl, start=False, stop=False, skip_group_check=True)
                        mm.then_inc(hi_used, 1)
                        pe.wait_ge(lo_ready, ready + TILES)
                        for c in range(DC):
                            o = bank[c // 2][:, (c % 2) * SEQ:(c % 2 + 1) * SEQ]
                            mm = nc.tensor.matmul(o, wl[:, c, :], gh, start=False, stop=last, skip_group_check=True)
                        mm.then_inc(piece_done, 1)

                    pe.wait_ge(rt_free, 3)
                    for s in range(SLOTS):
                        pe.wait_ge(o_ready, HK + s + 1)
                        pe.wait_ge(w_used, HK + s - 1)
                        place(s % 2)
                        experts_out(s, s + 1, s == 0, False)
                    with pe.Fori(1, HK // SLOTS) as r:
                        for s in range(SLOTS):
                            pe.wait_ge(o_ready, r * SLOTS + (HK + s + 1))
                            pe.wait_ge(w_used, r * SLOTS + (HK + s - 1))
                            place(s % 2)
                            experts_out(s, r * SLOTS + (s + 1), False, False)
                    with pe.Fori(HK // SLOTS, TILES // SLOTS - 1) as r:
                        for s in range(SLOTS):
                            experts_out(s, r * SLOTS + (s + 1), False, False)
                    for s in range(SLOTS):
                        experts_out(s, TILES - SLOTS + s + 1, False, s == SLOTS - 1)
                    pe.wait_ge(w_used, 2 * HK)
                    for k in range(4):
                        sum_squares(k, 1)

                @block.scalar
                def _(act):
                    def rough_root(src, dst, ready, done, n, steps):
                        act.wait_ge(ready, n)
                        nc.scalar.activation(dst, src, ACT.Ln).then_inc(act_step, 1)
                        act.wait_ge(act_step, steps)
                        nc.scalar.activation(dst, dst, ACT.Exp, scale=-0.5).then_inc(done, 1)

                    def arrival(n):
                        return landed[n % SLOTS], 16 * (n // SLOTS + 1)

                    def upper(q):
                        n = 2 * SPLIT[q // 2] + q % 2
                        act.wait_ge(*arrival(n))
                        if q >= 2:
                            act.wait_ge(mix_used, q - 1)
                            act.wait_ge(mix_lo, q - 1)
                        nc.scalar.copy(WH[:, q % 2, :], ring[:, n % SLOTS, :]).then_inc(mix_hi, 1)

                    def take(n, next_too=True):
                        j = PROJ.index(n)
                        if next_too:
                            upper(2 * j + 2)
                            upper(2 * j + 3)
                        act.wait_ge(piece_done, 2 * n + 2)
                        b = j % 2
                        if n < N_XBC:
                            dst = XB[:, 2 * n:2 * n + 2, CONV - 1:]
                        else:
                            c = 256 * Y_BLOCK[n]
                            dst = Y[:, :, c:c + 256]
                        nc.scalar.copy(dst, bank[b].rearrange("p (k m) -> p k m", k=2)).then_inc(evac, 1)

                    turned = [0]

                    def taken(dst, width=512):
                        k = turned[0]
                        act.wait_ge(tr_done, k + 1)
                        src = bank[2 + k % 2][:, 0:width]
                        turned[0] += 1
                        return nc.scalar.copy(dst, src if len(dst.shape) == 2 else
                                              src.rearrange("p (k m) -> p k m", k=dst.shape[1]))

                    def exps(g, buf):
                        act.wait_ge(negm_ready, g + 1)
                        for h in range(NH):
                            for t in range(TT):
                                s = buf[:, h, 0:P] if t == 0 else buf[:, h, P:3 * P]
                                k = t * NH + h
                                nc.scalar.activation(s, s, ACT.Exp, bias=negm[g][:, k:k + 1], scale=HD ** -0.5,
                                                     accum_out=rsum[g][:, k:k + 1]).then_inc(exp_done, 1)

                    def probabilities(buf):
                        for h in range(NH):
                            taken(buf[:, h, :], 384).then_inc(tr_evac, 1)

                    def squares(k, added):
                        act.wait_ge(x_added, added)
                        nc.scalar.activation(SQ[:, 2 * k:2 * k + 2, :], X[:, 2 * k:2 * k + 2, :],
                                             ACT.Square).then_inc(sq_ready, 1)

                    rough_root(var, rs, var_ready, rs_ready, 1, 1)
                    upper(0)
                    for c in range(DC):
                        if c == 3:
                            upper(1)
                        act.wait_ge(h_ready, c + 1)
                        nc.scalar.copy(HH[:, c, :], H[:, c, :]).then_inc(hh_ready, 1)
                    for n in (0, 1, 2, 3, 4):
                        take(n)
                    act.wait_ge(conv_ready, 6)
                    nc.scalar.activation(CE[:, :, :], XC[:, :, :], ACT.Exp, scale=-1.0).then_inc(conv_exp, 1)
                    take(5)
                    act.wait_ge(tr_done, 1)
                    for s in range(2):
                        nc.scalar.copy(K2[0:HD, s, :], bank[2][0:HD, s * SEQ:(s + 1) * SEQ])
                        cp = nc.scalar.copy(K2[HD:P, s, 0:SEQ - 1], bank[2][HD:P, s * SEQ + 1:(s + 1) * SEQ])
                    cp.then_inc(tr_evac, 1)
                    turned[0] += 1
                    taken(T[:, TK_WIN:TK_WIN + 2, :]).then_inc(tr_evac, 1)
                    take(6, next_too=False)
                    act.wait_ge(dt_abs, 1)
                    nc.scalar.activation(dte, dte, ACT.Exp).then_inc(dt_exp, 1)
                    act.wait_ge(s_par, 16)
                    nc.scalar.activation(avec, pr("a_log"), ACT.Exp).then_inc(dt_exp, 1)
                    act.wait_ge(evac, 5)
                    nc.scalar.activation(gate.rearrange("p (t k) -> p t k", t=TT), Y[:, :, GATE:GATE + 12],
                                         ACT.Exp, scale=-1.0).then_inc(z_exp, 1)
                    act.wait_ge(dt_one, 1)
                    nc.scalar.activation(dtl, dtu, ACT.Ln).then_inc(dt_ln, 1)
                    for q in range(2):
                        upper(2 * PROJ.index(11) + q)
                    taken(XS[:, :, :]).then_inc(tr_evac, 1)
                    taken(T[:, TQ_NSA:TQ_NSA + 2, :]).then_inc(tr_evac, 1)
                    act.wait_ge(piece_done, 2 * W1 + 8)
                    nc.scalar.activation(HID[0:NCMP, :, :], bank[7][0:NCMP, :].rearrange("p (s n) -> p s n", s=2),
                                         ACT.Gelu).then_inc(hid_ready, 1)
                    act.wait_ge(padded, 2)
                    act.wait_ge(hid_tr, 1)
                    for i in range(4):
                        s, b = i // 2, i % 2
                        heads = 1 if s == 0 else NH
                        nc.scalar.copy(HV[:, s, b, 0:heads, 0:NCMP],
                                       bc(bank[7][:, 16 * i:16 * i + NCMP], 1, heads)).then_inc(hid_ready, 1)
                    exps(0, SC4[0])
                    take(11)
                    take(12)
                    probabilities(PT[0])
                    exps(1, SC4[1])
                    act.wait_ge(cs_ready, 1)
                    nc.scalar.activation(CS[:, :, :, :], CS[:, :, :, :], ACT.Exp, scale=HD ** -0.5).then_inc(cs_exp, 1)
                    take(13)
                    take(14)
                    probabilities(PT[1])
                    taken(T[:, TQ_MOBA:TQ_MOBA + 2, :]).then_inc(tr_evac, 1)
                    taken(T[:, TK_MOBA:TK_MOBA + 2, :]).then_inc(tr_evac, 1)
                    take(15)
                    act.wait_ge(seg_ready, 4)
                    nc.scalar.activation(SEG[:, :, :], SEG[:, :, :], ACT.Exp).then_inc(seg_exp, 1)
                    taken(CP[:, :, :], 256).then_inc(tr_evac, 1)
                    take(16)
                    act.wait_ge(evac, 13)
                    nc.scalar.activation(TB[:, 0:512].rearrange("p (t n) -> p t n", t=TT),
                                         Y[:, :, RET_G:RET_G + GW], ACT.Exp, scale=-1.0).then_inc(z_exp, 1)
                    taken(T[:, TQ_RET:TQ_RET + 2, :]).then_inc(tr_evac, 1)
                    taken(T[:, TK_RET:TK_RET + 2, :]).then_inc(tr_evac, 1)
                    exps(2, SC4[0])
                    take(17)
                    act.wait_ge(evac, len(PROJ))
                    nc.scalar.activation(TB[:, 512:1024].rearrange("p (t n) -> p t n", t=TT),
                                         Y[:, :, SSM_Z:SSM_Z + GW], ACT.Exp, scale=-1.0).then_inc(z_exp, 1)
                    probabilities(PT[0])
                    rough_root(rvar, rrs, g_var, g_rs, 1, 2)
                    def taken_m(c, norm_weight):
                        k = turned[0]
                        turned[0] += 1
                        act.wait_ge(tr_done, k + 1)
                        for i in range(2):
                            for dst in (MT, HH):
                                src = bank[2 + k % 2][:, i * SEQ:(i + 1) * SEQ]
                                if norm_weight is None:
                                    ins = nc.scalar.copy(dst[:, c + i, :], src)
                                else:
                                    ins = nc.scalar.mul(dst[:, c + i, :], src, pr(norm_weight, i, i + 1))
                            if i == 0:
                                ins.then_inc(hh_ready, 1)
                        ins.then_inc(tr_evac, 1)

                    taken_m(6, None)
                    rough_root(gvar, grs, g_var, g_rs, 2, 3)
                    taken_m(2, None)
                    taken_m(0, "ret_norm")
                    taken_m(4, "ssm_norm")
                    first_wq = 2 * (len(PROJ) + N_OUT)
                    for k in range(N_OUT):
                        upper(2 * (len(PROJ) + k + 1))
                        if k < N_OUT - 1:
                            upper(2 * (len(PROJ) + k + 1) + 1)
                        squares(k, k + 1)

                    upper(first_wq + 1)
                    rough_root(var, rs, var_ready, rs_ready, 2, 4)
                    for c in range(DC):
                        act.wait_ge(h_ready, DC + c + 1)
                        nc.scalar.copy(HH[:, c, :], H[:, c, :]).then_inc(hh_ready, 1)
                    for k in range(N_WQ):
                        if k < N_WQ - 1:
                            for q in range(2):
                                upper(first_wq + 2 * k + 2 + q)
                        act.wait_ge(piece_done, 2 * (WQ0 + k) + 2)
                        nc.scalar.copy(QT[:, 2 * k:2 * k + 2, :],
                                       bank[k % 2].rearrange("p (k m) -> p k m", k=2)).then_inc(qt_evac, 1)
                    def high(b, slot):
                        nc.scalar.copy(WH[:, b, :], ring[:, slot, :]).then_inc(hi_ready, 1)

                    def gelu(dst, b):
                        nc.scalar.activation(dst, bank[4 + b].rearrange("p (e n) -> p e n", e=2),
                                             ACT.Gelu).then_inc(gelu_done, 1)

                    def high_k(k):
                        act.wait_ge(*arrival(U0 + k))
                        if k >= 2:
                            act.wait_ge(hi_used, k - 1)
                            act.wait_ge(lo_ready, k - 1)
                        else:
                            act.wait_ge(mix_used, 2 * len(SPLIT) - 1 + k)
                            act.wait_ge(mix_lo, 2 * len(SPLIT) - 1 + k)
                        high(k % 2, (U0 + k) % SLOTS)

                    def high_r(r, s, k0=0):
                        q, n = arrival(U0 + k0 + s)
                        act.wait_ge(q, r * 16 + n)
                        act.wait_ge(hi_used, r * SLOTS + (k0 + s - 1))
                        act.wait_ge(lo_ready, r * SLOTS + (k0 + s - 1))
                        high(s % 2, (U0 + s) % SLOTS)

                    for k in range(2):
                        high_k(k)
                    for k in range(8):
                        kp, t, quad = k // 4, k // 2 % 2, k % 2
                        if k % 4 == 3:
                            act.wait_ge(piece_done, KEY0 + kp + 1)
                        else:
                            act.wait_ge(key_done, 3 * kp + k % 4 + 1)
                        nc.scalar.copy(S[:, t, 8 * kp + 4 * quad:8 * kp + 4 * quad + 4, :],
                                       bank[k % 4].rearrange("p (b n) -> p b n", b=4)).then_inc(key_evac, 1)

                    for k in (2, 3):
                        high_k(k)
                    act.wait_ge(piece_done, U0 + 2)
                    gelu(G[:, 0:2, :], 0)

                    def rounds_gelu(lo, hi):
                        with act.Fori(lo, hi) as r:
                            for s in range(SLOTS):
                                high_r(r, s)
                                if s == 1:
                                    act.wait_ge(piece_done, r * SLOTS + U0)
                                    gelu(G[:, bass.ds(r * SLOTS - 2, 2), :], 1)
                                if s == 3:
                                    act.wait_ge(piece_done, r * SLOTS + (U0 + 2))
                                    gelu(G[:, bass.ds(r * SLOTS, 2), :], 0)

                    rounds_gelu(1, EXP_ROUND)
                    act.wait_ge(rt_sub, TT)
                    nc.scalar.activation(VC[:, :, :, :], VC[:, :, :, :], ACT.Exp).then_inc(rt_exp, 1)
                    rounds_gelu(EXP_ROUND, HK // SLOTS)
                    act.wait_ge(rt_free, 3)
                    rounds_gelu(HK // SLOTS, TILES // SLOTS)

                    def high_g(s, tile):
                        nc.scalar.copy(GH[:, s, :], G[:, tile, :]).then_inc(gh_ready, 1)

                    high_k(TILES)
                    act.wait_ge(w_used, HK)
                    act.wait_ge(piece_done, V0)
                    high_g(0, 0)
                    gelu(G[:, TILES - 2:TILES, :], 1)
                    high_g(1, 1)
                    for s in range(1, SLOTS):
                        high_k(TILES + s)
                        high_g((s + 1) % SLOTS, s + 1)

                    def rounds_out(lo, hi, last):
                        with act.Fori(lo, hi) as r:
                            for s in range(last):
                                high_r(r, s, TILES)
                                high_g((s + 1) % SLOTS, r * SLOTS + (s + 1))

                    rounds_out(1, HK // SLOTS - 1, SLOTS)
                    for s in range(SLOTS):
                        high_k(TILES + HK - SLOTS + s)
                        if s == SLOTS - 1:
                            act.wait_ge(w_used, 2 * HK)
                        high_g((s + 1) % SLOTS, HK - SLOTS + s + 1)
                    rounds_out(HK // SLOTS, TILES // SLOTS - 1, SLOTS)
                    for s in range(SLOTS):
                        high_k(2 * TILES - SLOTS + s)
                        if s < SLOTS - 1:
                            high_g(s + 1, TILES - SLOTS + s + 1)
                    for k in range(4):
                        squares(k, N_OUT + k + 1)

                @block.vector
                def _(dve):
                    n = [0]

                    def step(ins):
                        n[0] += 1
                        ins.then_inc(dve_step, 1)
                        dve.wait_ge(dve_step, n[0])

                    V = nc.vector

                    def newton(v, r, t):
                        step(V.tensor_tensor(t, r, r, ALU.mult))
                        step(V.tensor_tensor(t, t, v, ALU.mult))
                        step(V.tensor_scalar(t, t, -0.5, 1.5, ALU.mult, ALU.add))
                        step(V.tensor_tensor(r, r, t, ALU.mult))

                    def lower(c, ready, whole):
                        dve.wait_ge(hh_ready, ready)
                        V.tensor_tensor(HL[:, c, :], whole[:, c, :], HH[:, c, :].bitcast(F32),
                                        ALU.subtract).then_inc(hl_ready, 1)

                    def norm(k, weight):
                        hh0 = (0, DC + DC // 2)
                        if k == 1:
                            dve.wait_ge(ssq_done, 1)
                        V.tensor_scalar(var, bank[7][:, 0:SEQ], 1.0 / D, EPS, ALU.mult, ALU.add).then_inc(var_ready, 1)
                        dve.wait_ge(var_ready, k + 1)
                        dve.wait_ge(rs_ready, k + 1)
                        newton(var, rs, nt[:, :])
                        if k == 0:
                            dve.wait_ge(s_par, 16)
                        for c in range(DC):
                            V.scalar_tensor_tensor(out=H[:, c, :], in0=X[:, c, :], scalar=pr(weight, c, c + 1),
                                                   in1=rs, op0=ALU.mult, op1=ALU.mult).then_inc(h_ready, 1)
                            if c >= 1:
                                lower(c - 1, hh0[k] + c, H)
                        lower(DC - 1, hh0[k] + DC, H)

                    def rope(y, cos, sin, half, heads):
                        w = TT * heads * 2 * half
                        a = TA[:, 0:w].rearrange("p (t h d) -> p t h d", t=TT, h=heads)
                        b = TB[:, 1024:1024 + w].rearrange("p (t h d) -> p t h d", t=TT, h=heads)
                        c = bc(cos.rearrange("p (t d) -> p t d", t=TT), 2, heads)
                        s = bc(sin.rearrange("p (t d) -> p t d", t=TT), 2, heads)
                        V.tensor_tensor(a, y, c, ALU.mult)
                        V.tensor_tensor(b[:, :, :, 0:half], y[:, :, :, half:], s[:, :, :, 0:half], ALU.mult)
                        step(V.tensor_tensor(b[:, :, :, half:], y[:, :, :, 0:half], s[:, :, :, half:], ALU.mult))
                        return V.tensor_tensor(y, a, b, ALU.add)

                    def silu_factor(e):
                        step(V.tensor_scalar(e, e, 1.0, None, ALU.add))
                        step(V.reciprocal(e, e))

                    def attention_scores(g, buf, first):
                        for h in range(NH):
                            dve.wait_ge(sc_done, first + h + 1)
                            V.tensor_tensor(buf[:, h, :], bank[4 + h % 2][:, 0:384], cn("negq"), ALU.add).then_inc(sc_evac, 1)
                        dve.wait_ge(sc_evac, first + NH)
                        V.tensor_reduce(mx[:, 0:4], buf[:, :, 0:P], AX.X, ALU.max)
                        step(V.tensor_reduce(mx[:, 4:8], buf[:, :, P:3 * P], AX.X, ALU.max))
                        V.tensor_scalar(negm[g], mx, -(HD ** -0.5), None, ALU.mult).then_inc(negm_ready, 1)

                    def heads(flat):
                        return flat.rearrange("p (t h d) -> p t h d", t=TT, h=NH)

                    def columns(f8):
                        return bc(f8.rearrange("p (t h) -> p t h", t=TT), 3, HD)

                    def m_part(c):
                        return M[:, :, c:c + GW].rearrange("p t (h d) -> p t h d", h=NH)

                    def nsa_factor(g, kind):
                        dve.wait_ge(exp_done, 8 * g + 8)
                        step(V.reciprocal(rinv[g], rsum[g]))
                        if kind is not None:
                            step(V.tensor_tensor(rinv[g].rearrange("p (t h) -> p t h", t=TT),
                                                 rinv[g].rearrange("p (t h) -> p t h", t=TT),
                                                 gate.rearrange("p (t k h) -> p t k h", t=TT, k=3)[:, :, kind, :],
                                                 ALU.mult))

                    norm(0, "norm_mix")

                    dve.wait_ge(padded, 1)
                    for b in range(6):
                        dve.wait_ge(evac, b // 2 + 1)
                        w = pr("conv_w").rearrange("p (b j) -> p b j", b=6)
                        step(V.tensor_scalar(XC[:, b, :], XB[:, b, 0:SEQ], w[:, b, 0:1], pr("conv_b", b, b + 1),
                                             ALU.mult, ALU.add))
                        for j in range(1, CONV):
                            ins = V.scalar_tensor_tensor(out=XC[:, b, :], in0=XB[:, b, j:j + SEQ], scalar=w[:, b, j:j + 1],
                                                         in1=XC[:, b, :], op0=ALU.mult, op1=ALU.add)
                            if j < CONV - 1:
                                step(ins)
                            else:
                                ins.then_inc(conv_ready, 1)

                    dve.wait_ge(evac, 5)
                    rope(Y[:, :, K_WIN:K_WIN + 384].rearrange("p t (b n) -> p t b n", n=P)[:, :, :, 0:ROPE16],
                         cn("c16"), cn("s16"), ROPE16 // 2, 3).then_inc(roped, 1)
                    dve.wait_ge(roped, 1)
                    for e in range(2):
                        V.tensor_copy(DUP[:, :, :, e, :],
                                      Y[:, :, K_WIN:K_WIN + 384].rearrange("p t (b n) -> p t b n", n=HD)).then_inc(dup_ready, 1)
                    x8 = dtx.rearrange("p (t h) -> p t h", t=TT)
                    step(V.tensor_tensor(x8, Y[:, :, DT:DT + NH], bc(pr("dt_bias"), 1, TT), ALU.add))
                    step(V.tensor_scalar(dtz, dtx, -1.0, None, ALU.mult))
                    V.tensor_tensor(dte, dtx, dtz, ALU.min).then_inc(dt_abs, 1)
                    dve.wait_ge(tr_evac, 1)
                    for s, pe_name in enumerate(("pe_k", "pe_v")):
                        k2 = K2[:, s, :].rearrange("p (c j e) -> p e j c", e=2, j=CMP_STRIDE // 2)
                        for hi in range(2):
                            src = k2[:, 0, :, hi:hi + NCMP]
                            ins = V.tensor_tensor(BL[:, s, 8 * hi:8 * hi + 8, :], src,
                                                  bc(pr(pe_name, 8 * hi, 8 * hi + 8), 2, NCMP), ALU.add)
                            if hi == 1:
                                ins.then_inc(blocks_ready, 1)
                    dve.wait_ge(conv_exp, 1)
                    step(V.tensor_scalar(CE[:, :, :], CE[:, :, :], 1.0, None, ALU.add))
                    step(V.reciprocal(CE[:, :, :], CE[:, :, :]))
                    V.tensor_tensor(XC[:, :, :], XC[:, :, :], CE[:, :, :], ALU.mult).then_inc(xc_ready, 1)
                    dve.wait_ge(evac, 6)
                    rope(Y[:, :, NSA_Q:NSA_Q + GW].rearrange("p t (b n) -> p t b n", n=HD)[:, :, :, 0:ROPE16],
                         cn("c16"), cn("s16"), ROPE16 // 2, NH).then_inc(roped, 1)
                    dve.wait_ge(dt_exp, 1)
                    V.tensor_scalar(dtu, dte, 1.0, None, ALU.add).then_inc(dt_one, 1)
                    dve.wait_ge(dt_one, 1)
                    step(V.tensor_scalar(dtd, dtu, -1.0, None, ALU.add))
                    step(V.tensor_scalar(dtz, dtd, 0.0, None, ALU.is_equal))
                    step(V.tensor_tensor(dtd, dtd, dtz, ALU.add))
                    step(V.reciprocal(dtd, dtd))
                    dve.wait_ge(dt_ln, 1)
                    step(V.tensor_tensor(dtl, dtl, dtz, ALU.add))
                    step(V.tensor_tensor(dtl, dtl, dtd, ALU.mult))
                    step(V.tensor_tensor(dtl, dtl, dte, ALU.mult))
                    step(V.tensor_scalar(dtx, dtx, 0.0, None, ALU.max))
                    step(V.tensor_tensor(dtx, dtx, dtl, ALU.add))
                    dve.wait_ge(dt_exp, 2)
                    step(V.tensor_scalar(avec, avec, -1.0, None, ALU.mult))
                    V.tensor_tensor(dta.rearrange("p (t h) -> p t h", t=TT), x8, bc(avec, 1, TT), ALU.mult).then_inc(da_ready, 1)
                    dve.wait_ge(da_ready, 1)
                    V.tensor_copy(DA[:, :, :, :], bc(dta.rearrange("p (t h) -> p t h", t=TT), 3, P)).then_inc(da_ready, 1)
                    dve.wait_ge(z_exp, 1)
                    silu_factor(gate)
                    for g in range(2):
                        dve.wait_ge(sc_done, g + 1)
                        V.tensor_copy(GS[:, g, :], bank[4 + g][:, 0:384]).then_inc(sc_evac, 1)
                    attention_scores(0, SC4[0], 2)
                    attention_scores(1, SC4[1], 6)
                    dve.wait_ge(kcvc_done, 1)
                    V.tensor_copy(KC, bank[7][:, 64:96]).then_inc(kc_ready, 1)
                    V.tensor_tensor(VB[:, :, :], bc(bank[7][:, 96:160], 1, NH), bc(cn("blkd"), 2, HD),
                                    ALU.mult).then_inc(vb_ready, 1)
                    dve.wait_ge(acs_done, 1)
                    cs_e = CS[:, :, :, :].rearrange("p t (i e) c -> p e t i c", e=2)
                    for e in range(2):
                        V.tensor_tensor(cs_e[:, e], bank[7 - e][:, 256:384].rearrange("p (t i c) -> p t i c", t=TT, i=2),
                                        bc(cn("cmpneg").rearrange("p (t c) -> p t c", t=TT), 2, 2), ALU.add).then_inc(b6_free, 1)
                    dve.wait_ge(b6_free, 2)
                    V.tensor_copy(acs, bank[6][:, 0:8]).then_inc(b6_free, 1)
                    cs8 = CS[:, :, :, :].rearrange("p t h c -> p (t h) c")
                    step(V.tensor_reduce(cmx, cs8, AX.X, ALU.max))
                    V.tensor_tensor(cs8, cs8, bc(cmx, 2, CPAD), ALU.subtract).then_inc(cs_ready, 1)
                    nsa_factor(0, 2)
                    dve.wait_ge(pv_done, 1)
                    V.tensor_tensor(m_part(768), heads(bank[6]), columns(rinv[0]), ALU.mult).then_inc(pv_evac, 1)

                    def decays(pair):
                        dve.wait_ge(acr_done, pair + 1)
                        for i in range(2):
                            h = 2 * pair + i
                            V.scalar_tensor_tensor(out=SEG[:, h, 0:256], in0=bank[7][:, i * SEQ:(i + 1) * SEQ],
                                                   scalar=acs[:, h:h + 1], in1=cn("negk", 0, 256),
                                                   op0=ALU.subtract, op1=ALU.add)
                            V.scalar_tensor_tensor(out=SEG[:, h, 256:384], in0=bank[7][:, i * SEQ + P:(i + 1) * SEQ],
                                                   scalar=acs[:, 4 + h:5 + h], in1=cn("negk", 256, 384),
                                                   op0=ALU.subtract, op1=ALU.add).then_inc(seg_ready, 1)

                    dve.wait_ge(b6_free, 3)
                    decays(0)
                    dve.wait_ge(evac, 8)
                    rope(Y[:, :, MOBA_Q:MOBA_Q + 2 * GW].rearrange("p t (b n) -> p t b n", n=HD)[:, :, :, 0:ROPE16],
                         cn("c16"), cn("s16"), ROPE16 // 2, 2 * NH).then_inc(roped, 1)
                    dve.wait_ge(roped, 3)
                    nsa_factor(1, 1)
                    dve.wait_ge(pv_done, 2)
                    V.tensor_tensor(heads(TA[:, 0:512]), heads(bank[6]), columns(rinv[1]), ALU.mult).then_inc(pv_evac, 1)
                    dve.wait_ge(pv_evac, 2)
                    step(V.tensor_tensor(m_part(768), m_part(768), heads(TA[:, 0:512]), ALU.add))
                    decays(1)
                    dve.wait_ge(cs_exp, 1)
                    step(V.tensor_reduce(csum, cs8, AX.X, ALU.add))
                    step(V.reciprocal(cinv, csum))
                    c8 = cinv.rearrange("p (t h) -> p t h", t=TT)
                    step(V.tensor_tensor(c8, c8, bc(cn("any"), 2, NH), ALU.mult))
                    step(V.tensor_tensor(c8, c8, gate.rearrange("p (t k h) -> p t k h", t=TT, k=3)[:, :, 0, :], ALU.mult))
                    dve.wait_ge(evac, 11)
                    dve.wait_ge(roped, 3)
                    qk = Y[:, :, RET_Q:RET_Q + 2 * GW].rearrange("p t (b n) -> p t b n", n=HD)
                    step(rope(qk, cn("cr"), cn("sr"), HD // 2, 2 * NH))
                    V.tensor_tensor(qk, qk, bc(cn("gamma").rearrange("p (t b) -> p t b", t=TT), 3, HD),
                                    ALU.mult).then_inc(roped, 1)
                    attention_scores(2, SC4[0], 10)
                    dve.wait_ge(tr_evac, 3)
                    V.tensor_tensor(heads(XDT[:, :, :].rearrange("p t n -> p (t n)")),
                                    heads(XS[:, :, :].rearrange("p t n -> p (t n)")), columns(dtx), ALU.mult).then_inc(ps_ready, 1)
                    dve.wait_ge(seg_exp, 1)
                    V.tensor_tensor(SEG[:, :, :].rearrange("p (g h) n -> p g h n", g=2),
                                    SEG[:, :, :].rearrange("p (g h) n -> p g h n", g=2), bc(GS[:, :, :], 2, 2),
                                    ALU.mult).then_inc(ps_ready, 1)
                    dve.wait_ge(pv_done, 3)
                    V.tensor_tensor(heads(TA[:, 0:512]), heads(bank[6]), columns(cinv), ALU.mult).then_inc(pv_evac, 1)
                    dve.wait_ge(pv_evac, 3)
                    V.tensor_tensor(m_part(768), m_part(768), heads(TA[:, 0:512]), ALU.add).then_inc(m_ready, 1)
                    dve.wait_ge(z_exp, 2)
                    silu_factor(TB[:, 0:512])
                    for h in range(NH):
                        dve.wait_ge(sc_done, 15 + h)
                        V.tensor_tensor(SC4[1][:, h, :], bank[4 + h % 2][:, 0:384], cn("tri"),
                                        ALU.mult).then_inc(sc_evac, 1)
                    ya = TA[:, 0:512]
                    yb = TA[:, 512:1024]
                    step(V.tensor_tensor(heads(yb), heads(XS[:, :, :].rearrange("p t n -> p (t n)")),
                                         bc(bc(pr("ssm_d"), 2, HD), 1, TT), ALU.mult))
                    dve.wait_ge(pv_done, 4)
                    V.tensor_tensor(ya, bank[6], yb, ALU.add).then_inc(pv_evac, 1)
                    dve.wait_ge(z_exp, 3)
                    silu_factor(TB[:, 512:1024])
                    dve.wait_ge(pv_evac, 4)
                    ra, rb = TB[:, 1024:1536], TB[:, 1536:2048]
                    dve.wait_ge(pv_done, 5)
                    V.tensor_copy(ra, bank[7]).then_inc(pv_evac, 1)
                    dve.wait_ge(pv_evac, 5)
                    step(V.tensor_tensor(rb, ra, ra, ALU.mult))
                    step(V.tensor_reduce(rvar, rb.rearrange("p (k n) -> p k n", n=HD), AX.X, ALU.add))
                    V.tensor_scalar(rvar, rvar, 1.0 / HD, EPS, ALU.mult, ALU.add).then_inc(g_var, 1)
                    step(V.tensor_tensor(ya, ya, TB[:, 512:1024], ALU.mult))
                    yt = ya.rearrange("p (t n) -> p t n", t=TT)
                    step(V.tensor_tensor(yt, yt, Y[:, :, SSM_Z:SSM_Z + GW], ALU.mult))
                    step(V.tensor_tensor(yb, ya, ya, ALU.mult))
                    step(V.tensor_reduce(gvar, yb.rearrange("p (k n) -> p k n", n=P), AX.X, ALU.add))
                    V.tensor_scalar(gvar, gvar, 1.0 / P, EPS, ALU.mult, ALU.add).then_inc(g_var, 1)
                    nsa_factor(2, None)
                    dve.wait_ge(pv_done, 6)
                    V.tensor_tensor(m_part(256), heads(bank[6]), columns(rinv[2]), ALU.mult).then_inc(pv_evac, 1)
                    rt = ra.rearrange("p (t n) -> p t n", t=TT)
                    step(V.tensor_tensor(ra, ra, TB[:, 0:512], ALU.mult))
                    step(V.tensor_tensor(rt, rt, Y[:, :, RET_G:RET_G + GW], ALU.mult))
                    dve.wait_ge(g_var, 1)
                    dve.wait_ge(g_rs, 1)
                    newton(rvar, rrs, gnt)
                    V.tensor_tensor(m_part(0), heads(ra), columns(rrs), ALU.mult).then_inc(m_ready, 1)
                    dve.wait_ge(g_rs, 2)
                    newton(gvar, grs, gnt[:, 0:4])
                    V.tensor_tensor(M[:, :, 512:768].rearrange("p t (g n) -> p t g n", g=2),
                                    ya.rearrange("p (t g n) -> p t g n", t=TT, g=2),
                                    bc(grs.rearrange("p (t g) -> p t g", t=TT), 3, P), ALU.mult).then_inc(m_ready, 1)
                    for i, c in enumerate(M_ORDER):
                        if i % 2 == 1:
                            dve.wait_ge(tr_evac, 22 + i // 2)
                        lower(c, DC + i // 2 + 1, MT)
                    for k in range(N_OUT):
                        dve.wait_ge(piece_done, 2 * (OUT0 + k) + 2)
                        V.tensor_tensor(X[:, 2 * k:2 * k + 2, :], X[:, 2 * k:2 * k + 2, :],
                                        bank[k % 2].rearrange("p (k m) -> p k m", k=2), ALU.add).then_inc(x_added, 1)

                    dve.wait_ge(x_added, N_OUT)
                    norm(1, "norm_ffn")

                    def top16(rows, vals, idxs):
                        for r, v in zip(rows, vals):
                            ins = V.max(v[:, 0:8], r)
                        step(ins)
                        for r, v, i in zip(rows, vals, idxs):
                            V.max_index(i[:, 0:8], v[:, 0:8], r)
                            ins = V.match_replace(r, v[:, 0:8], r, -3e38)
                        step(ins)
                        for r, v in zip(rows, vals):
                            ins = V.max(v[:, 8:16], r)
                        step(ins)
                        for r, v, i in zip(rows, vals, idxs):
                            ins = V.max_index(i[:, 8:16], v[:, 8:16], r)
                        step(ins)

                    for kp in range(N_KEYS):
                        for t in range(TT):
                            dve.wait_ge(key_evac, 4 * kp + 2 * t + 2)
                            bs = range(8 * kp, 8 * kp + 8)
                            top16([S[:, t, b, :] for b in bs], [V16[:, t, b, :] for b in bs],
                                  [I16[:, t, b, :] for b in bs])
                    for t in range(TT):
                        v = V16[:, t, :, :].rearrange("p (h e) k -> p e h k", e=2)
                        step(V.tensor_tensor(CAND[t].rearrange("p h (a b) -> p h a b", a=TOPK),
                                             bc(v[:, 0], 3, TOPK), bc(v[:, 1], 2, TOPK), ALU.add))
                        top16([CAND[t][:, h, :] for h in range(HEADS)], [VC[:, t, h, :] for h in range(HEADS)],
                              [PC[:, t, h, :] for h in range(HEADS)])
                        step(V.tensor_copy(esum[:, 0:8], VC[:, t, :, 0]))
                        V.tensor_tensor(VC[:, t, :, :], VC[:, t, :, :], bc(esum[:, 0:8], 2, TOPK),
                                        ALU.subtract).then_inc(rt_sub, 1)
                        for e in range(2):
                            if e == 0:
                                step(V.tensor_scalar(PAB, PC[:, t, :, :], 4, None, ALU.logical_shift_right))
                            else:
                                step(V.tensor_scalar(PAB, PC[:, t, :, :], TOPK - 1, None, ALU.bitwise_and))
                            step(V.tensor_tensor(EQ, bc(PAB, 3, TOPK), bc(bc(cn("iota", 0, TOPK), 1, TOPK), 1, HEADS),
                                                 ALU.is_equal))
                            step(V.tensor_tensor(EQ2, EQ, bc(I16[:, t, :, :].rearrange("p (h e) k -> p e h k", e=2)[:, e], 2, TOPK),
                                                 ALU.mult))
                            V.tensor_reduce(RT[:, t, e, :].rearrange("p (h k) -> p h k", h=HEADS), EQ2, AX.X,
                                            ALU.add).then_inc(rt_ready, 1)
                            dve.wait_ge(rt_ready, 2 * t + e + 1)
                    dve.wait_ge(rt_exp, 1)
                    for t in range(TT):
                        step(V.tensor_reduce(esum[:, 0:8], VC[:, t, :, :], AX.X, ALU.add))
                        step(V.reciprocal(esum[:, 8:16], esum[:, 0:8]))
                        V.tensor_tensor(RT[:, t, 2, :].rearrange("p (h k) -> p h k", h=HEADS), VC[:, t, :, :],
                                        bc(esum[:, 8:16], 2, TOPK), ALU.mult).then_inc(rt_ready, 1)
                    for k in range(2):
                        dve.wait_ge(rt_tr, k + 1)
                        V.tensor_copy(slotT[:, k, :], bank[k][:, 0:SEQ]).then_inc(rt_free, 1)
                    dve.wait_ge(rt_tr, 3)
                    step(V.tensor_copy(PART[:, 0, :], bank[2][:, 0:SEQ]))
                    step(V.tensor_copy(slotW[:, 0, :], PART[:, 0, :]))
                    step(V.tensor_tensor(slotW[:, 2, :], bank[2][:, 0:SEQ], slotW[:, 0, :], ALU.subtract))
                    step(V.tensor_copy(PART[:, 1, :], slotW[:, 2, :]))
                    step(V.tensor_copy(slotW[:, 1, :], PART[:, 1, :]))
                    V.tensor_tensor(slotW[:, 2, :], slotW[:, 2, :], slotW[:, 1, :], ALU.subtract).then_inc(rt_free, 1)
                    dve.wait_ge(rt_free, 3)

                    def one_hot(t0, g, half):
                        V.tensor_tensor(O2[:, 4 * g:4 * g + 4, :], bc(cn("iota"), 1, 4),
                                        bc(slotT[:, 1, bass.ds(t0, 4)], 2, P), ALU.is_equal)
                        for i in range(4):
                            ins = V.scalar_tensor_tensor(out=O1[:, 4 * g + i, :, :],
                                                         in0=bc(cn("iota", half * HK, (half + 1) * HK), 1, 3),
                                                         scalar=slotT[:, 0, bass.ds(t0 + i, 1)],
                                                         in1=slotW[:, :, bass.ds(t0 + i, 1)].broadcast_to([P, 3, HK]),
                                                         op0=ALU.is_equal, op1=ALU.mult)
                        ins.then_inc(o_ready, 1)

                    def weigh(t0, g, half):
                        acts = G[:, half * HK:(half + 1) * HK, bass.ds(t0, 4)]
                        V.tensor_tensor(acts, acts, bank[6 + g][:, 0:4 * HK].rearrange("p (i e) -> p e i", i=4),
                                        ALU.mult).then_inc(w_used, 1)

                    for g in range(2):
                        one_hot(4 * g, g, 0)
                    dve.wait_ge(gelu_done, HK // 2)
                    with dve.Fori(0, HK // SLOTS - 1) as r:
                        for s in range(SLOTS):
                            dve.wait_ge(w_done, r * SLOTS + (s + 1))
                            weigh(r * 16 + 4 * s, s % 2, 0)
                            one_hot(r * 16 + (4 * s + 8), s % 2, 0)
                    for s in range(SLOTS):
                        dve.wait_ge(w_done, HK - SLOTS + s + 1)
                        weigh(SEQ - 16 + 4 * s, s % 2, 0)
                        one_hot((SEQ - 8 + 4 * s) % SEQ, s % 2, s // 2)

                    def low_g(s, tile, value):
                        dve.wait_ge(gh_ready, value)
                        V.tensor_tensor(GL[:, s, :], G[:, tile, :], GH[:, s, :].bitcast(F32),
                                        ALU.subtract).then_inc(gl_ready, 1)

                    low_g(0, 0, 1)
                    dve.wait_ge(gelu_done, TILES // 2)
                    with dve.Fori(0, HK // SLOTS - 1) as r:
                        for s in range(SLOTS):
                            dve.wait_ge(w_done, r * SLOTS + (HK + s + 1))
                            weigh(r * 16 + 4 * s, s % 2, 1)
                            low_g((s + 1) % SLOTS, r * SLOTS + (s + 1), r * SLOTS + (s + 2))
                            one_hot(r * 16 + (4 * s + 8), s % 2, 1)
                    for s in range(SLOTS):
                        dve.wait_ge(w_done, 2 * HK - SLOTS + s + 1)
                        weigh(SEQ - 16 + 4 * s, s % 2, 1)
                        low_g((s + 1) % SLOTS, HK - SLOTS + s + 1, HK - SLOTS + s + 2)
                        if s < 2:
                            one_hot(SEQ - 8 + 4 * s, s, 1)
                    with dve.Fori(HK // SLOTS, TILES // SLOTS - 1) as r:
                        for s in range(SLOTS):
                            low_g((s + 1) % SLOTS, r * SLOTS + (s + 1), r * SLOTS + (s + 2))
                    for s in range(SLOTS - 1):
                        low_g(s + 1, TILES - SLOTS + s + 1, TILES - SLOTS + s + 2)
                    dve.wait_ge(piece_done, PIECES)
                    for k in range(4):
                        V.tensor_tensor(X[:, 2 * k:2 * k + 2, :], X[:, 2 * k:2 * k + 2, :],
                                        bank[k].rearrange("p (k m) -> p k m", k=2), ALU.add).then_inc(x_added, 1)
                    dve.wait_ge(ssq_done, 2)

            ids = [s.num for s in sems]
            nc.gpsimd.sem_clear(range(min(ids), max(ids) + 1))
            nc.all_engine_barrier()

        with nc.Block() as block:
            @block.scalar
            def _(act):
                act.wait_ge(f_var, 1)
                nc.scalar.activation(rs, var, ACT.Ln).then_inc(f_rs, 1)
                act.wait_ge(f_rs, 1)
                nc.scalar.activation(rs, rs, ACT.Exp, scale=-0.5).then_inc(f_rs, 1)

            @block.vector
            def _(dve):
                nc.vector.tensor_scalar(var, bank[7][:, 0:SEQ], 1.0 / D, EPS, ALU.mult, ALU.add).then_inc(f_var, 1)
                dve.wait_ge(f_var, 1)
                dve.wait_ge(f_rs, 2)
                nc.vector.tensor_tensor(nt[:, :], rs, rs, ALU.mult).then_inc(f_step, 1)
                dve.wait_ge(f_step, 1)
                nc.vector.tensor_tensor(nt[:, :], nt[:, :], var, ALU.mult).then_inc(f_step, 1)
                dve.wait_ge(f_step, 2)
                nc.vector.tensor_scalar(nt[:, :], nt[:, :], -0.5, 1.5, ALU.mult, ALU.add).then_inc(f_step, 1)
                dve.wait_ge(f_step, 3)
                nc.vector.tensor_tensor(rs, rs, nt[:, :], ALU.mult).then_inc(f_step, 1)
                dve.wait_ge(f_step, 4)
                for c in range(DC):
                    nc.vector.scalar_tensor_tensor(out=H[:, c, :], in0=X[:, c, :], scalar=pr("norm_final", c, c + 1),
                                                   in1=rs, op0=ALU.mult, op1=ALU.mult).then_inc(f_out, 1)

            @block.sync
            def _(sp):
                sp.wait_ge(f_out, DC)
                sp.dma_start(out_t, H[:, :, :]).then_inc(stored, 16)
                sp.wait_ge(stored, 16)


def by_column(w):
    L, k, n = w.shape
    return w.reshape(L, DC, P, n // P, P).transpose(0, 3, 2, 1, 4).reshape(L, n // P, P, PIECE)


def by_token(w):
    L = w.shape[0]
    return w.reshape(L, 2, DC // 2, P, 256).transpose(0, 1, 3, 2, 4).reshape(L, 2, P, PIECE)


def lay_out(inp):
    f = {k: np.asarray(v) for k, v in inp.items()}
    L = DEPTH
    w_in = f["w_in"]
    off, at = {}, 0
    for name, width in (("ret_q", GW), ("ret_k", GW), ("ret_v", GW), ("ret_g", GW), ("moba_q", GW), ("moba_k", GW),
                        ("moba_v", GW), ("z", GW), ("xbc", 768), ("dt", 4), ("nsa_q", GW), ("k_cmp", HD),
                        ("v_cmp", HD), ("k_slc", HD), ("v_slc", HD), ("k_win", HD), ("v_win", HD), ("gate", 12)):
        off[name] = slice(at, at + width)
        at += width
    col = {k: w_in[:, :, s] for k, s in off.items()}
    g2 = np.zeros((L, D, 256), np.float32)
    for name, c in (("gate", GATE), ("dt", DT), ("k_win", K_WIN), ("v_win", V_WIN)):
        g2[:, :, c:c + col[name].shape[2]] = col[name]
    g1 = np.concatenate([col[k] for k in ("k_cmp", "v_cmp", "k_slc", "v_slc")], 2)
    stream = np.zeros((L, PIECES, P, PIECE), np.float32)
    stream[:, 0:2 * N_XBC] = by_column(col["xbc"])
    for n, w in ((3, g1), (4, g2), (5, col["nsa_q"]), (6, col["moba_q"]), (11, col["moba_k"]), (12, col["moba_v"]),
                 (13, col["ret_q"]), (14, col["ret_k"]), (15, col["ret_v"]), (16, col["ret_g"]), (17, col["z"])):
        stream[:, 2 * n:2 * n + 2] = by_token(w)
    for n, name in ((7, "nsa_w1_k"), (9, "nsa_w1_v")):
        w = f[name].reshape(L, 4, CHUNKS // 4, P, 256).transpose(0, 1, 3, 2, 4)
        stream[:, 2 * n:2 * n + 4] = w.reshape(L, 4, P, PIECE)
    stream[:, 2 * OUT0:2 * (OUT0 + N_OUT)] = by_column(f["w_out"])
    stream[:, 2 * WQ0:2 * (WQ0 + N_WQ)] = by_column(f["peer_wq"])
    keys = f["peer_keys"].reshape(L, N_KEYS, 8, KEYS, P).transpose(0, 1, 4, 2, 3)
    stream[:, KEY0:KEY0 + N_KEYS] = keys.reshape(L, N_KEYS, P, PIECE)
    u = f["peer_u"].reshape(L, TILES, P, DC, P).transpose(0, 1, 4, 3, 2)
    stream[:, U0:V0] = u.reshape(L, TILES, P, PIECE)
    stream[:, V0:] = f["peer_v"].reshape(L, TILES, P, PIECE)

    params = np.zeros((L, P, NPARAM), np.float32)

    def put(name, a):
        lo, hi = PARAMS[name]
        params[:, :, lo:hi] = a.reshape(a.shape[0], P, hi - lo)

    def on_partitions(a, n):
        return a.reshape(L, n, P).transpose(0, 2, 1)

    put("norm_mix", on_partitions(f["norm_mix"], DC))
    put("norm_ffn", on_partitions(f["norm_ffn"], DC))
    put("conv_w", f["ssm_conv_w"].reshape(L, CONV, 6, P).transpose(0, 3, 2, 1))
    put("conv_b", on_partitions(f["ssm_conv_b"], 6))
    put("ret_norm", on_partitions(f["ret_norm"], 2))
    put("ssm_norm", on_partitions(f["ssm_norm"], 2))
    put("pe_k", on_partitions(f["nsa_pe_k"], CHUNKS))
    put("pe_v", on_partitions(f["nsa_pe_v"], CHUNKS))
    w2k = f["nsa_w2_k"].reshape(L, 2, P, 1, HD)
    put("w2k", np.broadcast_to(w2k, (L, 2, P, 2, HD)).transpose(0, 2, 1, 3, 4))
    put("w2v", f["nsa_w2_v"].reshape(L, 2, P, HD).transpose(0, 2, 1, 3))
    for name, src in (("dt_bias", "ssm_dt_bias"), ("a_log", "ssm_a_log"), ("ssm_d", "ssm_d")):
        put(name, np.broadcast_to(f[src][:, None, :], (L, P, NH)))
    put("norm_final", np.broadcast_to(f["norm_final"].reshape(1, DC, P).transpose(0, 2, 1), (L, P, DC)))
    x_t = np.ascontiguousarray(f["x"].reshape(SEQ, DC, P).transpose(2, 1, 0))
    return {"x_t": x_t, "stream": stream, "params": params, "consts": shape_constants()}


def kernel(**inputs):
    import concourse.bacc as bacc
    from concourse.bass_utils import run_bass_kernel_spmd as run

    nc = bacc.Bacc("TRN2", target_bir_lowering=False, num_devices=1)
    arrays = lay_out(inputs)
    args = [nc.dram_tensor(k, a.shape, F32, kind="ExternalInput").ap() for k, a in arrays.items()]
    args.append(nc.dram_tensor("out_t", (P, DC, SEQ), F32, kind="ExternalOutput").ap())
    program(nc, *args)
    r = run(nc, [arrays], core_ids=[0])
    out = r.results[0]["out_t"]
    return out.transpose(2, 1, 0).reshape(1, SEQ, D)
```
